# Optimizing a Trainium2 kernel written in Bass

```python
import jax, jax.numpy as jnp
from jax import lax
import numpy as np

D_MODEL = 1024
BATCH = 1
SEQ = 1024
DEPTH = 1
DEC_BATCH = 1
DEC_SEQ = 32
PAST_LEN = 1024

CHUNK = 64
D_MIX = D_MODEL
RET_HEADS = 4
RET_DK = 128
RET_DV = 128
HG_HEADS = 4
HG_DK = 128
HG_DV = 128
RET_QK = RET_HEADS * RET_DK
RET_W = RET_HEADS * RET_DV
HG_QK = HG_HEADS * HG_DK
HG_W = HG_HEADS * HG_DV
IN_SIZES = (RET_QK, RET_QK, RET_W, RET_W, HG_QK, HG_QK, HG_W, HG_W)
D_IN = RET_QK * 2 + RET_W * 2 + HG_QK * 2 + HG_W * 2
N_GROUPS = 4
EXP_PER_GROUP = 4
N_EXPERTS = N_GROUPS * EXP_PER_GROUP
TOP_K = 2
D_EXPERT = 512
ROPE_BASE = 10000.0
EPS = 1e-6

kernel_name = "hymba_retention_hgrn2_hmoe_stream_step"

def rmsnorm(x, g):
    xf = x.astype(jnp.float32)
    y = xf * lax.rsqrt(jnp.mean(xf * xf, axis=-1, keepdims=True) + EPS)
    return (y * g.astype(jnp.float32)).astype(x.dtype)

def head_rmsnorm(o, g):
    H, dv = o.shape[2], o.shape[3]
    y = o * lax.rsqrt(jnp.mean(o * o, axis=-1, keepdims=True) + EPS)
    return y * g.astype(jnp.float32).reshape(H, dv)

def rotary(x, pos):
    half = x.shape[-1] // 2
    inv = 1.0 / (ROPE_BASE ** (jnp.arange(half, dtype=jnp.float32) / half))
    ang = pos.astype(jnp.float32)[:, None] * inv[None, :]
    cos = jnp.cos(ang)[None, :, None, :]
    sin = jnp.sin(ang)[None, :, None, :]
    x1 = x[..., :half].astype(jnp.float32)
    x2 = x[..., half:].astype(jnp.float32)
    return jnp.concatenate([x1 * cos - x2 * sin, x2 * cos + x1 * sin], axis=-1)

def retention_log_decay():
    return jnp.log(1.0 - jnp.exp2(-5.0 - jnp.arange(RET_HEADS, dtype=jnp.float32)))

def retention_chunk(S, q, k, v):
    L = q.shape[1]
    lg = retention_log_decay()
    j = jnp.arange(L, dtype=jnp.float32)
    diff = j[:, None] - j[None, :]
    D = jnp.where(diff[None] >= 0, jnp.exp(jnp.maximum(diff, 0.0)[None] * lg[:, None, None]), 0.0)
    A = jnp.einsum('blhk,bmhk->bhlm', q, k) * D[None]
    intra = jnp.einsum('bhlm,bmhv->blhv', A, v)
    inter_dec = jnp.exp((j[:, None] + 1.0) * lg[None, :])
    inter = jnp.einsum('blhk,bhkv->blhv', q, S) * inter_dec[None, :, :, None]
    k_dec = k * jnp.exp((L - 1.0 - j)[:, None] * lg[None, :])[None, :, :, None]
    S_new = jnp.exp(L * lg)[None, :, None, None] * S + jnp.einsum('blhk,blhv->bhkv', k_dec, v)
    return S_new, intra + inter

def hgrn2_chunk(S, q, k, v, logf):
    L = q.shape[1]
    b = jnp.cumsum(logf, axis=1)
    inter = jnp.einsum('blhk,bhkv->blhv', q * jnp.exp(b), S)
    causal = jnp.tril(jnp.ones((L, L), dtype=bool))
    diff = b[:, :, None] - b[:, None, :]
    dec = jnp.exp(jnp.where(causal[None, :, :, None, None], diff, -jnp.inf))
    A = jnp.einsum('blhk,bmhk,blmhk->bhlm', q, k, dec)
    intra = jnp.einsum('bhlm,bmhv->blhv', A, v)
    bl = b[:, -1]
    k_dec = k * jnp.exp(bl[:, None] - b)
    S_new = jnp.exp(bl)[..., None] * S + jnp.einsum('blhk,blhv->bhkv', k_dec, v)
    return S_new, intra + inter

def run_chunks(step, S0, seqs):
    T = seqs[0].shape[1]
    S0 = S0.astype(jnp.float32)
    if T <= CHUNK:
        return step(S0, *seqs)
    nc = T // CHUNK

    def to_chunks(a):
        return jnp.moveaxis(a.reshape((a.shape[0], nc, CHUNK) + a.shape[2:]), 1, 0)

    S, ys = lax.scan(lambda S, xs: step(S, *xs), S0, tuple(to_chunks(a) for a in seqs))
    ys = jnp.moveaxis(ys, 0, 1)
    return S, ys.reshape((ys.shape[0], T) + ys.shape[3:])

def split_cols(a, sizes):
    out, start = [], 0
    for s in sizes:
        out.append(a[..., start:start + s])
        start += s
    return out

def token_mixer(h, s_ret, s_hg, pos, W_in, ret_norm_g, hg_norm_g, lb, W_out):
    B, T, _ = h.shape
    proj = h @ W_in
    rq, rk, rv, rg, hq, hf, hi, hgt = split_cols(proj, IN_SIZES)
    q_r = rotary(rq.reshape(B, T, RET_HEADS, RET_DK), pos)
    k_r = rotary(rk.reshape(B, T, RET_HEADS, RET_DK), pos) * (RET_DK ** -0.5)
    v_r = rv.reshape(B, T, RET_HEADS, RET_DV)
    s_ret_new, o_r = run_chunks(retention_chunk, s_ret, (q_r, k_r, v_r))
    o_r = head_rmsnorm(o_r, ret_norm_g).reshape(B, T, RET_W) * jax.nn.silu(rg.astype(jnp.float32))
    z = hf.astype(jnp.float32)
    lb = lb.astype(jnp.float32)
    logf = jnp.log(lb + (1.0 - lb) * jax.nn.sigmoid(z)).reshape(B, T, HG_HEADS, HG_DK)
    k_h = ((1.0 - lb) * jax.nn.sigmoid(-z)).reshape(B, T, HG_HEADS, HG_DK)
    q_h = hq.reshape(B, T, HG_HEADS, HG_DK) * (HG_DK ** -0.5)
    v_h = hi.reshape(B, T, HG_HEADS, HG_DV)
    s_hg_new, o_h = run_chunks(hgrn2_chunk, s_hg, (q_h, k_h, v_h, logf))
    o_h = head_rmsnorm(o_h, hg_norm_g).reshape(B, T, HG_W) * jax.nn.silu(hgt.astype(jnp.float32))
    o = jnp.concatenate([o_r, o_h], axis=-1).astype(h.dtype)
    return o @ W_out, s_ret_new, s_hg_new

def hier_moe(h, W_rg, b_rg, W_re, b_re, W_gate_e, W_up_e, W_down_e):
    B, T, D = h.shape
    xt = h.reshape(B * T, D)
    pg = jax.nn.softmax((xt @ W_rg + b_rg).astype(jnp.float32), axis=-1)
    g_w, g_idx = lax.top_k(pg, 1)
    g_w, g_idx = g_w[:, 0], g_idx[:, 0]
    el = (xt @ W_re + b_re).astype(jnp.float32).reshape(-1, N_GROUPS, EXP_PER_GROUP)
    el_sel = jnp.einsum('ng,nge->ne', jax.nn.one_hot(g_idx, N_GROUPS, dtype=jnp.float32), el)
    pe = jax.nn.softmax(el_sel, axis=-1)
    e_w, e_loc = lax.top_k(pe, TOP_K)
    e_w = e_w / jnp.sum(e_w, axis=-1, keepdims=True)
    w = g_w[:, None] * e_w
    e_idx = g_idx[:, None] * EXP_PER_GROUP + e_loc
    combine = jnp.sum(jax.nn.one_hot(e_idx, N_EXPERTS, dtype=jnp.float32) * w[..., None], axis=1)
    combine = combine.astype(xt.dtype)
    y = jnp.zeros_like(xt)
    for e in range(N_EXPERTS):
        hid = jax.nn.silu(xt @ W_gate_e[e]) * (xt @ W_up_e[e])
        y = y + combine[:, e:e + 1] * (hid @ W_down_e[e])
    return y.reshape(B, T, D)

def trunk(x, c, s_ret, s_hg, pos, W_ada, b_ada, norm1_g, norm2_g, W_in, ret_norm_g, hgrn_norm_g,
          hgrn_lb_logits, W_out, W_router_group, b_router_group, W_router_expert, b_router_expert,
          W_gate_e, W_up_e, W_down_e, final_norm_g):
    lb_all = jnp.cumsum(jax.nn.softmax(hgrn_lb_logits.astype(jnp.float32), axis=0), axis=0)
    new_r, new_h = [], []
    for l in range(DEPTH):
        mod = jax.nn.silu(c) @ W_ada[l] + b_ada[l]
        sh1, sc1, gt1, sh2, sc2, gt2 = jnp.split(mod[:, None, :], 6, axis=-1)
        h = rmsnorm(x, norm1_g[l]) * (1 + sc1) + sh1
        mix, sr, shg = token_mixer(h, s_ret[l], s_hg[l], pos, W_in[l], ret_norm_g[l], hgrn_norm_g[l],
                                   lb_all[l], W_out[l])
        x = x + (gt1 * mix).astype(x.dtype)
        h = rmsnorm(x, norm2_g[l]) * (1 + sc2) + sh2
        ff = hier_moe(h, W_router_group[l], b_router_group[l], W_router_expert[l], b_router_expert[l],
                      W_gate_e[l], W_up_e[l], W_down_e[l])
        x = x + (gt2 * ff).astype(x.dtype)
        new_r.append(sr)
        new_h.append(shg)
    return rmsnorm(x, final_norm_g), jnp.stack(new_r), jnp.stack(new_h)

def setup_inputs(seed: int = 0) -> dict:
    key = jax.random.key(seed)
    ks = jax.random.split(key, 24)
    f32 = jnp.float32
    D = D_MODEL
    n = lambda k, shape, s: jax.random.normal(k, shape, f32) * s
    return {
        'x_prompt': n(ks[0], (BATCH, SEQ, D), 1.0),
        'x_sample': n(ks[1], (DEC_BATCH, DEC_SEQ, D), 1.0),
        'c_prompt': n(ks[2], (BATCH, D), 1.0),
        'c_sample': n(ks[3], (DEC_BATCH, D), 1.0),
        'state_ret': n(ks[4], (DEPTH, DEC_BATCH, RET_HEADS, RET_DK, RET_DV), 1.0),
        'state_hgrn': n(ks[5], (DEPTH, DEC_BATCH, HG_HEADS, HG_DK, HG_DV), 1.0),
        'W_ada': n(ks[6], (DEPTH, D, 6 * D), 0.5 * D ** -0.5),
        'b_ada': n(ks[7], (DEPTH, 6 * D), 0.02),
        'norm1_g': 1.0 + n(ks[8], (DEPTH, D), 0.02),
        'norm2_g': 1.0 + n(ks[9], (DEPTH, D), 0.02),
        'W_in': n(ks[10], (DEPTH, D, D_IN), D ** -0.5),
        'ret_norm_g': 1.0 + n(ks[11], (DEPTH, RET_W), 0.02),
        'hgrn_norm_g': 1.0 + n(ks[12], (DEPTH, HG_W), 0.02),
        'hgrn_lb_logits': n(ks[13], (DEPTH + 1, HG_QK), 0.5),
        'W_out': n(ks[14], (DEPTH, D_MIX, D), D_MIX ** -0.5),
        'W_router_group': n(ks[15], (DEPTH, D, N_GROUPS), D ** -0.5),
        'b_router_group': n(ks[16], (DEPTH, N_GROUPS), 0.01),
        'W_router_expert': n(ks[17], (DEPTH, D, N_EXPERTS), D ** -0.5),
        'b_router_expert': n(ks[18], (DEPTH, N_EXPERTS), 0.01),
        'W_gate_e': n(ks[19], (DEPTH, N_EXPERTS, D, D_EXPERT), D ** -0.5),
        'W_up_e': n(ks[20], (DEPTH, N_EXPERTS, D, D_EXPERT), D ** -0.5),
        'W_down_e': n(ks[21], (DEPTH, N_EXPERTS, D_EXPERT, D), D_EXPERT ** -0.5),
        'final_norm_g': 1.0 + n(ks[22], (D,), 0.02),
    }

def reference(x_prompt, x_sample, c_prompt, c_sample, state_ret, state_hgrn, W_ada, b_ada, norm1_g,
              norm2_g, W_in, ret_norm_g, hgrn_norm_g, hgrn_lb_logits, W_out, W_router_group,
              b_router_group, W_router_expert, b_router_expert, W_gate_e, W_up_e, W_down_e,
              final_norm_g):
    Bp, Tp, _ = x_prompt.shape
    Ts = x_sample.shape[1]
    s_ret0 = jnp.zeros((DEPTH, Bp, RET_HEADS, RET_DK, RET_DV), jnp.float32)
    s_hg0 = jnp.zeros((DEPTH, Bp, HG_HEADS, HG_DK, HG_DV), jnp.float32)
    pos_p = jnp.arange(Tp, dtype=jnp.int32)
    y_prompt, state_ret_prompt, state_hgrn_prompt = trunk(
        x_prompt, c_prompt, s_ret0, s_hg0, pos_p, W_ada, b_ada, norm1_g, norm2_g, W_in, ret_norm_g,
        hgrn_norm_g, hgrn_lb_logits, W_out, W_router_group, b_router_group, W_router_expert,
        b_router_expert, W_gate_e, W_up_e, W_down_e, final_norm_g)
    pos_s = PAST_LEN + jnp.arange(Ts, dtype=jnp.int32)
    y_sample, state_ret_sample, state_hgrn_sample = trunk(
        x_sample, c_sample, state_ret, state_hgrn, pos_s, W_ada, b_ada, norm1_g, norm2_g, W_in,
        ret_norm_g, hgrn_norm_g, hgrn_lb_logits, W_out, W_router_group, b_router_group,
        W_router_expert, b_router_expert, W_gate_e, W_up_e, W_down_e, final_norm_g)
    return (y_prompt, y_sample, state_ret_prompt, state_hgrn_prompt, state_ret_sample, state_hgrn_sample)


_drawn_inputs = setup_inputs


def setup_inputs(seed=0):
    import zlib

    import numpy as np

    out = dict(_drawn_inputs(seed))
    spreads = {}
    factors = {'norm1_g': 2.866,
     'norm2_g': 5.837,
     'ret_norm_g': 8.0,
     'hgrn_norm_g': 8.0,
     'b_router_group': 8.0,
     'b_router_expert': 27.949,
     'final_norm_g': 7.836}
    for name, (base, spread) in spreads.items():
        noise = np.random.default_rng([zlib.crc32(name.encode()), seed]).standard_normal(out[name].shape)
        drawn = base * np.exp(spread * noise) if base else spread * noise
        out[name] = __import__('jax').numpy.asarray(drawn.astype(out[name].dtype))
    for name, factor in factors.items():
        out[name] = (out[name] * factor).astype(out[name].dtype)
    return out
```

```python
from contextlib import ExitStack

import numpy as np

import concourse.bass as bass
from concourse import mybir

F32 = mybir.dt.float32
F32R = mybir.dt.float32r
I32 = mybir.dt.int32
ALU = mybir.AluOpType
ACT = mybir.ActivationFunctionType
AX = mybir.AxisListType.X

P = 128
D = 1024
KD = D // P
SEQ = 1024
DEC = 32
PAST = 1024
NTOK = SEQ + DEC
NP_T = SEQ // P
NT = NP_T + 1
HEADS = 4
D_IN = 4096
EPS = 1e-6
N_GROUPS = 4
PER_GROUP = 4
NE = N_GROUPS * PER_GROUP
F = 512
KF = F // P
SLOTS = 2 * NTOK
ROWS = SLOTS + NT * P
PIECE = NTOK // 3
SCALE = float(np.float32(128.0) ** np.float32(-0.5))
LEVELS = (64, 32, 16, 8, 4, 2, 1)
SMALL = 5

CONSTS = dict(ident=P, ones=P, tri=P, cos=NT * 64, sin=NT * 64, ret_decay=HEADS * P, q_decay=HEADS * P,
              level_mask=(SMALL + 1) * 32, k_decay=2 * HEADS, s_decay=2 * HEADS, iota=NE, limits=8)
AT = dict(zip(CONSTS, np.cumsum([0, *CONSTS.values()])[:-1].tolist()))
N_CONST = sum(CONSTS.values())


def width(i):
    return P if i < NP_T else DEC


def constants():
    f = np.float32
    c = {}
    c["ident"] = np.eye(P)
    c["ones"] = np.ones((P, P))
    c["tri"] = np.triu(np.ones((P, P)), 1)
    inv = (f(1.0) / (f(10000.0) ** (np.arange(64, dtype=f) / f(64)))).astype(f)
    pos = np.concatenate([np.arange(SEQ), PAST + np.arange(P)]).astype(f)
    ang = (pos[:, None] * inv[None, :]).astype(f).reshape(NT, P, 64).transpose(1, 0, 2)
    c["cos"], c["sin"] = np.cos(ang).reshape(P, -1), np.sin(ang).reshape(P, -1)
    lg = np.log(1.0 - np.exp2(-5.0 - np.arange(HEADS)))
    j = np.arange(P)
    diff = j[None, :] - j[:, None]
    decay = np.where(diff[:, None] >= 0, np.exp(np.maximum(diff, 0)[:, None] * lg[None, :, None]), 0.0)
    c["ret_decay"] = decay * SCALE
    c["q_decay"] = np.broadcast_to(np.exp((j[None, None] + 1.0) * lg[None, :, None]), (P, HEADS, P))
    full, short = np.exp((P - 1.0 - j)[:, None] * lg), np.exp(np.maximum(DEC - 1.0 - j, 0)[:, None] * lg)
    c["k_decay"] = np.stack([full, short], -1) * SCALE
    c["s_decay"] = np.broadcast_to(np.stack([np.exp(P * lg), np.exp(DEC * lg)], -1), (P, HEADS, 2))
    m, l = np.arange(P)[:, None] % 32, np.arange(32)[None, :]
    masks = [(m // (2 * h) == l // (2 * h)) & (m % (2 * h) < h) & (l % (2 * h) >= h) for h in LEVELS[2:]]
    c["level_mask"] = np.stack([*masks, m == l], 1)
    c["iota"] = np.broadcast_to(np.arange(NE), (P, NE))
    c["limits"] = np.broadcast_to(P * (1.0 + np.arange(8)), (P, 8))
    return np.concatenate([np.asarray(c[k], f).reshape(P, -1) for k in CONSTS], 1)


class Shared:

    def const(self, name, a=0, b=None):
        b = CONSTS[name] if b is None else b
        return self.consts[:, AT[name] + a:AT[name] + b]


def allocate(nc, ctx, phase):
    def sb(name, shape, dt=F32):
        return ctx.enter_context(nc.sbuf_tensor(f"{phase}_{name}", shape, dt))

    def ps(name, shape):
        return ctx.enter_context(nc.psum_tensor(f"{phase}_{name}", shape, F32))

    def sem(name):
        return ctx.enter_context(nc.semaphore(f"{phase}_{name}"))

    return sb, ps, sem


def carry(e, idle):
    e.sem_inc(idle, 1)


def f32(ap):
    return ap.bitcast(F32)


def phase_condition(nc, s):
    with ExitStack() as ctx:
        sb, ps, sem = allocate(nc, ctx, "condition")
        rows = sb("rows", [56, P])
        w_ada = sb("w_ada_in", [P, 2, KD, 512])
        xt = sb("xt", [P, 3, D])
        h32 = sb("h32", [P, KD, NTOK])
        mod_row = sb("mod_row", [2, 4, 512])
        mod_col = sb("mod_col", [P, 16, 2])
        gain = sb("gain", [P, KD, 2])
        squares = sb("squares", [P, D])
        mean_sq = sb("mean_sq", [P, NT])
        rstd = sb("rstd", [P, NT])
        lbx = sb("lbx", [P, 3, HEADS])
        ps_col = ps("ps_col", [P, 512])
        ps_ada = [ps(f"ps_ada{n}", [P, 512]) for n in range(2)]
        ps_x = [ps(f"ps_x{n}", [P, 4, P]) for n in range(4)]
        ps_mod = ps("ps_mod", [P, 512])
        const_in, rows_in = sem("const_in"), sem("rows_in")
        x_in = [sem(f"x_in{n}") for n in range(3)]
        w_in = [sem(f"w_in{n}") for n in range(2)]
        c_silu, cols_t, cols_done, ct_done = sem("c_silu"), sem("cols_t"), sem("cols_done"), sem("ct_done")
        ms_done, rstd_done, xn_done, xt_done = sem("ms_done"), sem("rstd_done"), sem("xn_done"), sem("xt_done")
        xlow, xhigh = sem("xlow_copied"), sem("xhigh_copied")
        ada_done, ada_copied, mod_t, mod_added, gain_done = (sem("ada_done"), sem("ada_copied"), sem("mod_t"),
                                                             sem("mod_added"), sem("gain_done"))
        h_done, hi_done, lb_exp, lb_step = sem("h_done"), sem("hi_done"), sem("lb_exp"), sem("lb_step")
        lo_done, root_done, eps_set = sem("lo_done"), sem("root_done"), sem("eps_set")
        block = ctx.enter_context(nc.Block())
        ident = s.const("ident")
        a = s.args

        @block.sync
        def _(sp):
            sp.dma_start(s.consts[:, :], a["consts"]).then_inc(const_in, 16)
            split = [(0, 8, a["c_prompt"][0]), (8, 16, a["c_sample"][0]), (16, 32, a["b_ada"][0, 0:2 * D]),
                     (32, 40, a["norm1_g"][0]), (40, 44, a["hgrn_lb_logits"][0]),
                     (44, 48, a["hgrn_lb_logits"][1]), (48, 52, a["ret_norm_g"][0]),
                     (52, 56, a["hgrn_norm_g"][0])]
            for lo, hi, src in split:
                sp.dma_start(rows[lo:hi, :], src.rearrange("(k p) -> k p", p=P)).then_inc(rows_in, 16)
            w_view = a["W_ada"][0].rearrange("(k p) n -> p k n", p=P)
            for i in range(NT):
                if i >= 3:
                    sp.wait_ge(xt_done, i - 2)
                src = a["x_prompt"][0, i * P:(i + 1) * P, :] if i < NP_T else a["x_sample"][0]
                sp.dma_start(xt[0:width(i), i % 3, :], src).then_inc(x_in[i % 3], 16)
                if i % 2 == 0 and i < 8:
                    b = i // 2
                    if b >= 2:
                        sp.wait_ge(ada_done, b - 1)
                    sp.dma_start(w_ada[:, b % 2], w_view[:, :, b * 512:(b + 1) * 512]).then_inc(w_in[b % 2], 16)

        def copy_low(act, i):
            w = width(i)
            act.wait_ge(xt_done, i + 1)
            act.activation(h32[:, 0:4, i * P:i * P + w], ps_x[2 * (i % 2)][:, :, 0:w], ACT.Copy).then_inc(xlow, 1)

        @block.scalar
        def _(act):
            act.wait_ge(eps_set, 1)
            act.wait_ge(rows_in, 128)
            act.activation(rows[0:16, :], rows[0:16, :], ACT.Silu).then_inc(c_silu, 1)
            for i in range(NT):
                w = width(i)
                act.wait_ge(x_in[i % 3], 16 * (i // 3 + 1))
                if i:
                    act.wait_ge(ms_done, i)
                act.activation(squares[0:w, :], xt[0:w, i % 3, :], ACT.Square, scale=1.0 / 32.0,
                               accum_out=mean_sq[0:w, i:i + 1]).then_inc(ms_done, 1)
                act.wait_ge(ms_done, i + 1)
                act.activation(rstd[0:w, i:i + 1], mean_sq[0:w, i:i + 1], ACT.Sqrt, bias=s.eps[0:w, :])\
                   .then_inc(root_done, 1)
                if i:
                    copy_low(act, i - 1)
            copy_low(act, NT - 1)
            act.wait_ge(lb_step, 2)
            act.activation(lbx[:, 0:2, :], lbx[:, 0:2, :], ACT.Exp).then_inc(lb_exp, 1)
            for k in range(KD):
                act.wait_ge(h_done, k + 1)
                act.activation(s.h_hi[:, k, :], h32[:, k, :], ACT.Copy).then_inc(hi_done, 1)

        @block.tensor
        def _(pe):
            pe.wait_ge(const_in, 16)
            pe.wait_ge(c_silu, 1)
            pe.transpose(ps_col[:, 0:56], rows[:, :], ident[0:56, 0:56]).then_inc(cols_t, 1)
            pe.wait_ge(ct_done, 1)
            for i in range(NT):
                w = width(i)
                pe.wait_ge(xn_done, i + 1)
                if i >= 2:
                    pe.wait_ge(xlow, i - 1)
                    pe.wait_ge(xhigh, i - 1)
                for k in range(KD):
                    last = pe.transpose(ps_x[2 * (i % 2) + k // 4][:, k % 4, 0:w],
                                        xt[0:w, i % 3, k * P:(k + 1) * P], ident[0:w, 0:w])
                last.then_inc(xt_done, 1)
                if i % 2 == 1:
                    b = i // 2
                    pe.wait_ge(w_in[b % 2], 16 * (b // 2 + 1))
                    if b >= 2:
                        pe.wait_ge(ada_copied, b - 1)
                    for k in range(KD):
                        last = pe.matmul(ps_ada[b % 2][0:2, :], s.cT[:, k, :], w_ada[:, b % 2, k, :],
                                         start=(k == 0), stop=(k == KD - 1))
                    last.then_inc(ada_done, 1)
            pe.wait_ge(ada_copied, 4)
            for j in range(16):
                last = pe.transpose(ps_mod[:, 2 * j:2 * j + 2], mod_row[:, j // 4, (j % 4) * P:(j % 4 + 1) * P],
                                    ident[0:2, 0:2])
            last.then_inc(mod_t, 1)

        @block.vector
        def _(dve):
            dve.memset(s.eps[:, :], EPS).then_inc(eps_set, 1)
            dve.wait_ge(cols_t, 1)
            dve.tensor_copy(s.cT[:, :, :], ps_col[:, 0:16].rearrange("p (s k) -> p k s", s=2)).then_inc(ct_done, 1)
            dve.tensor_copy(s.cols[:, :], ps_col[:, 16:56]).then_inc(cols_done, 1)

            def turn(i):
                w = width(i)
                dve.wait_ge(root_done, i + 1)
                dve.reciprocal(rstd[0:w, i:i + 1], rstd[0:w, i:i + 1]).then_inc(rstd_done, 1)
                dve.wait_ge(rstd_done, i + 1)
                dve.tensor_scalar(xt[0:w, i % 3, :], xt[0:w, i % 3, :], rstd[0:w, i:i + 1], None,
                                  ALU.mult).then_inc(xn_done, 1)

            def copy_high(i):
                w = width(i)
                dve.wait_ge(xt_done, i + 1)
                dve.tensor_copy(h32[:, 4:8, i * P:i * P + w], ps_x[2 * (i % 2) + 1][:, :, 0:w]).then_inc(xhigh, 1)

            for i in range(NT):
                turn(i)
                if i:
                    copy_high(i - 1)
                if i % 2 == 0 and i >= 2:
                    b = i // 2 - 1
                    dve.wait_ge(ada_done, b + 1)
                    dve.tensor_copy(mod_row[:, b, :], ps_ada[b % 2][0:2, :]).then_inc(ada_copied, 1)
            copy_high(NT - 1)
            dve.wait_ge(cols_done, 1)
            logits = s.cols[:, 24:32].rearrange("p (l h) -> p l h", l=2)
            dve.tensor_tensor(lbx[:, 2, :], logits[:, 0, :], logits[:, 1, :], ALU.max).then_inc(lb_step, 1)
            dve.wait_ge(lb_step, 1)
            dve.tensor_tensor(lbx[:, 0:2, :], logits, lbx[:, 2:3, :].broadcast_to([P, 2, HEADS]),
                              ALU.subtract).then_inc(lb_step, 1)
            dve.wait_ge(lb_exp, 1)
            dve.tensor_tensor(lbx[:, 2, :], lbx[:, 0, :], lbx[:, 1, :], ALU.add).then_inc(lb_step, 1)
            dve.wait_ge(lb_step, 3)
            dve.reciprocal(lbx[:, 2, :], lbx[:, 2, :]).then_inc(lb_step, 1)
            dve.wait_ge(lb_step, 4)
            dve.tensor_tensor(s.bound[:, 0, :], lbx[:, 0, :], lbx[:, 2, :], ALU.mult).then_inc(lb_step, 1)
            dve.wait_ge(lb_step, 5)
            dve.tensor_scalar(s.bound[:, 1, :], s.bound[:, 0, :], -1.0, 1.0, ALU.mult, ALU.add)
            dve.wait_ge(mod_t, 1)
            dve.tensor_tensor(mod_col[:, :, :], ps_mod[:, 0:32].rearrange("p (j s) -> p j s", s=2),
                              s.cols[:, 0:16].unsqueeze(2).broadcast_to([P, 16, 2]), ALU.add).then_inc(mod_added, 1)
            dve.wait_ge(mod_added, 1)
            dve.scalar_tensor_tensor(out=gain[:, :, :], in0=mod_col[:, 8:16, :], scalar=1.0,
                                     in1=s.cols[:, 16:24].unsqueeze(2).broadcast_to([P, KD, 2]),
                                     op0=ALU.add, op1=ALU.mult).then_inc(gain_done, 1)
            dve.wait_ge(gain_done, 1)
            dve.wait_ge(xlow, NT)
            dve.wait_ge(xhigh, NT)
            for k in range(KD + 1):
                if k < KD:
                    dve.tensor_scalar(h32[:, k, 0:SEQ], h32[:, k, 0:SEQ], gain[:, k, 0:1], mod_col[:, k, 0:1],
                                      ALU.mult, ALU.add)
                    dve.tensor_scalar(h32[:, k, SEQ:NTOK], h32[:, k, SEQ:NTOK], gain[:, k, 1:2],
                                      mod_col[:, k, 1:2], ALU.mult, ALU.add).then_inc(h_done, 1)
                if k:
                    dve.wait_ge(hi_done, k)
                    dve.tensor_tensor(s.h_lo[:, k - 1, :], h32[:, k - 1, :], f32(s.h_hi[:, k - 1, :]),
                                      ALU.subtract).then_inc(lo_done, 1)


def phase_mixers(nc, s):
    R = HEADS
    with ExitStack() as ctx:
        sb, ps, sem = allocate(nc, ctx, "mixers")
        raw = sb("raw", [P, 4, KD, P])
        w_hi = sb("w_hi", [P, KD, 4, P], F32R)
        w_lo = sb("w_lo", [P, KD, 4, P], F32R)
        log_f = sb("log_f", [P, NTOK])
        hk = sb("hk", [P, NTOK])
        hq = sb("hq", [P, NTOK])
        gate = sb("gate", [P, 2, NTOK])
        ones = s.const("ones")
        decay = sb("decay", [P, 9, P])
        q_lv = sb("q_lv", [P, 7, P])
        k_lv = sb("k_lv", [P, 8, P])
        q_in = sb("q_in", [P, 2, P])
        last_f = sb("last_f", [P, 2])
        qk_cos = sb("qk_cos", [P, 4, 64])
        qk_sin = sb("qk_sin", [P, 4, 64])
        rot = sb("rot", [P, 2, 2, 64])
        k_dec = sb("k_dec", [P, 2, P])
        kd_col = sb("kd_col", [P, 2])
        qkv = sb("qkv", [P, 2, 512])
        turned = sb("turned", [P, 3, P])
        q_t, k_t, hk_dec = (turned[:, c, :] for c in range(3))
        qd_t = sb("qd_t", [P, P])
        a_ret = sb("a_ret", [P, P])
        a_hg = sb("a_hg", [P, 2, P])
        masked = sb("masked", [P, SMALL + 1, 32])
        squares = sb("squares", [P, 2, P])
        mean_sq = sb("mean_sq", [P, 2, 2])
        norm = sb("norm", [P, 2, 4, 2])
        normed = sb("normed", [P, 2, P])
        o_out = sb("o_out", [P, 2, 2, P])
        s_pr = sb("s_prompt", [P, 2, P])
        s_sa = sb("s_sample", [P, 2, P])
        ada_bias = sb("ada_bias", [2, D])
        ada_row = sb("ada_row", [2, D])
        ps_p = [ps(f"ps_proj{n}", [P, 512]) for n in range(2)]
        ps_tr = ps("ps_tr", [P, 4, P])
        ps_a = ps("ps_a", [P, 512])
        ps_lv = ps("ps_lv", [P, 512])
        ps_o = ps("ps_o", [P, 4, P])
        ps_s = ps("ps_s", [P, 4, P])
        ps_ot = ps("ps_ot", [P, 4, P])
        wide = ps_lv[:, 256:384]
        lv = ps_lv[:, 0:(SMALL + 1) * 32].rearrange("p (s l) -> p s l", l=32)

        raw_in = [sem(f"raw_in{n}") for n in range(4)]
        hi_done, lo_done, t_done, t_read = sem("hi_done"), sem("lo_done"), sem("t_done"), sem("t_read")
        proj_done, ada_done, ada_read = sem("proj_done"), sem("ada_done"), sem("ada_read")
        bias_in, ada_out = sem("bias_in"), sem("ada_out")
        f_done, logf_done, hk_done = sem("f_done"), sem("logf_done"), sem("hk_done")
        roped, rot_done, v_done, kdec_done = sem("roped"), sem("rot_done"), sem("v_done"), sem("kdec_done")
        tr_done, qkt_done, qd_done = sem("tr_done"), sem("qkt_done"), sem("qd_done")
        cum_done, diff_done, abs_done, exp_done = sem("cum_done"), sem("diff_done"), sem("abs_done"), sem("exp_done")
        ql_done, kl_done = sem("ql_done"), sem("kl_done")
        lv_done, ra_done, masked_done, ah_done, ahc_done, ar_done = (
            sem("lv_done"), sem("ra_done"), sem("masked_done"), sem("ah_done"), sem("ahc_done"), sem("ar_done"))
        o_done, s_done, ms_done, seed_log, seed_done, norm_step, normed_done = (
            sem("o_done"), sem("s_done"), sem("ms_done"), sem("seed_log"), sem("seed_done"), sem("norm_step"),
            sem("normed_done"))
        kd_copied, idle = sem("kd_copied"), sem("idle")
        ot_done, out_done, cleared = sem("ot_done"), sem("out_done"), sem("cleared")
        o_stored = [sem(f"o_stored{n}") for n in range(2)]
        sp_stored, ss_stored, ss_in = sem("sp_stored"), sem("ss_stored"), sem("ss_in")
        block = ctx.enter_context(nc.Block())
        a = s.args
        ident = s.const("ident")
        unit_at = [2560, 2048, 1536, 3584, 0, 512, 1024, 3072]
        pieces = [slice(n * PIECE, (n + 1) * PIECE) for n in range(3)]

        def counts(e, g):
            n = {}
            for m in (1, 2, 4, 8, 9, 12, 16, 32, 64):
                n[m] = e.snap(g * m)
            return n

        @block.sync
        def _(sp):
            w_in = a["W_in"][0].rearrange("(k p) n -> p k n", p=P)
            w_ada = a["W_ada"][0].rearrange("(k p) n -> p k n", p=P)
            with sp.Fori(0, R) as g:
                for u in range(16):
                    if u < 8:
                        at = sp.snap(g * P + unit_at[u])
                        src = w_in[:, :, bass.ds(at, P)]
                    else:
                        at = sp.snap(g * D + (2 * D + (u - 8) * P))
                        src = w_ada[:, :, bass.ds(at, P)]
                    if u < 4:
                        sp.wait_ge(ada_done, sp.snap(g * 8))
                    elif u < 12:
                        sp.wait_ge(lo_done, sp.snap(g * 8 + (u - 3)))
                    else:
                        sp.wait_ge(ada_done, sp.snap(g * 8 + (u - 11)))
                    carry(sp, idle)
                    sp.dma_start(raw[:, u % 4], src).then_inc(raw_in[u % 4], 16)
                    if u == 8:
                        head = sp.snap(g * 1)
                        sp.wait_ge(ss_stored, sp.snap(g * 32))
                        carry(sp, idle)
                        for n, name in enumerate(("state_ret", "state_hgrn")):
                            sp.dma_start(s_sa[:, n:n + 1, :],
                                         a[name][0, 0, bass.ds(head, 1)].rearrange("h k v -> k h v"))\
                              .then_inc(ss_in, 16)
                        at = sp.snap(g * D + 2 * D)
                        sp.wait_ge(ada_read, sp.snap(g * 2))
                        carry(sp, idle)
                        sp.dma_start(ada_bias[:, :], a["b_ada"][0:1, bass.ds(at, D)].broadcast_to([2, D]))\
                          .then_inc(bias_in, 16)

        @block.gpsimd
        def _(pool):
            pool.memset(a_hg[:, :, :], 0.0).then_inc(cleared, 1)
            with pool.Fori(0, R) as g:
                n = counts(pool, g)

                def keys(i):
                    w = width(i)
                    pool.wait_ge(exp_done, n[9] + (i + 1))
                    pool.wait_ge(lv_done, n[9] + i)
                    if i == 0:
                        pool.wait_ge(hk_done, n[1] + 1)
                    kb = hk[:, i * P:i * P + w]
                    for c, (lo, hi) in enumerate([(0, 8)] if w == P else [(0, 1), (3, 8)]):
                        last = pool.tensor_tensor(k_lv[:, lo:hi, 0:w], decay[:, lo:hi, 0:w],
                                                  kb.unsqueeze(1).broadcast_to([P, hi - lo, w]), ALU.mult)
                    last.then_inc(kl_done, 1)

                def refine(i):
                    w = width(i)
                    b = i % 2
                    step = lambda m: n[36] + (4 * i + m)
                    m, y = mean_sq[0:w, b, :], norm[0:w, b, 0, :]
                    t = [norm[0:w, b, c, :] for c in range(4)]
                    pool.wait_ge(seed_done, n[9] + (i + 1))
                    pool.tensor_tensor(t[1], y, y, ALU.mult).then_inc(norm_step, 1)
                    pool.wait_ge(norm_step, step(1))
                    pool.tensor_tensor(t[2], t[1], m, ALU.mult).then_inc(norm_step, 1)
                    pool.wait_ge(norm_step, step(2))
                    carry(pool, idle)
                    pool.tensor_scalar(t[1], t[2], -0.5, 1.5, ALU.mult, ALU.add).then_inc(norm_step, 1)
                    pool.wait_ge(norm_step, step(3))
                    pool.tensor_tensor(t[3], y, t[1], ALU.mult).then_inc(norm_step, 1)

                n[36] = pool.snap(g * 36)
                for i in range(NT + 2):
                    if i >= 2:
                        refine(i - 2)
                    if i < NT:
                        keys(i)

        @block.scalar
        def _(act):
            with act.Fori(0, R) as g:
                n = counts(act, g)
                n[36] = act.snap(g * 36)

                def split(u):
                    act.wait_ge(raw_in[u % 4], n[64] + 16 * (u // 4 + 1))
                    if u < 4:
                        act.wait_ge(proj_done, n[9])
                    else:
                        act.wait_ge(t_done, n[12] + 3 * (u - 3))
                    act.activation(w_hi[:, :, u % 4, :], raw[:, u % 4], ACT.Copy).then_inc(hi_done, 1)

                def read_block(j):
                    for c in range(3):
                        at, src = pieces[c], ps_p[(3 * j + c) % 2][:, 0:PIECE]
                        act.wait_ge(t_done, n[12] + (3 * j + c + 1))
                        if j == 0:
                            if c == 0:
                                act.wait_ge(out_done, n[9])
                            act.activation(log_f[:, at], src, ACT.Sigmoid)
                            last = act.activation(hk[:, at], src, ACT.Sigmoid, scale=-1.0)
                        elif j == 1:
                            last = act.activation(hq[:, at], src, ACT.Copy, scale=SCALE)
                        else:
                            last = act.activation(gate[:, j - 2, at], src, ACT.Silu)
                        last.then_inc(t_read, 1)

                split(0)
                split(1)
                read_block(0)
                split(2)
                read_block(1)
                act.wait_ge(f_done, n[1] + 1)
                act.activation(log_f[:, :], log_f[:, :], ACT.Ln).then_inc(logf_done, 1)
                split(3)
                split(4)
                read_block(2)
                split(5)
                read_block(3)
                split(6)
                split(7)
                act.preload_act_table_set("natural_log_exp_and_others")

                def squares_of(i):
                    w, b = width(i), i % 2
                    act.wait_ge(o_done, n[9] + (i + 1))
                    for c in range(2):
                        last = act.activation(squares[0:w, c, :], ps_o[0:w, c, :], ACT.Square,
                                              scale=float(P) ** -0.5, accum_out=mean_sq[0:w, b, c:c + 1])
                    last.then_inc(ms_done, 1)
                    act.wait_ge(ms_done, n[9] + (i + 1))
                    act.activation(norm[0:w, b, 1, :], mean_sq[0:w, b, :], ACT.Ln, bias=s.eps[0:w, :])\
                       .then_inc(seed_log, 1)
                    act.wait_ge(seed_log, n[9] + (i + 1))
                    act.activation(norm[0:w, b, 0, :], norm[0:w, b, 1, :], ACT.Exp, scale=-0.5)
                    act.activation(mean_sq[0:w, b, :], mean_sq[0:w, b, :], ACT.Identity, bias=s.eps[0:w, :])\
                       .then_inc(seed_done, 1)

                def normalise(i):
                    w, b = width(i), i % 2
                    act.wait_ge(norm_step, n[36] + 4 * (i + 1))
                    act.wait_ge(ot_done, n[9] + i)
                    for c in range(2):
                        last = act.activation(normed[0:w, c, :], ps_o[0:w, c, :], ACT.Copy,
                                              scale=norm[0:w, b, 3, c:c + 1])
                    last.then_inc(normed_done, 1)

                def decays(i):
                    w = width(i)
                    act.wait_ge(diff_done, n[9] + (i + 1))
                    parts = [(0, 9)] if w == P else [(0, 1), (3, 9)]
                    for lo, hi in parts:
                        last = act.activation(decay[:, lo:hi, 0:w], decay[:, lo:hi, 0:w], ACT.Abs)
                    last.then_inc(abs_done, 1)
                    act.wait_ge(abs_done, n[9] + (i + 1))
                    for lo, hi in parts:
                        last = act.activation(decay[:, lo:hi, 0:w], decay[:, lo:hi, 0:w], ACT.Exp, scale=-1.0)
                    last.then_inc(exp_done, 1)

                def copies(i):
                    w, b = width(i), i % 2
                    act.wait_ge(tr_done, n[9] + (i + 1))
                    if w == P:
                        act.activation(turned[:, :, :], ps_tr[:, 0:3, :], ACT.Copy).then_inc(qkt_done, 1)
                        act.wait_ge(masked_done, n[9] + (i + 1))
                        act.activation(a_hg[0:64, b, 64:128], wide[0:64, 64:128], ACT.Copy)
                        act.activation(a_hg[0:32, b, 32:64], wide[0:32, 32:64], ACT.Copy)
                        act.activation(a_hg[64:96, b, 96:128], wide[64:96, 96:128], ACT.Copy)\
                           .then_inc(ahc_done, 1)
                    else:
                        act.activation(turned[:, 0:2, 0:w], ps_tr[:, 0:2, 0:w], ACT.Copy)
                        act.activation(turned[0:w, 2, :], ps_tr[0:w, 2, :], ACT.Copy).then_inc(qkt_done, 1)

                def values(i):
                    w, b = width(i), i % 2
                    act.wait_ge(proj_done, n[9] + (i + 1))
                    if i >= 2:
                        act.wait_ge(roped, n[9] + (i - 1))
                    act.activation(qkv[0:w, b, :], ps_p[b][0:w, :], ACT.Copy).then_inc(v_done, 1)
                    act.wait_ge(rot_done, n[9] + (i + 1))
                    act.wait_ge(kd_copied, n[1] + 1)
                    act.activation(k_dec[0:w, b, :], rot[0:w, 1].rearrange("p a d -> p (a d)"), ACT.Copy,
                                   scale=kd_col[0:w, 0:1] if w == P else kd_col[0:w, 1:2]).then_inc(kdec_done, 1)

                def store_states(which, i, stored):
                    act.wait_ge(s_done, n[9] + (i + 1))
                    buf = s_pr if which == "prompt" else s_sa
                    for c, name in enumerate(("ret", "hgrn")):
                        act.dma_start(s.outs[f"state_{name}_{which}"][0, 0, bass.ds(n[1], 1)]
                                      .rearrange("h k v -> k h v"), buf[:, c:c + 1, :]).then_inc(stored, 16)

                for i in range(NT + 2):
                    if i >= 2:
                        squares_of(i - 2)
                    if i < NT:
                        decays(i)
                    if i >= 2:
                        normalise(i - 2)
                    if 1 <= i <= NT:
                        copies(i - 1)
                    if i < NT:
                        values(i)
                    if i >= 2:
                        t = i - 2
                        w = width(t)
                        act.wait_ge(out_done, n[9] + (t + 1))
                        dst = s.o_scr.rearrange("(c g p) t -> g p c t", c=2, g=HEADS)
                        act.dma_start(dst[bass.ds(n[1], 1), :, :, t * P:t * P + w].rearrange("g p c t -> (g p) c t"),
                                      o_out[:, t % 2, :, 0:w]).then_inc(o_stored[t % 2], 16)
                    if i == NT:
                        store_states("prompt", NP_T - 1, sp_stored)
                    if i == NT + 1:
                        store_states("sample", NT - 1, ss_stored)
                        act.wait_ge(ada_read, n[2] + 2)
                        act.dma_start(s.mod_scr[:, bass.ds(act.snap(g * D), D)], ada_row[:, :]).then_inc(ada_out, 16)
            act.wait_ge(o_stored[0], 16 * 5 * R)
            act.wait_ge(o_stored[1], 16 * 4 * R)
            act.wait_ge(sp_stored, 32 * R)
            act.wait_ge(ss_stored, 32 * R)
            act.wait_ge(ada_out, 16 * R)

        @block.tensor
        def _(pe):
            pe.wait_ge(cleared, 1)
            with pe.Fori(0, R) as g:
                n = counts(pe, g)

                def turned_block(j):
                    pe.wait_ge(lo_done, n[8] + (j + 1))
                    for c in range(3):
                        p = 3 * j + c
                        if p == 0:
                            pe.wait_ge(ada_read, n[2])
                            pe.wait_ge(v_done, n[9])
                        elif p >= 2:
                            pe.wait_ge(t_read, n[12] + (p - 1))
                        at = pieces[c]
                        for k in range(KD):
                            whi, wlo = w_hi[:, k, j, :], w_lo[:, k, j, :]
                            xhi, xlo = s.h_hi[:, k, at], s.h_lo[:, k, at]
                            out = ps_p[p % 2][:, 0:PIECE]
                            pe.matmul(out, whi, xhi, start=(k == 0), stop=False)
                            pe.matmul(out, whi, xlo, start=False, stop=False)
                            last = pe.matmul(out, wlo, xhi, start=False, stop=(k == KD - 1))
                        last.then_inc(t_done, 1)

                def project(i, half):
                    w = width(i)
                    out = ps_p[i % 2][0:w, :]
                    if half == 0:
                        if i == 0:
                            pe.wait_ge(lo_done, n[8] + 8)
                            pe.wait_ge(t_read, n[12] + 12)
                        elif i >= 2:
                            pe.wait_ge(v_done, n[9] + (i - 1))
                    for k in range(4 * half, 4 * half + 4):
                        xhi, xlo = s.h_hi[:, k, i * P:i * P + w], s.h_lo[:, k, i * P:i * P + w]
                        whi = w_hi[:, k].rearrange("p u n -> p (u n)")
                        wlo = w_lo[:, k].rearrange("p u n -> p (u n)")
                        pe.matmul(out, xhi, whi, start=(k == 0), stop=False)
                        pe.matmul(out, xhi, wlo, start=False, stop=False)
                        last = pe.matmul(out, xlo, whi, start=False, stop=(k == KD - 1))
                    if half:
                        last.then_inc(proj_done, 1)

                def scores(i):
                    w = width(i)
                    pe.wait_ge(rot_done, n[9] + (i + 1))
                    pe.wait_ge(qkt_done, n[9] + i)
                    pe.wait_ge(kl_done, n[9] + (i + 1))
                    if w < P:
                        carry(pe, idle)
                    for c in range(2):
                        pe.transpose(ps_tr[:, c, 0:w], rot[0:w, c].rearrange("p a d -> p (a d)"), ident[0:w, 0:w])
                    pe.transpose(ps_tr[0:w, 2, :], k_lv[:, 0, 0:w], ident).then_inc(tr_done, 1)
                    pe.wait_ge(ql_done, n[9] + (i + 1))
                    pe.wait_ge(ah_done, n[9] + i)
                    pe.wait_ge(ahc_done, n[8] + min(i, 8))
                    if w < P:
                        carry(pe, idle)
                    if w == P:
                        pe.matmul(wide[0:64, 64:128], k_lv[:, 1, 0:64], q_lv[:, 0, 64:128], start=True, stop=True)
                        for lo in (0, 64):
                            pe.matmul(wide[lo:lo + 32, lo + 32:lo + 64], k_lv[:, 2, lo:lo + 32],
                                      q_lv[:, 1, lo + 32:lo + 64], start=True, stop=True)
                    for j in range(w // 32):
                        at = slice(32 * j, 32 * j + 32)
                        for c in range(SMALL):
                            pe.matmul(lv[at, c, :], k_lv[:, 3 + c, at], q_lv[:, 2 + c, at], start=True, stop=True)
                        tok = slice(i * P + 32 * j, i * P + 32 * j + 32)
                        last = pe.matmul(lv[at, SMALL, :], hk[:, tok], hq[:, tok], start=True, stop=True)
                    last.then_inc(lv_done, 1)
                    pe.wait_ge(qkt_done, n[9] + (i + 1))
                    pe.wait_ge(ar_done, n[9] + i)
                    if w < P:
                        carry(pe, idle)
                    pe.matmul(ps_a[0:w, 0:w], k_t[:, 0:w], q_t[:, 0:w], start=True, stop=True).then_inc(ra_done, 1)

                def mix(i):
                    w, b = width(i), i % 2
                    st = s_pr if i < NP_T else s_sa
                    pe.wait_ge(v_done, n[9] + (i + 1))
                    pe.wait_ge(kdec_done, n[9] + (i + 1))
                    pe.wait_ge(qd_done, n[9] + (i + 1))
                    pe.wait_ge(normed_done, n[9] + i)
                    pe.wait_ge(s_done, n[9] + i)
                    pe.wait_ge(ar_done, n[9] + (i + 1))
                    if i == NP_T:
                        pe.wait_ge(ss_in, n[32] + 32)
                    if w < P:
                        carry(pe, idle)
                    pe.matmul(ps_o[0:w, 0, :], a_ret[0:w, 0:w], qkv[0:w, b, 256:384], start=True, stop=(i == 0))
                    if i:
                        pe.matmul(ps_o[0:w, 0, :], qd_t[:, 0:w], st[:, 0, :], start=False, stop=True)
                    pe.matmul(ps_s[:, 0, :], k_dec[0:w, b, :], qkv[0:w, b, 256:384], start=True, stop=True)
                    pe.matmul(ps_s[:, 1, :], hk_dec[0:w, :], qkv[0:w, b, 384:512], start=True, stop=True)
                    pe.wait_ge(ah_done, n[9] + (i + 1))
                    if w == P:
                        pe.wait_ge(ahc_done, n[8] + (i + 1))
                    else:
                        carry(pe, idle)
                    last = pe.matmul(ps_o[0:w, 1, :], a_hg[0:w, b, 0:w], qkv[0:w, b, 384:512], start=True, stop=(i == 0))
                    if i:
                        last = pe.matmul(ps_o[0:w, 1, :], q_in[:, b, 0:w], st[:, 1, :], start=False, stop=True)
                    last.then_inc(o_done, 1)

                def turn_out(i):
                    w = width(i)
                    pe.wait_ge(normed_done, n[9] + (i + 1))
                    pe.wait_ge(out_done, n[9] + i)
                    if w < P:
                        carry(pe, idle)
                    for c in range(2):
                        last = pe.transpose(ps_ot[:, c, 0:w], normed[0:w, c, :], ident[0:w, 0:w])
                    last.then_inc(ot_done, 1)

                def condition(units):
                    for u in units:
                        pe.wait_ge(raw_in[u % 4], n[64] + 16 * (u // 4 + 3))
                        if u % 4 == 0:
                            pe.wait_ge(v_done, n[9] + (8 + u // 4))
                        for k in range(KD):
                            last = pe.matmul(ps_p[1 - u // 4][0:2, (u % 4) * P:(u % 4 + 1) * P], s.cT[:, k, :],
                                             raw[:, u % 4, k, :], start=(k == 0), stop=(k == KD - 1))
                        last.then_inc(ada_done, 1)

                for j in range(4):
                    turned_block(j)
                for i in range(NT):
                    project(i, 0)
                    if i >= 2:
                        turn_out(i - 2)
                    if i >= 1:
                        scores(i - 1)
                    project(i, 1)
                    if i >= 1:
                        mix(i - 1)
                condition(range(0, 3))
                turn_out(NT - 2)
                scores(NT - 1)
                condition(range(3, 6))
                mix(NT - 1)
                condition(range(6, 8))
                turn_out(NT - 1)

        @block.vector
        def _(dve):
            with dve.Fori(0, R) as g:
                n = counts(dve, g)
                bound_at = lambda c: s.bound[:, c, bass.ds(n[1], 1)]

                def split(u):
                    dve.wait_ge(hi_done, n[8] + (u + 1))
                    dve.tensor_tensor(w_lo[:, :, u % 4, :], raw[:, u % 4], f32(w_hi[:, :, u % 4, :]),
                                      ALU.subtract).then_inc(lo_done, 1)

                dve.wait_ge(kdec_done, n[9])
                col = dve.snap(g * 2 + AT["k_decay"])
                dve.tensor_scalar(kd_col[:, :], s.consts[:, bass.ds(col, 2)], 1.0, None, ALU.mult)\
                   .then_inc(kd_copied, 1)
                split(0)
                split(1)
                dve.wait_ge(t_read, n[12] + 3)
                dve.tensor_scalar(log_f[:, :], log_f[:, :], bound_at(1), bound_at(0), ALU.mult, ALU.add)\
                   .then_inc(f_done, 1)
                dve.tensor_scalar(hk[:, :], hk[:, :], bound_at(1), None, ALU.mult).then_inc(hk_done, 1)
                for u in range(2, 8):
                    split(u)

                def state(i):
                    w = width(i)
                    dve.wait_ge(o_done, n[9] + (i + 1))
                    dve.wait_ge(s_done, n[9] + i)
                    if i == 0:
                        dve.wait_ge(sp_stored, n[32])
                        dve.tensor_copy(s_pr[:, :, :], ps_s[:, 0:2, :]).then_inc(s_done, 1)
                        return
                    st = s_pr if i < NP_T else s_sa
                    if i == NP_T:
                        dve.wait_ge(ss_in, n[32] + 32)
                    col = dve.snap(g * 2 + (AT["s_decay"] + (0 if w == P else 1)))
                    dve.scalar_tensor_tensor(out=st[:, 0, :], in0=st[:, 0, :], scalar=s.consts[:, bass.ds(col, 1)],
                                             in1=ps_s[:, 0, :], op0=ALU.mult, op1=ALU.add)
                    dve.scalar_tensor_tensor(out=st[:, 1, :], in0=st[:, 1, :], scalar=last_f[:, i % 2:i % 2 + 1],
                                             in1=ps_s[:, 1, :], op0=ALU.mult, op1=ALU.add).then_inc(s_done, 1)

                def differences(i):
                    w = width(i)
                    if i == 0:
                        dve.wait_ge(logf_done, n[1] + 1)
                    dve.wait_ge(kl_done, n[9] + i)
                    dve.wait_ge(ql_done, n[9] + i)
                    b = decay[:, 8, 0:w]
                    dve.tensor_tensor_scan(b, ones[:, 0:w], log_f[:, i * P:i * P + w], 0.0, ALU.mult, ALU.add)\
                       .then_inc(cum_done, 1)
                    dve.wait_ge(cum_done, n[9] + (i + 1))
                    for c, h in enumerate(LEVELS):
                        if 2 * h > w:
                            continue
                        x = b.rearrange("p (n t) -> p n t", t=2 * h)
                        dve.tensor_tensor(decay[:, 1 + c, 0:w].rearrange("p (n t) -> p n t", t=2 * h), x,
                                          x[:, :, h - 1:h].broadcast_to([P, w // (2 * h), 2 * h]), ALU.subtract)
                    dve.tensor_scalar(decay[:, 0, 0:w], b, decay[:, 8, w - 1:w], None, ALU.subtract)\
                       .then_inc(diff_done, 1)

                def gated(i):
                    w, b = width(i), i % 2
                    dve.wait_ge(ot_done, n[9] + (i + 1))
                    use = i // 2
                    dve.wait_ge(o_stored[b], (n[16] * (5 if b == 0 else 4)) + 16 * use)
                    for c in range(2):
                        col = dve.snap(g * 1 + (32 + 4 * c))
                        last = dve.scalar_tensor_tensor(
                            out=o_out[:, b, c, 0:w], in0=ps_ot[:, c, 0:w], scalar=s.cols[:, bass.ds(col, 1)],
                            in1=gate[:, c, i * P:i * P + w], op0=ALU.mult, op1=ALU.mult)
                    last.then_inc(out_done, 1)

                def scored(i):
                    w, b = width(i), i % 2
                    dve.wait_ge(qkt_done, n[9] + (i + 1))
                    qd = dve.snap(g * P + AT["q_decay"])
                    dve.tensor_tensor(qd_t[:, 0:w], q_t[:, 0:w], s.consts[:, bass.ds(qd, w)], ALU.mult)\
                       .then_inc(qd_done, 1)
                    dve.wait_ge(lv_done, n[9] + (i + 1))
                    dve.wait_ge(ah_done, n[9] + i)
                    mask = s.const("level_mask")[0:w].rearrange("p (s l) -> p s l", l=32)
                    dve.tensor_tensor(masked[0:w], lv[0:w], mask, ALU.mult).then_inc(masked_done, 1)
                    dve.wait_ge(masked_done, n[9] + (i + 1))
                    for j in range(w // 32):
                        at = slice(32 * j, 32 * j + 32)
                        last = dve.tensor_reduce(a_hg[at, b, at], masked[at].rearrange("p s l -> p l s"), AX, ALU.add)
                    last.then_inc(ah_done, 1)
                    dve.wait_ge(ra_done, n[9] + (i + 1))
                    rd = dve.snap(g * P + AT["ret_decay"])
                    dve.tensor_tensor(a_ret[0:w, 0:w], ps_a[0:w, 0:w], s.consts[0:w, bass.ds(rd, w)], ALU.mult)\
                       .then_inc(ar_done, 1)

                def queries(i):
                    w, b = width(i), i % 2
                    dve.wait_ge(exp_done, n[9] + (i + 1))
                    dve.wait_ge(lv_done, n[9] + i)
                    dve.tensor_copy(last_f[:, b:b + 1], decay[:, 8, w - 1:w])
                    q = hq[:, i * P:i * P + w]
                    lo = 0 if w == P else 2
                    dve.tensor_tensor(q_in[:, b, 0:w], decay[:, 8, 0:w], q, ALU.mult)
                    dve.tensor_tensor(q_lv[:, lo:7, 0:w], decay[:, 1 + lo:8, 0:w],
                                      q.unsqueeze(1).broadcast_to([P, 7 - lo, w]), ALU.mult).then_inc(ql_done, 1)

                def rotary(i):
                    w = width(i)
                    dve.wait_ge(v_done, n[9] + (i + 1))
                    dve.wait_ge(rot_done, n[9] + i)
                    qk = qkv[0:w, i % 2, 0:256].rearrange("p (c d) -> p c d", c=4)
                    for name, out in (("cos", qk_cos), ("sin", qk_sin)):
                        tab = s.consts[0:w, AT[name] + 64 * i:AT[name] + 64 * i + 64]
                        last = dve.tensor_tensor(out[0:w], qk, tab.unsqueeze(1).broadcast_to([w, 4, 64]), ALU.mult)
                    last.then_inc(roped, 1)
                    dve.wait_ge(roped, n[9] + (i + 1))
                    if i:
                        dve.wait_ge(kdec_done, n[9] + i)
                    pair = lambda t, half: t[0:w].rearrange("p (c a) d -> p c a d", a=2)[:, :, half, :]
                    dve.tensor_tensor(rot[0:w, :, 0, :], pair(qk_cos, 0), pair(qk_sin, 1), ALU.subtract)
                    dve.tensor_tensor(rot[0:w, :, 1, :], pair(qk_cos, 1), pair(qk_sin, 0), ALU.add)\
                       .then_inc(rot_done, 1)

                def conditioned(half):
                    dve.wait_ge(ada_done, n[8] + (4 * half + 4))
                    if half == 0:
                        dve.wait_ge(bias_in, n[16] + 16)
                        dve.wait_ge(ada_out, n[16])
                    at = slice(512 * half, 512 * half + 512)
                    dve.tensor_tensor(ada_row[:, at], ps_p[1 - half][0:2, :], ada_bias[:, at], ALU.add).then_inc(ada_read, 1)

                for i in range(NT + 2):
                    if i >= 2:
                        state(i - 2)
                    if i < NT:
                        differences(i)
                    if i >= 2:
                        gated(i - 2)
                    if 1 <= i <= NT:
                        scored(i - 1)
                    if i < NT:
                        queries(i)
                        rotary(i)
                    if i == NT:
                        conditioned(0)
                conditioned(1)


def phase_output(nc, s):
    with ExitStack() as ctx:
        sb, ps, sem = allocate(nc, ctx, "output")
        raw = sb("raw", [P, 3, D])
        w_hi = sb("w_hi", [P, KD, D], F32R)
        w_lo = sb("w_lo", [P, KD, D], F32R)
        mod = sb("mod", [P, 2, 3, D])
        gain = sb("gain", [P, D])
        o_raw = sb("o_raw", [P, KD, P])
        o_hi = sb("o_hi", [P, 2, KD, P], F32R)
        o_lo = sb("o_lo", [P, 2, KD, P], F32R)
        x_old = sb("x_old", [P, 2, D])
        x_new = sb("x_new", [P, 2, D])
        h2 = sb("h2", [P, NT, D])
        h2_t = sb("h2_t", [P, KD, P])
        squares = sb("squares", [P, D])
        w_route = sb("w_route", [P, KD, N_GROUPS + NE])
        b_route = sb("b_route", [P, N_GROUPS + NE])
        mean_sq = sb("mean_sq", [P, NT])
        rstd = sb("rstd", [P, NT])
        logits = sb("logits", [P, NT, N_GROUPS + NE])
        ps_o = [ps(f"ps_o{b}", [P, 2, 512]) for b in range(2)]
        ps_t = ps("ps_t", [P, KD, P])
        ps_l = ps("ps_l", [P, 512])
        ps_r = ps("ps_r", [P, 512])

        raw_in = [sem(f"raw_in{n}") for n in range(3)]
        o_in, x_in = sem("o_in"), [sem(f"x_in{n}") for n in range(2)]
        rows_in, route_in = sem("rows_in"), sem("route_in")
        hi_done, lo_done, ohi_done, olo_done = sem("hi_done"), sem("lo_done"), sem("ohi_done"), sem("olo_done")
        gain_done, mm_done, gated, added, x_stored = (sem("gain_done"), sem("mm_done"), sem("gated"), sem("added"),
                                                      sem("x_stored"))
        ms_done, root_done, rstd_done, scaled, h2_done = (sem("ms_done"), sem("root_done"), sem("rstd_done"),
                                                          sem("scaled"), sem("h2_done"))
        t_done, t_read, l_done, l_read = sem("t_done"), sem("t_read"), sem("l_done"), sem("l_read")
        zeroed, pad_stored, cleared = sem("zeroed"), sem("pad_stored"), sem("cleared")
        route, exp_done, picked, counted = sem("route"), sem("exp_done"), sem("picked"), sem("counted")
        slots_done, scattered = sem("slots_done"), sem("scattered")
        less_max = sem("less_max")
        gp = sb("group_p", [P, NT, N_GROUPS])
        eq4 = sb("eq4", [P, NT, 4])
        one_g = sb("one_group", [P, NT, 4])
        ep = sb("expert_p", [P, NT, PER_GROUP])
        one_e = sb("one_expert", [P, 2, NT, 4])
        col = sb("col", [P, NT])
        group_w = sb("group_w", [P, NT])
        top = sb("top", [P, 2, NT])
        chosen = sb("chosen", [P, 2, NT, NE])
        both = sb("both", [P, NT, NE])
        before = sb("before", [P, NT, NE])
        prod = sb("prod", [P, NT, NE])
        n_of = sb("n_of", [P, NE])
        first = sb("first", [P, NE + 1])
        over = sb("over", [P, NE, 8])
        extra = sb("extra", [P, NE])
        tiles = sb("tiles", [P, NE + 1])
        slot_f = sb("slot_f", [P, 2, NT])
        block = ctx.enter_context(nc.Block())
        a = s.args
        ident = s.const("ident")

        @block.sync
        def _(sp):
            def w_out(k):
                if k >= 3:
                    sp.wait_ge(lo_done, k - 2)
                sp.dma_start(raw[:, k % 3], a["W_out"][0, k * P:(k + 1) * P, :]).then_inc(raw_in[k % 3], 16)

            def tile_in(i):
                w = width(i)
                if i:
                    sp.wait_ge(olo_done, i)
                sp.dma_start(o_raw[:, :, 0:w], s.o_scr.rearrange("(k p) t -> p k t", p=P)[:, :, i * P:i * P + w])\
                  .then_inc(o_in, 16)
                if i >= 2:
                    sp.wait_ge(added, i - 1)
                src = a["x_prompt"][0, i * P:(i + 1) * P, :] if i < NP_T else a["x_sample"][0]
                sp.dma_start(x_old[0:w, i % 2, :], src).then_inc(x_in[i % 2], 16)

            for k in range(3):
                w_out(k)
            tile_in(0)
            for k in range(3, KD):
                w_out(k)
            for q, rows in ((0, P), (1, DEC)):
                sp.dma_start(mod[0:rows, q].rearrange("p c d -> p (c d)"),
                             s.mod_scr[q:q + 1, 0:3 * D].broadcast_to([rows, 3 * D])).then_inc(rows_in, 16)
            sp.dma_start(gain[:, :], a["norm2_g"].broadcast_to([P, D])).then_inc(rows_in, 16)
            sp.dma_start(w_route[:, :, 0:4], a["W_router_group"][0].rearrange("(k p) n -> p k n", p=P))\
              .then_inc(route_in, 16)
            sp.dma_start(w_route[:, :, 4:20], a["W_router_expert"][0].rearrange("(k p) n -> p k n", p=P))\
              .then_inc(route_in, 16)
            sp.dma_start(b_route[:, 0:4], a["b_router_group"].broadcast_to([P, 4])).then_inc(route_in, 16)
            sp.dma_start(b_route[:, 4:20], a["b_router_expert"].broadcast_to([P, NE])).then_inc(route_in, 16)
            sp.wait_ge(zeroed, 1)
            sp.dma_start(s.xs_scr[SLOTS:SLOTS + P, :], squares[:, :]).then_inc(pad_stored, 16)
            for i in range(NT):
                if i + 1 < NT:
                    tile_in(i + 1)
                w = width(i)
                sp.wait_ge(added, i + 1)
                sp.dma_start(s.x_scr[i * P:i * P + w, :], x_new[0:w, i % 2, :]).then_inc(x_stored, 16)
            sp.wait_ge(x_stored, 16 * NT)
            sp.wait_ge(pad_stored, 16)

        @block.gpsimd
        def _(pool):
            pool.memset(squares[:, :], 0.0).then_inc(zeroed, 1)
            pool.memset(logits[:, :, :], 0.0).then_inc(cleared, 1)
            pool.wait_ge(slots_done, 1)
            for i in range(NT):
                w = width(i)
                for c in range(2):
                    pool.indirect_dma_start(out=s.xs_scr[0:SLOTS, :],
                                            out_offset=bass.IndirectOffsetOnAxis(ap=s.slot[0:w, c, i:i + 1], axis=0),
                                            in_=h2[0:w, i, :], in_offset=None).then_inc(scattered, 16)
            pool.wait_ge(scattered, 16 * 2 * NT)

        @block.scalar
        def _(act):
            def o_high(i):
                w = width(i)
                act.wait_ge(o_in, 16 * (i + 1))
                if i >= 2:
                    act.wait_ge(mm_done, 2 * (i - 1))
                act.activation(o_hi[:, i % 2, :, 0:w], o_raw[:, :, 0:w], ACT.Copy).then_inc(ohi_done, 1)

            def turned(i):
                w = width(i)
                act.wait_ge(t_done, i + 1)
                for c in range(2):
                    last = act.activation(h2_t[:, 4 * c:4 * c + 4, 0:w], ps_t[:, 4 * c:4 * c + 4, 0:w], ACT.Copy)
                last.then_inc(t_read, 1)

            for k in range(KD):
                act.wait_ge(raw_in[k % 3], 16 * (k // 3 + 1))
                act.activation(w_hi[:, k], raw[:, k % 3], ACT.Copy).then_inc(hi_done, 1)
                if k == 2:
                    o_high(0)
            act.wait_ge(pad_stored, 16)
            for i in range(NT):
                w = width(i)
                if i + 1 < NT:
                    o_high(i + 1)
                act.wait_ge(added, i + 1)
                if i:
                    act.wait_ge(ms_done, i)
                act.activation(squares[0:w, :], x_new[0:w, i % 2, :], ACT.Square, scale=1.0 / 32.0,
                               accum_out=mean_sq[0:w, i:i + 1]).then_inc(ms_done, 1)
                act.wait_ge(ms_done, i + 1)
                act.activation(rstd[0:w, i:i + 1], mean_sq[0:w, i:i + 1], ACT.Sqrt, bias=s.eps[0:w, :])\
                   .then_inc(root_done, 1)
                if i:
                    turned(i - 1)
            turned(NT - 1)
            for n, probs in enumerate((gp, ep)):
                act.wait_ge(less_max, n + 1)
                act.activation(probs[:, :, :], probs[:, :, :], ACT.Exp).then_inc(exp_done, 1)

        @block.tensor
        def _(pe):
            def to_logits(i):
                w = width(i)
                pe.wait_ge(h2_done, i + 1)
                pe.wait_ge(t_read, i)
                for k in range(KD):
                    last = pe.transpose(ps_t[:, k, 0:w], h2[0:w, i, k * P:(k + 1) * P], ident[0:w, 0:w])
                last.then_inc(t_done, 1)

            def score(i):
                w = width(i)
                pe.wait_ge(t_read, i + 1)
                pe.wait_ge(l_read, i)
                for k in range(KD):
                    last = pe.matmul(ps_l[0:w, 0:20], h2_t[:, k, 0:w], w_route[:, k, :],
                                     start=(k == 0), stop=(k == KD - 1))
                last.then_inc(l_done, 1)

            for i in range(NT):
                w, b = width(i), i % 2
                pe.wait_ge(olo_done, i + 1)
                if i >= 2:
                    pe.wait_ge(gated, i - 1)
                for c in range(2):
                    for k in range(KD):
                        if i == 0 and c == 0:
                            pe.wait_ge(lo_done, k + 1)
                        at = slice(512 * c, 512 * c + 512)
                        out = ps_o[b][0:w, c, :]
                        hi, lo = o_hi[:, b, k, 0:w], o_lo[:, b, k, 0:w]
                        pe.matmul(out, hi, w_hi[:, k, at], start=(k == 0), stop=False)
                        pe.matmul(out, hi, w_lo[:, k, at], start=False, stop=False)
                        last = pe.matmul(out, lo, w_hi[:, k, at], start=False, stop=(k == KD - 1))
                    last.then_inc(mm_done, 1)
                    if i and c == 0:
                        to_logits(i - 1)
                if i == 1:
                    pe.wait_ge(route_in, 64)
                if i:
                    score(i - 1)
            to_logits(NT - 1)
            score(NT - 1)
            pe.wait_ge(picked, 1)
            flat = lambda t: t.rearrange("p t e -> p (t e)")
            pe.matmul(ps_r[:, 0:NT * NE], s.const("tri"), flat(both[:, :, :]), start=True, stop=False)
            pe.matmul(ps_r[:, 0:NT * NE], s.const("ones"), flat(before[:, :, :]), start=False, stop=True)
            pe.matmul(ps_r[:, 256:256 + NE], s.const("ones"), prod[:, 0, :], start=True, stop=True)\
              .then_inc(counted, 1)

        @block.vector
        def _(dve):
            def o_low(i):
                w = width(i)
                dve.wait_ge(ohi_done, i + 1)
                dve.tensor_tensor(o_lo[:, i % 2, :, 0:w], o_raw[:, :, 0:w], f32(o_hi[:, i % 2, :, 0:w]),
                                  ALU.subtract).then_inc(olo_done, 1)

            def add_bias(i):
                w = width(i)
                dve.wait_ge(l_done, i + 1)
                dve.tensor_tensor(logits[0:w, i, :], ps_l[0:w, 0:20], b_route[0:w, :], ALU.add).then_inc(l_read, 1)

            for k in range(KD):
                dve.wait_ge(hi_done, k + 1)
                dve.tensor_tensor(w_lo[:, k], raw[:, k % 3], f32(w_hi[:, k]), ALU.subtract).then_inc(lo_done, 1)
                if k == 2:
                    o_low(0)
            dve.wait_ge(rows_in, 48)
            for q, rows in ((0, P), (1, DEC)):
                last = dve.scalar_tensor_tensor(out=mod[0:rows, q, 2], in0=mod[0:rows, q, 2], scalar=1.0,
                                                in1=gain[0:rows, :], op0=ALU.add, op1=ALU.mult)
            last.then_inc(gain_done, 1)
            dve.wait_ge(gain_done, 1)
            dve.wait_ge(route_in, 64)
            dve.wait_ge(cleared, 1)
            for i in range(NT):
                w, b, q = width(i), i % 2, i // NP_T
                if i + 1 < NT:
                    o_low(i + 1)
                dve.wait_ge(mm_done, 2 * i + 2)
                if i >= 2:
                    dve.wait_ge(x_stored, 16 * (i - 1))
                dve.tensor_tensor(x_new[0:w, b, :], ps_o[b][0:w].rearrange("p c d -> p (c d)"), mod[0:w, q, 0],
                                  ALU.mult).then_inc(gated, 1)
                dve.wait_ge(gated, i + 1)
                dve.wait_ge(x_in[b], 16 * (i // 2 + 1))
                dve.tensor_tensor(x_new[0:w, b, :], x_new[0:w, b, :], x_old[0:w, b, :], ALU.add).then_inc(added, 1)
                if i >= 2:
                    add_bias(i - 2)
                dve.wait_ge(root_done, i + 1)
                dve.reciprocal(rstd[0:w, i:i + 1], rstd[0:w, i:i + 1]).then_inc(rstd_done, 1)
                dve.wait_ge(rstd_done, i + 1)
                dve.scalar_tensor_tensor(out=h2[0:w, i, :], in0=x_new[0:w, b, :], scalar=rstd[0:w, i:i + 1],
                                         in1=mod[0:w, q, 2], op0=ALU.mult, op1=ALU.mult).then_inc(scaled, 1)
                dve.wait_ge(scaled, i + 1)
                dve.tensor_tensor(h2[0:w, i, :], h2[0:w, i, :], mod[0:w, q, 1], ALU.add).then_inc(h2_done, 1)
            add_bias(NT - 2)
            add_bias(NT - 1)
            steps = [0]

            def then(ins):
                steps[0] += 1
                ins.then_inc(route, 1)
                dve.wait_ge(route, steps[0])

            def wide(t, n=4):
                return t.unsqueeze(2).broadcast_to([P, NT, n])

            iota = s.const("iota")
            iota4 = iota[:, 0:4].unsqueeze(1).broadcast_to([P, NT, 4])

            def softmax(out, src, n):
                then(dve.tensor_reduce(col[:, :], src, AX, ALU.max))
                dve.tensor_tensor(out, src, wide(col[:, :]), ALU.subtract).then_inc(less_max, 1)
                dve.wait_ge(exp_done, n)
                then(dve.tensor_reduce(col[:, :], out, AX, ALU.add))
                then(dve.reciprocal(col[:, :], col[:, :]))
                then(dve.tensor_tensor(out, out, wide(col[:, :]), ALU.mult))

            def pick(one, value, probs):
                then(dve.tensor_reduce(value, probs, AX, ALU.max))
                then(dve.tensor_tensor(eq4[:, :, :], probs, wide(value), ALU.is_equal))
                then(dve.scalar_tensor_tensor(out=eq4[:, :, :], in0=eq4[:, :, :], scalar=-8.0, in1=iota4,
                                              op0=ALU.mult, op1=ALU.add))
                then(dve.tensor_reduce(col[:, :], eq4[:, :, :], AX, ALU.min))
                then(dve.tensor_tensor(one, eq4[:, :, :], wide(col[:, :]), ALU.is_equal))

            dve.wait_ge(l_read, NT)
            softmax(gp[:, :, :], logits[:, :, 0:4], 1)
            pick(one_g[:, :, :], group_w[:, :], gp[:, :, :])
            by_group = logits[:, :, 4:20].rearrange("p t (g e) -> p t g e", g=4)
            view = lambda t: t.rearrange("p t (g e) -> p t g e", g=4)
            then(dve.tensor_tensor(view(prod[:, :, :]), by_group,
                                   one_g[:, :, :].unsqueeze(3).broadcast_to([P, NT, 4, 4]), ALU.mult))
            then(dve.tensor_reduce(one_e[:, 0], view(prod[:, :, :]).rearrange("p t g e -> p t e g"), AX, ALU.add))
            softmax(ep[:, :, :], one_e[:, 0], 2)
            pick(one_e[:, 0], top[:, 0, :], ep[:, :, :])
            then(dve.scalar_tensor_tensor(out=ep[:, :, :], in0=one_e[:, 0], scalar=-2.0, in1=ep[:, :, :],
                                          op0=ALU.mult, op1=ALU.add))
            pick(one_e[:, 1], top[:, 1, :], ep[:, :, :])
            then(dve.tensor_tensor(col[:, :], top[:, 0, :], top[:, 1, :], ALU.add))
            then(dve.reciprocal(col[:, :], col[:, :]))
            then(dve.tensor_tensor(col[:, :], col[:, :], group_w[:, :], ALU.mult))
            for c in range(2):
                dve.tensor_tensor(s.weight[:, c, :], top[:, c, :], col[:, :], ALU.mult)
                then(dve.tensor_tensor(view(chosen[:, c]), one_g[:, :, :].unsqueeze(3).broadcast_to([P, NT, 4, 4]),
                                       one_e[:, c].unsqueeze(2).broadcast_to([P, NT, 4, 4]), ALU.mult))
                for lo, hi in ((DEC, 2 * DEC), (2 * DEC, P)):
                    then(dve.memset(chosen[lo:hi, c, NT - 1, :], 0.0))
            then(dve.tensor_tensor(both[:, :, :], chosen[:, 0], chosen[:, 1], ALU.add))
            then(dve.memset(before[:, 0, :], 0.0))
            for i in range(1, NT):
                then(dve.tensor_tensor(before[:, i, :], before[:, i - 1, :], both[:, i - 1, :], ALU.add))
            dve.tensor_tensor(prod[:, 0, :], before[:, NT - 1, :], both[:, NT - 1, :], ALU.add).then_inc(picked, 1)
            dve.wait_ge(counted, 1)
            then(dve.tensor_copy(n_of[:, :], ps_r[:, 256:256 + NE]))
            ones = s.const("ones")
            then(dve.memset(first[:, 0:1], 0.0))
            then(dve.tensor_tensor_scan(first[:, 1:NE + 1], ones[:, 0:NE], n_of[:, :], 0.0, ALU.mult, ALU.add))
            then(dve.tensor_tensor(over[:, :, :], n_of[:, :].unsqueeze(2).broadcast_to([P, NE, 8]),
                                   s.const("limits").unsqueeze(1).broadcast_to([P, NE, 8]), ALU.is_gt))
            then(dve.tensor_reduce(extra[:, :], over[:, :, :], AX, ALU.add))
            then(dve.memset(tiles[:, 0:1], 0.0))
            then(dve.tensor_tensor_scan(tiles[:, 1:NE + 1], ones[:, 0:NE], extra[:, :], 0.0, ALU.mult, ALU.add))
            then(dve.tensor_tensor(tiles[:, 0:NE], tiles[:, 0:NE], iota, ALU.add))
            then(dve.tensor_copy(s.plan[:, 0:NE + 1], first[0:1, :]))
            then(dve.tensor_copy(s.plan[:, 32:32 + NE], extra[0:1, :]))
            then(dve.tensor_copy(s.plan[:, 64:64 + NE], tiles[0:1, 0:NE]))
            counts = ps_r[:, 0:NT * NE].rearrange("p (t e) -> p t e", e=NE)
            then(dve.tensor_tensor(both[:, :, :], counts, first[:, 0:NE].unsqueeze(1).broadcast_to([P, NT, NE]),
                                   ALU.add))
            for c in range(2):
                then(dve.tensor_tensor(prod[:, :, :], both[:, :, :], chosen[:, c], ALU.mult))
                then(dve.tensor_reduce(slot_f[:, c, :], prod[:, :, :], AX, ALU.add))
            dve.tensor_copy(s.slot[:, :, :], slot_f[:, :, :]).then_inc(slots_done, 1)


def phase_experts(nc, s):
    CH, RAW = 12, 6
    with ExitStack() as ctx:
        sb, ps, sem = allocate(nc, ctx, "experts")
        raw = sb("raw", [P, RAW, D])
        w_hi = sb("w_hi", [P, CH, D], F32R)
        w_lo = sb("w_lo", [P, CH, D], F32R)
        x_rows = sb("x_rows", [P, D])
        x_hi = sb("x_hi", [P, KD, P], F32R)
        x_lo = sb("x_lo", [P, KD, P], F32R)
        act_g = sb("act_g", [P, 2, 256])
        hid = sb("hid", [P, 512])
        h_hi = sb("h_hi", [P, KF, P], F32R)
        h_lo = sb("h_lo", [P, KF, P], F32R)
        y = sb("y", [P, D])
        ps_g = [ps(f"ps_g{n}", [P, 512]) for n in range(2)]
        ps_x = [ps(f"ps_x{n}", [P, 4, P]) for n in range(2)]
        ps_h = [ps(f"ps_h{n}", [P, 4, P]) for n in range(2)]
        ps_y = [ps(f"ps_y{n}", [P, 512]) for n in range(2)]
        raw_in = [sem(f"raw_in{n}") for n in range(RAW)]
        hi_done, lo_done, used = sem("hi_done"), sem("lo_done"), sem("used")
        x_in, xt_done, xhi_done, xlo_done = sem("x_in"), sem("xt_done"), sem("xhi_done"), sem("xlo_done")
        silu_done, hid_done = sem("silu_done"), sem("hid_done")
        ht_done, hhi_done, hlo_done = sem("ht_done"), sem("hhi_done"), sem("hlo_done")
        y0_done, y1_done, y_stored, idle = sem("y0_done"), sem("y1_done"), sem("y_stored"), sem("idle")
        block = ctx.enter_context(nc.Block())
        a = s.args
        ident = s.const("ident")

        def experts(e, tile):
            def one(x, last_expert):
                extra = e.value_load(s.plan[0:1, bass.ds(x + 32, 1)], min_val=0, max_val=8)
                base = e.value_load(s.plan[0:1, bass.ds(x + 64, 1)], min_val=0, max_val=32)
                with e.If(extra > 0):
                    with e.Fori(0, extra) as j:
                        tile(x, e.snap(base + j), j, False, last_expert)
                tile(x, e.snap(base + extra), extra, True, last_expert)

            with e.Fori(0, NE - 1) as x:
                one(x, False)
            one(NE - 1, True)

        @block.sync
        def _(sp):
            def load(x, c, wait):
                dst = raw[:, c % RAW]
                at = x if isinstance(x, int) else sp.snap(x * 1)
                if wait is not None:
                    sp.wait_ge(lo_done, wait)
                    if not isinstance(wait, int):
                        carry(sp, idle)
                if c < 8:
                    half, rows = c // 4, slice((c % 4) * 256, (c % 4) * 256 + 256)
                    for m, name in enumerate(("W_gate_e", "W_up_e")):
                        src = a[name][0, bass.ds(at, 1), rows, half * 256:(half + 1) * 256]
                        sp.dma_start(dst.rearrange("p (k m n) -> p k m n", k=2, m=2)[:, :, m, :],
                                     src.rearrange("e (k p) n -> p (e k) n", p=P)).then_inc(raw_in[c % RAW], 16)
                else:
                    rows = slice((c - 8) * P, (c - 7) * P)
                    for m in range(2):
                        at_n = slice(512 * m, 512 * m + 512)
                        src = a["W_down_e"][0, bass.ds(at, 1), rows, at_n]
                        sp.dma_start(dst[:, at_n], src.rearrange("e p n -> p (e n)")).then_inc(raw_in[c % RAW], 16)

            for c in range(CH):
                load(0, c, c + 1 - RAW if c >= RAW else None)
            with sp.Fori(1, NE) as x:
                for c in range(CH):
                    load(x, c, sp.snap(x * CH + (c + 1 - RAW)))

        @block.gpsimd
        def _(pool):
            def load(row):
                pool.dma_start(x_rows[:, :], s.xs_scr[bass.ds(row, P), :]).then_inc(x_in, 16)

            pool.dma_start(x_rows[:, :], s.xs_scr[0:P, :]).then_inc(x_in, 16)

            def tile(x, t, j, last, _):
                start = pool.value_load(s.plan[0:1, bass.ds(x, 1)], min_val=0, max_val=SLOTS)
                row = pool.snap(start + j * P, min_val=0, max_val=SLOTS)
                if last:
                    after = pool.value_load(s.plan[0:1, bass.ds(x + 1, 1)], min_val=0, max_val=SLOTS)
                else:
                    after = pool.snap(start + j * P + P, min_val=0, max_val=SLOTS)
                pool.wait_ge(xt_done, pool.snap(t + 1))
                carry(pool, idle)
                load(after)
                pool.wait_ge(y_stored, pool.snap(t * 16))
                pool.wait_ge(y0_done, pool.snap(t + 1))
                pool.wait_ge(y1_done, pool.snap(t + 1))
                carry(pool, idle)
                pool.dma_start(s.y_scr[bass.ds(row, P), :], y[:, :]).then_inc(y_stored, 16)

            experts(pool, tile)
            total = pool.value_load(s.plan[0:1, 64 + NE - 1:64 + NE], min_val=0, max_val=32)
            extra = pool.value_load(s.plan[0:1, 32 + NE - 1:32 + NE], min_val=0, max_val=8)
            pool.wait_ge(y_stored, pool.snap((total + extra + 1) * 16))
            carry(pool, idle)

        @block.scalar
        def _(act):
            def split(x, c, t):
                act.wait_ge(raw_in[c % RAW], act.snap(x * 64 + 32 * (c // RAW + 1)) if t is not None
                            else 32 * (c // RAW + 1))
                if t is not None:
                    act.wait_ge(used, act.snap(t * CH + (c + 1)))
                act.activation(w_hi[:, c], raw[:, c % RAW], ACT.Copy).then_inc(hi_done, 1)

            def x_high(t):
                act.wait_ge(xt_done, t + 2 if isinstance(t, int) else act.snap(t + 2))
                for n in range(2):
                    act.activation(x_hi[:, 4 * n:4 * n + 4, :], ps_x[n][:, :, :], ACT.Copy).then_inc(xhi_done, 1)

            def tile(x, t, j, last, last_expert):
                splits = last and not last_expert
                after = act.snap(x + 1) if splits else None
                t2 = act.snap(t * 2)

                def some(lo, hi):
                    if splits:
                        for c in range(lo, hi):
                            split(after, c, t)

                def silu(n):
                    act.wait_ge(used, act.snap(t * CH + 4 * (n + 1)))
                    act.activation(act_g[:, n, :], ps_g[n][:, 0:256], ACT.Silu).then_inc(silu_done, 1)

                def h_high(n):
                    act.wait_ge(ht_done, act.snap(t2 + (n + 1)))
                    act.activation(h_hi[:, 2 * n:2 * n + 2, :], ps_h[n][:, 0:2, :], ACT.Copy).then_inc(hhi_done, 1)

                some(0, 3)
                silu(0)
                some(3, 6)
                silu(1)
                h_high(0)
                x_high(t)
                h_high(1)
                some(6, 9)
                act.wait_ge(used, act.snap(t * CH + CH))
                act.wait_ge(y_stored, act.snap(t * 16))
                act.activation(y[:, 0:512], ps_y[0][:, :], ACT.Copy).then_inc(y0_done, 1)
                some(9, CH)

            for c in range(6):
                split(0, c, None)
            x_high(-1)
            for c in range(6, CH):
                split(0, c, None)
            experts(act, tile)

        @block.vector
        def _(dve):
            def split(x, c, first):
                dve.wait_ge(hi_done, c + 1 if first else dve.snap(x * CH + (c + 1)))
                dve.tensor_tensor(w_lo[:, c], raw[:, c % RAW], f32(w_hi[:, c]), ALU.subtract).then_inc(lo_done, 1)

            def x_low(t):
                for n in range(2):
                    dve.wait_ge(xhi_done, 2 * t + n + 3 if isinstance(t, int) else dve.snap(t * 2 + (n + 3)))
                    last = dve.tensor_tensor(x_lo[:, 4 * n:4 * n + 4, :], ps_x[n][:, :, :],
                                             f32(x_hi[:, 4 * n:4 * n + 4, :]), ALU.subtract)
                last.then_inc(xlo_done, 1)

            def tile(x, t, j, last, last_expert):
                splits = last and not last_expert
                after = dve.snap(x + 1) if splits else None
                t2 = dve.snap(t * 2)

                def some(lo, hi):
                    if splits:
                        for c in range(lo, hi):
                            split(after, c, False)

                def product(n):
                    dve.wait_ge(silu_done, dve.snap(t2 + (n + 1)))
                    dve.tensor_tensor(hid[:, 256 * n:256 * n + 256], act_g[:, n, :], ps_g[n][:, 256:512],
                                      ALU.mult).then_inc(hid_done, 1)

                def h_low(n):
                    dve.wait_ge(hhi_done, dve.snap(t2 + (n + 1)))
                    dve.tensor_tensor(h_lo[:, 2 * n:2 * n + 2, :], ps_h[n][:, 0:2, :],
                                      f32(h_hi[:, 2 * n:2 * n + 2, :]), ALU.subtract).then_inc(hlo_done, 1)

                some(0, 3)
                product(0)
                some(3, 6)
                product(1)
                h_low(0)
                x_low(t)
                h_low(1)
                some(6, 9)
                dve.wait_ge(used, dve.snap(t * CH + CH))
                dve.wait_ge(y_stored, dve.snap(t * 16))
                dve.tensor_copy(y[:, 512:1024], ps_y[1][:, :]).then_inc(y1_done, 1)
                some(9, CH)

            for c in range(6):
                split(0, c, True)
            x_low(-1)
            for c in range(6, CH):
                split(0, c, True)
            experts(dve, tile)

        @block.tensor
        def _(pe):
            def turn_x(t):
                if isinstance(t, int):
                    pe.wait_ge(x_in, 16)
                else:
                    pe.wait_ge(x_in, pe.snap(t * 16 + 32))
                    pe.wait_ge(xlo_done, pe.snap(t + 1))
                for k in range(KD):
                    last = pe.transpose(ps_x[k // 4][:, k % 4, :], x_rows[:, k * P:(k + 1) * P], ident)
                last.then_inc(xt_done, 1)

            turn_x(-1)

            def tile(x, t, j, last, _):
                t2 = pe.snap(t * 2)
                chunk0 = pe.snap(x * CH) if not isinstance(x, int) else x * CH
                pe.wait_ge(xlo_done, pe.snap(t + 1))
                pe.wait_ge(hid_done, t2)
                for half in range(2):
                    out = ps_g[half][:, :]
                    for k in range(KD):
                        c = 4 * half + k // 2
                        if k % 2 == 0:
                            pe.wait_ge(lo_done, chunk0 + (c + 1))
                        at = slice(512 * (k % 2), 512 * (k % 2) + 512)
                        pe.matmul(out, x_hi[:, k, :], w_hi[:, c, at], start=(k == 0), stop=False)
                        pe.matmul(out, x_hi[:, k, :], w_lo[:, c, at], start=False, stop=False)
                        ins = pe.matmul(out, x_lo[:, k, :], w_hi[:, c, at], start=False, stop=(k == KD - 1))
                        if k % 2:
                            ins.then_inc(used, 1)

                def turn_h(n):
                    pe.wait_ge(hid_done, pe.snap(t2 + (n + 1)))
                    pe.wait_ge(hlo_done, t2)
                    for f in range(2):
                        ins = pe.transpose(ps_h[n][:, f, :], hid[:, (2 * n + f) * P:(2 * n + f + 1) * P], ident)
                    ins.then_inc(ht_done, 1)

                turn_h(0)
                turn_x(t)
                turn_h(1)
                pe.wait_ge(y0_done, t)
                pe.wait_ge(y1_done, t)
                for f in range(KF):
                    if f % 2 == 0:
                        pe.wait_ge(hlo_done, pe.snap(t2 + (f // 2 + 1)))
                    pe.wait_ge(lo_done, chunk0 + (9 + f))
                    for m in range(2):
                        at = slice(512 * m, 512 * m + 512)
                        pe.matmul(ps_y[m][:, :], h_hi[:, f, :], w_hi[:, 8 + f, at], start=(f == 0), stop=False)
                        pe.matmul(ps_y[m][:, :], h_hi[:, f, :], w_lo[:, 8 + f, at], start=False, stop=False)
                        ins = pe.matmul(ps_y[m][:, :], h_lo[:, f, :], w_hi[:, 8 + f, at], start=False,
                                        stop=(f == KF - 1))
                    ins.then_inc(used, 1)

            experts(pe, tile)


def phase_combine(nc, s):
    with ExitStack() as ctx:
        sb, ps, sem = allocate(nc, ctx, "combine")
        B = 3
        y = sb("y", [P, B, 2, D])
        x = sb("x", [P, B, D])
        part = sb("part", [P, B, D])
        gate = sb("gate", [P, 2, D])
        gain = sb("gain", [P, D])
        squares = sb("squares", [P, D])
        mean_sq = sb("mean_sq", [P, NT])
        rstd = sb("rstd", [P, NT])
        rows_in, x_in, y_in = sem("rows_in"), [sem(f"x_in{n}") for n in range(B)], [sem(f"y_in{n}") for n in range(B)]
        first_done, summed, gated, added, ms_done, root_done, rstd_done, out_done = (
            sem(n) for n in ("first_done", "summed", "gated", "added", "ms_done", "root_done", "rstd_done",
                             "out_done"))
        stored = [sem(f"stored{n}") for n in range(B)]
        block = ctx.enter_context(nc.Block())

        @block.sync
        def _(sp):
            for i in range(NT):
                w = width(i)
                if i >= B:
                    sp.wait_ge(stored[i % B], 16 * (i // B))
                sp.dma_start(x[0:w, i % B, :], s.x_scr[i * P:i * P + w, :]).then_inc(x_in[i % B], 16)
                if i == 0:
                    for q, rows in ((0, P), (1, DEC)):
                        sp.dma_start(gate[0:rows, q], s.mod_scr[q:q + 1, 3 * D:4 * D].broadcast_to([rows, D]))\
                          .then_inc(rows_in, 16)
                    sp.dma_start(gain[:, :], s.args["final_norm_g"].unsqueeze(0).broadcast_to([P, D]))\
                      .then_inc(rows_in, 16)

        @block.gpsimd
        def _(pool):
            for i in range(NT):
                w = width(i)
                if i >= B:
                    pool.wait_ge(summed, i - B + 1)
                for c in range(2):
                    pool.indirect_dma_start(out=y[0:w, i % B, c, :], out_offset=None, in_=s.y_scr[0:SLOTS, :],
                                            in_offset=bass.IndirectOffsetOnAxis(ap=s.slot[0:w, c, i:i + 1], axis=0))\
                        .then_inc(y_in[i % B], 16)

        def store(act, i):
            w, b = width(i), i % B
            act.wait_ge(out_done, i + 1)
            dst = s.outs["y_prompt"][0, i * P:i * P + w, :] if i < NP_T else s.outs["y_sample"][0]
            act.dma_start(dst, x[0:w, b]).then_inc(stored[b], 16)

        @block.scalar
        def _(act):
            for i in range(NT):
                w, b = width(i), i % B
                act.wait_ge(y_in[b], 32 * (i // B + 1))
                if i >= B:
                    act.wait_ge(added, i - B + 1)
                act.activation(part[0:w, b], y[0:w, b, 0], ACT.Copy, scale=s.weight[0:w, 0, i:i + 1])\
                   .then_inc(first_done, 1)
                act.wait_ge(added, i + 1)
                if i:
                    act.wait_ge(ms_done, i)
                act.activation(squares[0:w, :], x[0:w, b], ACT.Square, scale=1.0 / 32.0,
                               accum_out=mean_sq[0:w, i:i + 1]).then_inc(ms_done, 1)
                act.wait_ge(ms_done, i + 1)
                act.activation(rstd[0:w, i:i + 1], mean_sq[0:w, i:i + 1], ACT.Sqrt, bias=s.eps[0:w, :])\
                   .then_inc(root_done, 1)
                if i:
                    store(act, i - 1)
            store(act, NT - 1)
            for b in range(B):
                act.wait_ge(stored[b], 16 * len(range(b, NT, B)))

        @block.vector
        def _(dve):
            def normalise(i):
                w, b = width(i), i % B
                dve.wait_ge(root_done, i + 1)
                dve.reciprocal(rstd[0:w, i:i + 1], rstd[0:w, i:i + 1]).then_inc(rstd_done, 1)
                dve.wait_ge(rstd_done, i + 1)
                dve.scalar_tensor_tensor(out=x[0:w, b], in0=x[0:w, b], scalar=rstd[0:w, i:i + 1], in1=gain[0:w],
                                         op0=ALU.mult, op1=ALU.mult).then_inc(out_done, 1)

            dve.wait_ge(rows_in, 48)
            for i in range(NT):
                w, b, q = width(i), i % B, i // NP_T
                dve.wait_ge(first_done, i + 1)
                dve.scalar_tensor_tensor(out=part[0:w, b], in0=y[0:w, b, 1], scalar=s.weight[0:w, 1, i:i + 1],
                                         in1=part[0:w, b], op0=ALU.mult, op1=ALU.add).then_inc(summed, 1)
                dve.wait_ge(summed, i + 1)
                dve.tensor_tensor(part[0:w, b], part[0:w, b], gate[0:w, q], ALU.mult).then_inc(gated, 1)
                dve.wait_ge(gated, i + 1)
                dve.wait_ge(x_in[b], 16 * (i // B + 1))
                dve.tensor_tensor(x[0:w, b], x[0:w, b], part[0:w, b], ALU.add).then_inc(added, 1)
                if i:
                    normalise(i - 1)
            normalise(NT - 1)


def build(nc, args, outs):
    s = Shared()
    s.args, s.outs = args, outs
    with ExitStack() as ctx:
        sb, ps, sem = allocate(nc, ctx, "all")
        s.consts = sb("consts_sb", [P, N_CONST])
        s.eps = sb("eps", [P, 1])
        s.o_scr = nc.dram_tensor("o_scratch", [D, NTOK], F32).ap()
        s.mod_scr = nc.dram_tensor("mod_scratch", [2, 4 * D], F32).ap()
        s.xs_scr = nc.dram_tensor("xs_scratch", [ROWS, D], F32).ap()
        s.y_scr = nc.dram_tensor("y_scratch", [ROWS, D], F32).ap()
        s.x_scr = nc.dram_tensor("x_scratch", [NTOK, D], F32).ap()
        s.slot = sb("slot", [P, 2, NT], I32)
        s.weight = sb("weight", [P, 2, NT])
        s.plan = sb("plan", [1, 96], I32)
        with ExitStack() as ctx2:
            sb2, _, _ = allocate(nc, ctx2, "early")
            s.cT = sb2("cT", [P, KD, 2])
            s.cols = sb2("cols", [P, 40])
            s.bound = sb2("bound", [P, 2, HEADS])
            s.h_hi = sb2("h_hi", [P, KD, NTOK], F32R)
            s.h_lo = sb2("h_lo", [P, KD, NTOK], F32R)
            phase_condition(nc, s)
            phase_mixers(nc, s)
        phase_output(nc, s)
        phase_experts(nc, s)
        phase_combine(nc, s)


_INS = ["x_prompt", "x_sample", "c_prompt", "c_sample", "state_ret", "state_hgrn", "W_ada", "b_ada", "norm1_g",
        "norm2_g", "W_in", "ret_norm_g", "hgrn_norm_g", "hgrn_lb_logits", "W_out", "W_router_group",
        "b_router_group", "W_router_expert", "b_router_expert", "W_gate_e", "W_up_e", "W_down_e", "final_norm_g"]
_STATE = (1, 1, HEADS, P, P)
_OUTS = dict(y_prompt=(1, SEQ, D), y_sample=(1, DEC, D), state_ret_prompt=_STATE, state_hgrn_prompt=_STATE,
             state_ret_sample=_STATE, state_hgrn_sample=_STATE)


def kernel(**inputs):
    import concourse.bacc as _bacc
    from concourse.bass_utils import run_bass_kernel_spmd as _run

    nc = _bacc.Bacc("TRN2", target_bir_lowering=False, num_devices=1)
    arrays, args, outs = {}, {}, {}
    for name in [*_INS, "consts"]:
        a = np.ascontiguousarray(constants() if name == "consts" else inputs[name])
        arrays[f"in_{name}_dram"] = a
        args[name] = nc.dram_tensor(f"in_{name}_dram", a.shape, mybir.dt.from_np(a.dtype), kind="ExternalInput").ap()
    for name, shape in _OUTS.items():
        outs[name] = nc.dram_tensor(f"out_{name}_dram", shape, F32, kind="ExternalOutput").ap()
    build(nc, args, outs)
    r = _run(nc, [arrays], core_ids=[0])
    return tuple(r.results[0][f"out_{name}_dram"] for name in _OUTS)
```

```python
from contextlib import ExitStack

import numpy as np

import concourse.bass as bass
from concourse import mybir

F32 = mybir.dt.float32
F32R = mybir.dt.float32r
I32 = mybir.dt.int32
ALU = mybir.AluOpType
ACT = mybir.ActivationFunctionType
AX = mybir.AxisListType.X

P = 128
D = 1024
KD = D // P
SEQ = 1024
DEC = 32
PAST = 1024
NTOK = SEQ + DEC
NP_T = SEQ // P
NT = NP_T + 1
HEADS = 4
D_IN = 4096
EPS = 1e-6
N_GROUPS = 4
PER_GROUP = 4
NE = N_GROUPS * PER_GROUP
F = 512
KF = F // P
CHUNKS = 12
RAW = 6
W_OUT_AT = (4, 5, 0, 1, 2, 3, 4, 5)
UNIT_AT = (2560, 2048, 1536, 3584, 0, 512, 1024, 3072)
SLOTS = 2 * NTOK
ROWS = SLOTS + NT * P
PIECE = NTOK // 3
SCALE = float(np.float32(128.0) ** np.float32(-0.5))
LEVELS = (64, 32, 16, 8, 4, 2, 1)
SMALL = 5
PRIMED = 4

CONSTS = dict(ident=P, ones=P, tri=P, cos=NT * 64, sin=NT * 64, ret_decay=HEADS * P, q_decay=HEADS * P,
              level_mask=(SMALL + 1) * 32, k_decay=2 * HEADS, s_decay=2 * HEADS, iota=NE, limits=8,
              place=NE, token=NT)
AT = dict(zip(CONSTS, np.cumsum([0, *CONSTS.values()])[:-1].tolist()))
N_CONST = sum(CONSTS.values())


def width(i):
    return P if i < NP_T else DEC


def constants():
    f = np.float32
    c = {}
    c["ident"] = np.eye(P)
    c["ones"] = np.ones((P, P))
    c["tri"] = np.triu(np.ones((P, P)), 1)
    inv = (f(1.0) / (f(10000.0) ** (np.arange(64, dtype=f) / f(64)))).astype(f)
    pos = np.concatenate([np.arange(SEQ), PAST + np.arange(P)]).astype(f)
    ang = (pos[:, None] * inv[None, :]).astype(f).reshape(NT, P, 64).transpose(1, 0, 2)
    c["cos"], c["sin"] = np.cos(ang).reshape(P, -1), np.sin(ang).reshape(P, -1)
    lg = np.log(1.0 - np.exp2(-5.0 - np.arange(HEADS)))
    j = np.arange(P)
    diff = j[None, :] - j[:, None]
    decay = np.where(diff[:, None] >= 0, np.exp(np.maximum(diff, 0)[:, None] * lg[None, :, None]), 0.0)
    c["ret_decay"] = decay * SCALE
    c["q_decay"] = np.broadcast_to(np.exp((j[None, None] + 1.0) * lg[None, :, None]), (P, HEADS, P))
    full, short = np.exp((P - 1.0 - j)[:, None] * lg), np.exp(np.maximum(DEC - 1.0 - j, 0)[:, None] * lg)
    c["k_decay"] = np.stack([full, short], -1) * SCALE
    c["s_decay"] = np.broadcast_to(np.stack([np.exp(P * lg), np.exp(DEC * lg)], -1), (P, HEADS, 2))
    m, l = np.arange(P)[:, None] % 32, np.arange(32)[None, :]
    masks = [(m // (2 * h) == l // (2 * h)) & (m % (2 * h) < h) & (l % (2 * h) >= h) for h in LEVELS[2:]]
    c["level_mask"] = np.stack([*masks, m == l], 1)
    c["iota"] = np.broadcast_to(np.arange(NE), (P, NE))
    c["place"] = np.broadcast_to(np.arange(NE) * NT, (P, NE))
    c["token"] = np.arange(NT)[None, :] * P + np.arange(P)[:, None]
    c["limits"] = np.broadcast_to(P * (1.0 + np.arange(8)), (P, 8))
    return np.concatenate([np.asarray(c[k], f).reshape(P, -1) for k in CONSTS], 1)


class Shared:

    def const(self, name, a=0, b=None):
        b = CONSTS[name] if b is None else b
        return self.consts[:, AT[name] + a:AT[name] + b]


def allocate(nc, ctx, phase):
    def sb(name, shape, dt=F32):
        return ctx.enter_context(nc.sbuf_tensor(f"{phase}_{name}", shape, dt))

    def ps(name, shape):
        return ctx.enter_context(nc.psum_tensor(f"{phase}_{name}", shape, F32))

    def sem(name):
        return ctx.enter_context(nc.semaphore(f"{phase}_{name}"))

    return sb, ps, sem


def carry(e, idle):
    e.sem_inc(idle, 1)


def f32(ap):
    return ap.bitcast(F32)


def phase_condition(nc, s):
    with ExitStack() as ctx:
        sb, ps, sem = allocate(nc, ctx, "condition")
        rows = sb("rows", [56, P])
        w_ada = sb("w_ada_in", [P, 2, KD, 512])
        xt = sb("xt", [P, 3, D])
        h32 = sb("h32", [P, KD, NTOK])
        mod_row = sb("mod_row", [2, 4, 512])
        mod_col = sb("mod_col", [P, 16, 2])
        gain = sb("gain", [P, KD, 2])
        squares = sb("squares", [P, D])
        mean_sq = sb("mean_sq", [P, NT])
        rstd = sb("rstd", [P, NT])
        lbx = sb("lbx", [P, 3, HEADS])
        ps_col = ps("ps_col", [P, 512])
        ps_ada = [ps(f"ps_ada{n}", [P, 512]) for n in range(2)]
        ps_x = [ps(f"ps_x{n}", [P, 4, P]) for n in range(4)]
        ps_mod = ps("ps_mod", [P, 512])
        const_in, rows_in = sem("const_in"), sem("rows_in")
        x_in = [sem(f"x_in{n}") for n in range(3)]
        w_in = [sem(f"w_in{n}") for n in range(2)]
        c_silu, cols_t, cols_done, ct_done = sem("c_silu"), sem("cols_t"), sem("cols_done"), sem("ct_done")
        ms_done, rstd_done, xn_done, xt_done = sem("ms_done"), sem("rstd_done"), sem("xn_done"), sem("xt_done")
        xlow, xhigh = sem("xlow_copied"), sem("xhigh_copied")
        ada_done, ada_copied, mod_t, mod_added, gain_done = (sem("ada_done"), sem("ada_copied"), sem("mod_t"),
                                                             sem("mod_added"), sem("gain_done"))
        h_done, hi_done, lb_exp, lb_step = sem("h_done"), sem("hi_done"), sem("lb_exp"), sem("lb_step")
        root_done, eps_set, fetched = sem("root_done"), sem("eps_set"), sem("fetched")
        block = ctx.enter_context(nc.Block())
        ident = s.const("ident")
        a = s.args

        @block.sync
        def _(sp):
            sp.dma_start(s.consts[:, :], a["consts"]).then_inc(const_in, 16)
            split = [(0, 8, a["c_prompt"][0]), (8, 16, a["c_sample"][0]), (16, 32, a["b_ada"][0, 0:2 * D]),
                     (32, 40, a["norm1_g"][0]), (40, 44, a["hgrn_lb_logits"][0]),
                     (44, 48, a["hgrn_lb_logits"][1]), (48, 52, a["ret_norm_g"][0]),
                     (52, 56, a["hgrn_norm_g"][0])]
            for lo, hi, src in split:
                sp.dma_start(rows[lo:hi, :], src.rearrange("(k p) -> k p", p=P)).then_inc(rows_in, 16)
            w_view = a["W_ada"][0].rearrange("(k p) n -> p k n", p=P)
            for i in range(NT):
                if i >= 3:
                    sp.wait_ge(xt_done, i - 2)
                src = a["x_prompt"][0, i * P:(i + 1) * P, :] if i < NP_T else a["x_sample"][0]
                sp.dma_start(xt[0:width(i), i % 3, :], src).then_inc(x_in[i % 3], 16)
                if i % 2 == 0 and i < 8:
                    b = i // 2
                    if b >= 2:
                        sp.wait_ge(ada_done, b - 1)
                    sp.dma_start(w_ada[:, b % 2], w_view[:, :, b * 512:(b + 1) * 512]).then_inc(w_in[b % 2], 16)
            for u in range(4):
                sp.dma_start(s.raw[:, u].rearrange("p (k n) -> p k n", k=KD), a["W_in"][0]
                             .rearrange("(k p) n -> p k n", p=P)[:, :, UNIT_AT[u]:UNIT_AT[u] + P]).then_inc(fetched, 16)
            sp.wait_ge(fetched, 64)

        def copy_low(act, i):
            w = width(i)
            act.wait_ge(xt_done, i + 1)
            act.activation(h32[:, 0:4, i * P:i * P + w], ps_x[2 * (i % 2)][:, :, 0:w], ACT.Copy).then_inc(xlow, 1)

        @block.scalar
        def _(act):
            act.wait_ge(eps_set, 1)
            act.wait_ge(rows_in, 128)
            act.activation(rows[0:16, :], rows[0:16, :], ACT.Silu).then_inc(c_silu, 1)
            for i in range(NT):
                w = width(i)
                act.wait_ge(x_in[i % 3], 16 * (i // 3 + 1))
                if i:
                    act.wait_ge(ms_done, i)
                act.activation(squares[0:w, :], xt[0:w, i % 3, :], ACT.Square, scale=1.0 / 32.0,
                               accum_out=mean_sq[0:w, i:i + 1]).then_inc(ms_done, 1)
                act.wait_ge(ms_done, i + 1)
                act.activation(rstd[0:w, i:i + 1], mean_sq[0:w, i:i + 1], ACT.Sqrt, bias=s.eps[0:w, :])\
                   .then_inc(root_done, 1)
                if i:
                    copy_low(act, i - 1)
            copy_low(act, NT - 1)
            act.wait_ge(lb_step, 2)
            act.activation(lbx[:, 0:2, :], lbx[:, 0:2, :], ACT.Exp).then_inc(lb_exp, 1)
            for k in range(KD):
                act.wait_ge(h_done, k + 1)
                act.activation(s.h_hi[:, k, :], h32[:, k, :], ACT.Copy).then_inc(hi_done, 1)

        @block.tensor
        def _(pe):
            pe.wait_ge(const_in, 16)
            pe.wait_ge(c_silu, 1)
            pe.transpose(ps_col[:, 0:56], rows[:, :], ident[0:56, 0:56]).then_inc(cols_t, 1)
            pe.wait_ge(ct_done, 1)
            for i in range(NT):
                w = width(i)
                pe.wait_ge(xn_done, i + 1)
                if i >= 2:
                    pe.wait_ge(xlow, i - 1)
                    pe.wait_ge(xhigh, i - 1)
                for k in range(KD):
                    last = pe.transpose(ps_x[2 * (i % 2) + k // 4][:, k % 4, 0:w],
                                        xt[0:w, i % 3, k * P:(k + 1) * P], ident[0:w, 0:w])
                last.then_inc(xt_done, 1)
                if i % 2 == 1:
                    b = i // 2
                    pe.wait_ge(w_in[b % 2], 16 * (b // 2 + 1))
                    if b >= 2:
                        pe.wait_ge(ada_copied, b - 1)
                    for k in range(KD):
                        last = pe.matmul(ps_ada[b % 2][0:2, :], s.cT[:, k, :], w_ada[:, b % 2, k, :],
                                         start=(k == 0), stop=(k == KD - 1))
                    last.then_inc(ada_done, 1)
            pe.wait_ge(ada_copied, 4)
            for j in range(16):
                last = pe.transpose(ps_mod[:, 2 * j:2 * j + 2], mod_row[:, j // 4, (j % 4) * P:(j % 4 + 1) * P],
                                    ident[0:2, 0:2])
            last.then_inc(mod_t, 1)

        @block.vector
        def _(dve):
            dve.memset(s.eps[:, :], EPS).then_inc(eps_set, 1)
            dve.wait_ge(cols_t, 1)
            dve.tensor_copy(s.cT[:, :, :], ps_col[:, 0:16].rearrange("p (s k) -> p k s", s=2)).then_inc(ct_done, 1)
            dve.tensor_copy(s.cols[:, :], ps_col[:, 16:56]).then_inc(cols_done, 1)

            def turn(i):
                w = width(i)
                dve.wait_ge(root_done, i + 1)
                dve.reciprocal(rstd[0:w, i:i + 1], rstd[0:w, i:i + 1]).then_inc(rstd_done, 1)
                dve.wait_ge(rstd_done, i + 1)
                dve.tensor_scalar(xt[0:w, i % 3, :], xt[0:w, i % 3, :], rstd[0:w, i:i + 1], None,
                                  ALU.mult).then_inc(xn_done, 1)

            def copy_high(i):
                w = width(i)
                dve.wait_ge(xt_done, i + 1)
                dve.tensor_copy(h32[:, 4:8, i * P:i * P + w], ps_x[2 * (i % 2) + 1][:, :, 0:w]).then_inc(xhigh, 1)

            for i in range(NT):
                turn(i)
                if i:
                    copy_high(i - 1)
                if i % 2 == 0 and i >= 2:
                    b = i // 2 - 1
                    dve.wait_ge(ada_done, b + 1)
                    dve.tensor_copy(mod_row[:, b, :], ps_ada[b % 2][0:2, :]).then_inc(ada_copied, 1)
            copy_high(NT - 1)
            dve.wait_ge(cols_done, 1)
            logits = s.cols[:, 24:32].rearrange("p (l h) -> p l h", l=2)
            dve.tensor_tensor(lbx[:, 2, :], logits[:, 0, :], logits[:, 1, :], ALU.max).then_inc(lb_step, 1)
            dve.wait_ge(lb_step, 1)
            dve.tensor_tensor(lbx[:, 0:2, :], logits, lbx[:, 2:3, :].broadcast_to([P, 2, HEADS]),
                              ALU.subtract).then_inc(lb_step, 1)
            dve.wait_ge(lb_exp, 1)
            dve.tensor_tensor(lbx[:, 2, :], lbx[:, 0, :], lbx[:, 1, :], ALU.add).then_inc(lb_step, 1)
            dve.wait_ge(lb_step, 3)
            dve.reciprocal(lbx[:, 2, :], lbx[:, 2, :]).then_inc(lb_step, 1)
            dve.wait_ge(lb_step, 4)
            dve.tensor_tensor(s.bound[:, 0, :], lbx[:, 0, :], lbx[:, 2, :], ALU.mult).then_inc(lb_step, 1)
            dve.wait_ge(lb_step, 5)
            dve.tensor_scalar(s.bound[:, 1, :], s.bound[:, 0, :], -1.0, 1.0, ALU.mult, ALU.add)
            dve.wait_ge(mod_t, 1)
            dve.tensor_tensor(mod_col[:, :, :], ps_mod[:, 0:32].rearrange("p (j s) -> p j s", s=2),
                              s.cols[:, 0:16].unsqueeze(2).broadcast_to([P, 16, 2]), ALU.add).then_inc(mod_added, 1)
            dve.wait_ge(mod_added, 1)
            dve.scalar_tensor_tensor(out=gain[:, :, :], in0=mod_col[:, 8:16, :], scalar=1.0,
                                     in1=s.cols[:, 16:24].unsqueeze(2).broadcast_to([P, KD, 2]),
                                     op0=ALU.add, op1=ALU.mult).then_inc(gain_done, 1)
            dve.wait_ge(gain_done, 1)
            dve.wait_ge(xlow, NT)
            dve.wait_ge(xhigh, NT)
            for k in range(KD):
                dve.tensor_scalar(h32[:, k, 0:SEQ], h32[:, k, 0:SEQ], gain[:, k, 0:1], mod_col[:, k, 0:1],
                                  ALU.mult, ALU.add)
                dve.tensor_scalar(h32[:, k, SEQ:NTOK], h32[:, k, SEQ:NTOK], gain[:, k, 1:2],
                                  mod_col[:, k, 1:2], ALU.mult, ALU.add).then_inc(h_done, 1)
                if k % 2:
                    dve.wait_ge(hi_done, k)
                    dve.tensor_tensor(s.h_lo[:, k - 1, :], h32[:, k - 1, :], f32(s.h_hi[:, k - 1, :]), ALU.subtract)

        @block.gpsimd
        def _(pool):
            for k in range(1, KD, 2):
                pool.wait_ge(hi_done, k + 1)
                pool.tensor_tensor(s.h_lo[:, k, :], h32[:, k, :], f32(s.h_hi[:, k, :]), ALU.subtract)


def phase_mixers(nc, s):
    R = HEADS
    with ExitStack() as ctx:
        sb, ps, sem = allocate(nc, ctx, "mixers")
        raw = s.raw.rearrange("p u (k n) -> p u k n", k=KD)
        w_hi = sb("w_hi", [P, KD, 4, P], F32R)
        w_lo = sb("w_lo", [P, KD, 4, P], F32R)
        log_f = sb("log_f", [P, NTOK])
        hk = sb("hk", [P, NTOK])
        hq = sb("hq", [P, NTOK])
        gate = sb("gate", [P, 2, NTOK])
        ones = s.const("ones")
        decay = sb("decay", [P, 9, P])
        q_lv = sb("q_lv", [P, 7, P])
        k_lv = sb("k_lv", [P, 8, P])
        q_in = sb("q_in", [P, 2, P])
        last_f = sb("last_f", [P, 2])
        qk_cos = sb("qk_cos", [P, 4, 64])
        qk_sin = sb("qk_sin", [P, 4, 64])
        rot = sb("rot", [P, 2, 2, 64])
        k_dec = sb("k_dec", [P, 2, P])
        kd_col = sb("kd_col", [P, 2])
        qkv = sb("qkv", [P, 2, 512])
        turned = sb("turned", [P, 3, P])
        q_t, k_t, hk_dec = (turned[:, c, :] for c in range(3))
        qd_t = sb("qd_t", [P, P])
        a_ret = sb("a_ret", [P, P])
        a_hg = sb("a_hg", [P, 2, P])
        masked = sb("masked", [P, SMALL + 1, 32])
        squares = sb("squares", [P, 2, P])
        mean_sq = sb("mean_sq", [P, 2, 2])
        norm = sb("norm", [P, 2, 4, 2])
        normed = sb("normed", [P, 2, P])
        o_out = sb("o_out", [P, 2, 2, P])
        s_pr = sb("s_prompt", [P, 2, P])
        s_sa = sb("s_sample", [P, 2, P])
        ada_bias = sb("ada_bias", [2, D])
        ada_row = sb("ada_row", [2, D])
        ps_p = [ps(f"ps_proj{n}", [P, 512]) for n in range(2)]
        ps_tr = ps("ps_tr", [P, 4, P])
        ps_a = ps("ps_a", [P, 512])
        ps_lv = ps("ps_lv", [P, 512])
        ps_o = ps("ps_o", [P, 4, P])
        ps_s = ps("ps_s", [P, 4, P])
        ps_ot = ps("ps_ot", [P, 4, P])
        wide = ps_lv[:, 256:384]
        lv = ps_lv[:, 0:(SMALL + 1) * 32].rearrange("p (s l) -> p s l", l=32)

        raw_in = [sem(f"raw_in{n}") for n in range(4)]
        hi_done, lo_done, t_done, t_read = sem("hi_done"), sem("lo_done"), sem("t_done"), sem("t_read")
        proj_done, ada_done, ada_read = sem("proj_done"), sem("ada_done"), sem("ada_read")
        bias_in, ada_out = sem("bias_in"), sem("ada_out")
        f_done, logf_done, hk_done = sem("f_done"), sem("logf_done"), sem("hk_done")
        roped, rot_done, v_done, kdec_done = sem("roped"), sem("rot_done"), sem("v_done"), sem("kdec_done")
        tr_done, qkt_done, qd_done = sem("tr_done"), sem("qkt_done"), sem("qd_done")
        cum_done, diff_done, abs_done, exp_done = sem("cum_done"), sem("diff_done"), sem("abs_done"), sem("exp_done")
        ql_done, kl_done = sem("ql_done"), sem("kl_done")
        lv_done, ra_done, masked_done, ah_done, ahc_done, ar_done = (
            sem("lv_done"), sem("ra_done"), sem("masked_done"), sem("ah_done"), sem("ahc_done"), sem("ar_done"))
        o_done, s_done, ms_done, seed_log, seed_done, norm_step, normed_done = (
            sem("o_done"), sem("s_done"), sem("ms_done"), sem("seed_log"), sem("seed_done"), sem("norm_step"),
            sem("normed_done"))
        kd_copied, ot_done, out_done = sem("kd_copied"), sem("ot_done"), sem("out_done")
        o_stored = [sem(f"o_stored{n}") for n in range(2)]
        sp_stored, ss_stored, ss_in = sem("sp_stored"), sem("ss_stored"), sem("ss_in")
        cleared, idle, fetched = sem("cleared"), sem("idle"), sem("fetched")
        primed = [*raw_in, hi_done, lo_done, t_done, t_read, proj_done, ada_done, ada_read, bias_in, ada_out,
                  f_done, logf_done, hk_done, roped, rot_done, v_done, kdec_done, tr_done, qkt_done, qd_done,
                  cum_done, diff_done, abs_done, exp_done, ql_done, kl_done, lv_done, ra_done, masked_done,
                  ah_done, ahc_done, ar_done, o_done, s_done, ms_done, seed_log, seed_done, norm_step,
                  normed_done, kd_copied, ot_done, out_done, *o_stored, sp_stored, ss_stored, ss_in]
        block = ctx.enter_context(nc.Block())
        a = s.args
        ident = s.const("ident")
        pieces = [slice(n * PIECE, (n + 1) * PIECE) for n in range(3)]

        def counts(e, g):
            n = {m: e.snap(g * m + PRIMED) for m in (1, 2, 8, 9, 12, 16, 32, 36, 64, 80)}
            n["round"] = e.snap(g * 1)
            return n

        @block.sync
        def _(sp):
            w_in = a["W_in"][0].rearrange("(k p) n -> p k n", p=P)
            w_ada = a["W_ada"][0].rearrange("(k p) n -> p k n", p=P)
            def load(g, u):
                if u < 8:
                    at = nc.s_assert_within(sp.snap(g * P + UNIT_AT[u]), 0, D_IN - P,
                                            skip_runtime_bounds_check_because="a round is at most the last")
                    src = w_in[:, :, bass.ds(at, P)]
                else:
                    at = sp.snap(g * D + (2 * D + (u - 8) * P))
                    src = w_ada[:, :, bass.ds(at, P)]
                if u < 4:
                    sp.wait_ge(ada_done, sp.snap(g * 8 + (u - 3 + PRIMED)))
                elif u < 12:
                    sp.wait_ge(lo_done, sp.snap(g * 8 + (u - 3 + PRIMED)))
                else:
                    sp.wait_ge(ada_done, sp.snap(g * 8 + (u - 11 + PRIMED)))
                carry(sp, idle)
                sp.dma_start(raw[:, u % 4], src).then_inc(raw_in[u % 4], 16)
                if u == 8:
                    head = sp.snap(g * 1)
                    sp.wait_ge(ss_stored, sp.snap(g * 32 + PRIMED))
                    carry(sp, idle)
                    for n, name in enumerate(("state_ret", "state_hgrn")):
                        sp.dma_start(s_sa[:, n:n + 1, :],
                                     a[name][0, 0, bass.ds(head, 1)].rearrange("h k v -> k h v"))\
                          .then_inc(ss_in, 16)
                    at = sp.snap(g * D + 2 * D)
                    sp.wait_ge(ada_read, sp.snap(g * 1 + PRIMED))
                    carry(sp, idle)
                    sp.dma_start(ada_bias[:, :], a["b_ada"][0:1, bass.ds(at, D)].broadcast_to([2, D]))\
                      .then_inc(bias_in, 16)

            for u in range(4):
                sp.sem_inc(raw_in[u], 16)
            with sp.Fori(0, R) as g:
                for u in range(4, 16):
                    load(g, u)
                with sp.If(g < R - 1):
                    for u in range(4):
                        load(g + 1, u)
            for k in range(6):
                if k == 2:
                    sp.wait_ge(ada_done, 8 * R + PRIMED)
                sp.dma_start(s.raw[:, W_OUT_AT[k]], a["W_out"][0, k * P:(k + 1) * P, :]).then_inc(fetched, 16)
            sp.wait_ge(fetched, 16 * 6)

        @block.gpsimd
        def _(pool):
            for semaphore in primed:
                pool.sem_inc(semaphore, PRIMED)
            pool.memset(a_hg[:, :, :], 0.0).then_inc(cleared, 1)
            with pool.Fori(0, R) as g:
                n = counts(pool, g)

                def keys(i):
                    w = width(i)
                    pool.wait_ge(exp_done, n[9] + (i + 1))
                    pool.wait_ge(lv_done, n[9] + i)
                    if i == 0:
                        pool.wait_ge(hk_done, n[1] + 1)
                    kb = hk[:, i * P:i * P + w]
                    for c, (lo, hi) in enumerate([(0, 8)] if w == P else [(0, 1), (3, 8)]):
                        last = pool.tensor_tensor(k_lv[:, lo:hi, 0:w], decay[:, lo:hi, 0:w],
                                                  kb.unsqueeze(1).broadcast_to([P, hi - lo, w]), ALU.mult)
                    last.then_inc(kl_done, 1)

                def refine(i):
                    w = width(i)
                    b = i % 2
                    step = lambda m: n[36] + (4 * i + m)
                    m, y = mean_sq[0:w, b, :], norm[0:w, b, 0, :]
                    t = [norm[0:w, b, c, :] for c in range(4)]
                    pool.wait_ge(seed_done, n[9] + (i + 1))
                    pool.tensor_tensor(t[1], y, y, ALU.mult).then_inc(norm_step, 1)
                    pool.wait_ge(norm_step, step(1))
                    pool.tensor_tensor(t[2], t[1], m, ALU.mult).then_inc(norm_step, 1)
                    pool.wait_ge(norm_step, step(2))
                    carry(pool, idle)
                    pool.tensor_scalar(t[1], t[2], -0.5, 1.5, ALU.mult, ALU.add).then_inc(norm_step, 1)
                    pool.wait_ge(norm_step, step(3))
                    pool.tensor_tensor(t[3], y, t[1], ALU.mult).then_inc(norm_step, 1)

                for i in range(NT + 2):
                    if i >= 2:
                        refine(i - 2)
                    if i < NT:
                        keys(i)

        @block.scalar
        def _(act):
            def split(u, raws, before):
                act.wait_ge(raw_in[u % 4], raws + 16 * (u // 4 + 1))
                if before is not None:
                    act.wait_ge(*before)
                act.activation(w_hi[:, :, u % 4, :], raw[:, u % 4], ACT.Copy).then_inc(hi_done, 1)

            for u in range(4):
                split(u, PRIMED, None)
            with act.Fori(0, R) as g:
                n = counts(act, g)

                def split_here(u):
                    split(u, n[64], (t_done, n[12] + 3 * (u - 3)))

                def split_next(units):
                    with act.If(g < R - 1):
                        for u in units:
                            split(u, n[64] + 64, (proj_done, n[9] + 9))


                def read_block(j):
                    for c in range(3):
                        at, src = pieces[c], ps_p[(3 * j + c) % 2][:, 0:PIECE]
                        act.wait_ge(t_done, n[12] + (3 * j + c + 1))
                        if j == 0:
                            if c == 0:
                                act.wait_ge(out_done, n[9])
                            act.activation(log_f[:, at], src, ACT.Sigmoid)
                            last = act.activation(hk[:, at], src, ACT.Sigmoid, scale=-1.0)
                        elif j == 1:
                            last = act.activation(hq[:, at], src, ACT.Copy, scale=SCALE)
                        else:
                            last = act.activation(gate[:, j - 2, at], src, ACT.Silu)
                        last.then_inc(t_read, 1)

                read_block(0)
                split_here(4)
                read_block(1)
                act.wait_ge(f_done, n[1] + 1)
                act.activation(log_f[:, :], log_f[:, :], ACT.Ln).then_inc(logf_done, 1)
                split_here(5)
                read_block(2)
                split_here(6)
                read_block(3)
                split_here(7)
                act.preload_act_table_set("natural_log_exp_and_others")

                def squares_of(i):
                    w, b = width(i), i % 2
                    act.wait_ge(o_done, n[9] + (i + 1))
                    for c in range(2):
                        last = act.activation(squares[0:w, c, :], ps_o[0:w, c, :], ACT.Square,
                                              scale=float(P) ** -0.5, accum_out=mean_sq[0:w, b, c:c + 1])
                    last.then_inc(ms_done, 1)
                    act.wait_ge(ms_done, n[9] + (i + 1))
                    act.activation(norm[0:w, b, 1, :], mean_sq[0:w, b, :], ACT.Ln, bias=s.eps[0:w, :])\
                       .then_inc(seed_log, 1)
                    act.wait_ge(seed_log, n[9] + (i + 1))
                    act.activation(norm[0:w, b, 0, :], norm[0:w, b, 1, :], ACT.Exp, scale=-0.5)
                    act.activation(mean_sq[0:w, b, :], mean_sq[0:w, b, :], ACT.Identity, bias=s.eps[0:w, :])\
                       .then_inc(seed_done, 1)

                def normalise(i):
                    w, b = width(i), i % 2
                    act.wait_ge(norm_step, n[36] + 4 * (i + 1))
                    act.wait_ge(ot_done, n[9] + i)
                    for c in range(2):
                        last = act.activation(normed[0:w, c, :], ps_o[0:w, c, :], ACT.Copy,
                                              scale=norm[0:w, b, 3, c:c + 1])
                    last.then_inc(normed_done, 1)

                def decays(i):
                    w = width(i)
                    act.wait_ge(diff_done, n[9] + (i + 1))
                    parts = [(0, 9)] if w == P else [(0, 1), (3, 9)]
                    for lo, hi in parts:
                        last = act.activation(decay[:, lo:hi, 0:w], decay[:, lo:hi, 0:w], ACT.Abs)
                    last.then_inc(abs_done, 1)
                    act.wait_ge(abs_done, n[9] + (i + 1))
                    for lo, hi in parts:
                        last = act.activation(decay[:, lo:hi, 0:w], decay[:, lo:hi, 0:w], ACT.Exp, scale=-1.0)
                    last.then_inc(exp_done, 1)

                def copies(i):
                    w = width(i)
                    act.wait_ge(tr_done, n[9] + (i + 1))
                    if w == P:
                        act.activation(turned[:, :, :], ps_tr[:, 0:3, :], ACT.Copy).then_inc(qkt_done, 1)
                    else:
                        act.activation(turned[:, 0:2, 0:w], ps_tr[:, 0:2, 0:w], ACT.Copy)
                        act.activation(turned[0:w, 2, :], ps_tr[0:w, 2, :], ACT.Copy).then_inc(qkt_done, 1)

                def wide_levels(i):
                    w, b = width(i), i % 2
                    if w == P:
                        act.wait_ge(masked_done, n[9] + (i + 1))
                        act.activation(a_hg[0:64, b, 64:128], wide[0:64, 64:128], ACT.Copy)
                        act.activation(a_hg[0:32, b, 32:64], wide[0:32, 32:64], ACT.Copy)
                        act.activation(a_hg[64:96, b, 96:128], wide[64:96, 96:128], ACT.Copy)\
                           .then_inc(ahc_done, 1)

                def values(i):
                    w, b = width(i), i % 2
                    act.wait_ge(proj_done, n[9] + (i + 1))
                    if i >= 2:
                        act.wait_ge(roped, n[9] + (i - 1))
                    act.activation(qkv[0:w, b, :], ps_p[b][0:w, :], ACT.Copy).then_inc(v_done, 1)
                    act.wait_ge(rot_done, n[9] + (i + 1))
                    act.wait_ge(kd_copied, n[1] + 1)
                    act.activation(k_dec[0:w, b, :], rot[0:w, 1].rearrange("p a d -> p (a d)"), ACT.Copy,
                                   scale=kd_col[0:w, 0:1] if w == P else kd_col[0:w, 1:2]).then_inc(kdec_done, 1)

                def store_states(which, i, stored):
                    act.wait_ge(s_done, n[9] + (i + 1))
                    buf = s_pr if which == "prompt" else s_sa
                    for c, name in enumerate(("ret", "hgrn")):
                        act.dma_start(s.outs[f"state_{name}_{which}"][0, 0, bass.ds(n["round"], 1)]
                                      .rearrange("h k v -> k h v"), buf[:, c:c + 1, :]).then_inc(stored, 16)

                for i in range(NT + 2):
                    if i >= 2:
                        squares_of(i - 2)
                    if i < NT:
                        decays(i)
                    if 1 <= i <= NT:
                        copies(i - 1)
                    if i >= 2:
                        normalise(i - 2)
                    if 1 <= i <= NT:
                        wide_levels(i - 1)
                    if i < NT:
                        values(i)
                    if i == NT:
                        split_next((0,))
                    if i == NT + 1:
                        split_next((1,))
                    if i >= 2:
                        t = i - 2
                        w = width(t)
                        act.wait_ge(out_done, n[9] + (t + 1))
                        dst = s.o_scr.rearrange("(c g p) t -> g p c t", c=2, g=HEADS)
                        act.dma_start(dst[bass.ds(n["round"], 1), :, :, t * P:t * P + w].rearrange("g p c t -> (g p) c t"),
                                      o_out[:, t % 2, :, 0:w]).then_inc(o_stored[t % 2], 16)
                    if i == NT:
                        store_states("prompt", NP_T - 1, sp_stored)
                    if i == NT + 1:
                        store_states("sample", NT - 1, ss_stored)
                        act.wait_ge(ada_read, n[1] + 1)
                        act.dma_start(s.mod_scr[:, bass.ds(act.snap(g * D), D)], ada_row[:, :]).then_inc(ada_out, 16)
                        split_next((2, 3))
            act.wait_ge(o_stored[0], 16 * 5 * R + PRIMED)
            act.wait_ge(o_stored[1], 16 * 4 * R + PRIMED)
            act.wait_ge(sp_stored, 32 * R + PRIMED)
            act.wait_ge(ss_stored, 32 * R + PRIMED)
            act.wait_ge(ada_out, 16 * R + PRIMED)

        @block.tensor
        def _(pe):
            pe.wait_ge(cleared, 1)
            with pe.Fori(0, R) as g:
                n = counts(pe, g)

                def turned_block(j):
                    pe.wait_ge(lo_done, n[8] + (j + 1))
                    for c in range(3):
                        p = 3 * j + c
                        if p == 0:
                            pe.wait_ge(v_done, n[9])
                        elif p >= 2:
                            pe.wait_ge(t_read, n[12] + (p - 1))
                        at = pieces[c]
                        for k in range(KD):
                            whi, wlo = w_hi[:, k, j, :], w_lo[:, k, j, :]
                            xhi, xlo = s.h_hi[:, k, at], s.h_lo[:, k, at]
                            out = ps_p[p % 2][:, 0:PIECE]
                            pe.matmul(out, whi, xhi, start=(k == 0), stop=False)
                            pe.matmul(out, whi, xlo, start=False, stop=False)
                            last = pe.matmul(out, wlo, xhi, start=False, stop=(k == KD - 1))
                        last.then_inc(t_done, 1)

                def project(i, half):
                    w = width(i)
                    out = ps_p[i % 2][0:w, :]
                    if half == 0:
                        if i == 0:
                            pe.wait_ge(lo_done, n[8] + 8)
                            pe.wait_ge(t_read, n[12] + 12)
                        elif i >= 2:
                            pe.wait_ge(v_done, n[9] + (i - 1))
                    for k in range(4 * half, 4 * half + 4):
                        xhi, xlo = s.h_hi[:, k, i * P:i * P + w], s.h_lo[:, k, i * P:i * P + w]
                        whi = w_hi[:, k].rearrange("p u n -> p (u n)")
                        wlo = w_lo[:, k].rearrange("p u n -> p (u n)")
                        pe.matmul(out, xhi, whi, start=(k == 0), stop=False)
                        pe.matmul(out, xhi, wlo, start=False, stop=False)
                        last = pe.matmul(out, xlo, whi, start=False, stop=(k == KD - 1))
                    if half:
                        last.then_inc(proj_done, 1)

                def scores(i):
                    w = width(i)
                    pe.wait_ge(rot_done, n[9] + (i + 1))
                    pe.wait_ge(qkt_done, n[9] + i)
                    pe.wait_ge(kl_done, n[9] + (i + 1))
                    if w < P:
                        carry(pe, idle)
                    for c in range(2):
                        pe.transpose(ps_tr[:, c, 0:w], rot[0:w, c].rearrange("p a d -> p (a d)"), ident[0:w, 0:w])
                    pe.transpose(ps_tr[0:w, 2, :], k_lv[:, 0, 0:w], ident).then_inc(tr_done, 1)
                    pe.wait_ge(ql_done, n[9] + (i + 1))
                    pe.wait_ge(ah_done, n[9] + i)
                    pe.wait_ge(ahc_done, n[8] + min(i, 8))
                    if w < P:
                        carry(pe, idle)
                    if w == P:
                        pe.matmul(wide[0:64, 64:128], k_lv[:, 1, 0:64], q_lv[:, 0, 64:128], start=True, stop=True)
                        for lo in (0, 64):
                            pe.matmul(wide[lo:lo + 32, lo + 32:lo + 64], k_lv[:, 2, lo:lo + 32],
                                      q_lv[:, 1, lo + 32:lo + 64], start=True, stop=True)
                    for j in range(w // 32):
                        at = slice(32 * j, 32 * j + 32)
                        for c in range(SMALL):
                            pe.matmul(lv[at, c, :], k_lv[:, 3 + c, at], q_lv[:, 2 + c, at], start=True, stop=True)
                        tok = slice(i * P + 32 * j, i * P + 32 * j + 32)
                        last = pe.matmul(lv[at, SMALL, :], hk[:, tok], hq[:, tok], start=True, stop=True)
                    last.then_inc(lv_done, 1)

                def retention_scores(i):
                    w = width(i)
                    pe.wait_ge(qkt_done, n[9] + (i + 1))
                    pe.wait_ge(ar_done, n[9] + i)
                    if w < P:
                        carry(pe, idle)
                    pe.matmul(ps_a[0:w, 0:w], k_t[:, 0:w], q_t[:, 0:w], start=True, stop=True).then_inc(ra_done, 1)

                def mix(i):
                    w, b = width(i), i % 2
                    st = s_pr if i < NP_T else s_sa
                    pe.wait_ge(v_done, n[9] + (i + 1))
                    pe.wait_ge(kdec_done, n[9] + (i + 1))
                    pe.wait_ge(qd_done, n[9] + (i + 1))
                    pe.wait_ge(normed_done, n[9] + i)
                    pe.wait_ge(s_done, n[9] + i)
                    pe.wait_ge(ar_done, n[9] + (i + 1))
                    if i == NP_T:
                        pe.wait_ge(ss_in, n[32] + 32)
                    if w < P:
                        carry(pe, idle)
                    pe.matmul(ps_o[0:w, 0, :], a_ret[0:w, 0:w], qkv[0:w, b, 256:384], start=True, stop=(i == 0))
                    if i:
                        pe.matmul(ps_o[0:w, 0, :], qd_t[:, 0:w], st[:, 0, :], start=False, stop=True)
                    pe.matmul(ps_s[:, 0, :], k_dec[0:w, b, :], qkv[0:w, b, 256:384], start=True, stop=True)
                    pe.matmul(ps_s[:, 1, :], hk_dec[0:w, :], qkv[0:w, b, 384:512], start=True, stop=True)
                    pe.wait_ge(ah_done, n[9] + (i + 1))
                    if w == P:
                        pe.wait_ge(ahc_done, n[8] + (i + 1))
                    else:
                        carry(pe, idle)
                    last = pe.matmul(ps_o[0:w, 1, :], a_hg[0:w, b, 0:w], qkv[0:w, b, 384:512], start=True, stop=(i == 0))
                    if i:
                        last = pe.matmul(ps_o[0:w, 1, :], q_in[:, b, 0:w], st[:, 1, :], start=False, stop=True)
                    last.then_inc(o_done, 1)

                def condition(u):
                    pe.wait_ge(raw_in[u % 4], n[64] + 16 * (u // 4 + 1))
                    for k in range(KD):
                        last = pe.matmul(ps_ot[0:2, 2, :], s.cT[:, k, :], raw[:, u % 4, k, :],
                                         start=(k == 0), stop=(k == KD - 1))
                    last.then_inc(ada_done, 1)

                def turn_out(i):
                    w = width(i)
                    pe.wait_ge(out_done, n[9] + i)
                    if i < 8:
                        condition(8 + i)
                    pe.wait_ge(normed_done, n[9] + (i + 1))
                    if w < P:
                        carry(pe, idle)
                    for c in range(2):
                        last = pe.transpose(ps_ot[:, c, 0:w], normed[0:w, c, :], ident[0:w, 0:w])
                    last.then_inc(ot_done, 1)

                for j in range(4):
                    turned_block(j)
                for i in range(NT + 2):
                    if i < NT:
                        project(i, 0)
                    if 1 <= i <= NT:
                        scores(i - 1)
                    if i >= 2:
                        turn_out(i - 2)
                    if 1 <= i <= NT:
                        retention_scores(i - 1)
                    if i < NT:
                        project(i, 1)
                    if 1 <= i <= NT:
                        mix(i - 1)

        @block.vector
        def _(dve):
            def split(u, units):
                dve.wait_ge(hi_done, units + (u + 1))
                dve.tensor_tensor(w_lo[:, :, u % 4, :], raw[:, u % 4], f32(w_hi[:, :, u % 4, :]),
                                  ALU.subtract).then_inc(lo_done, 1)

            for u in range(4):
                split(u, PRIMED)
            with dve.Fori(0, R) as g:
                n = counts(dve, g)

                def split_next(units):
                    with dve.If(g < R - 1):
                        for u in units:
                            split(u, n[8] + 8)

                bound_at = lambda c: s.bound[:, c, bass.ds(n["round"], 1)]

                dve.wait_ge(kdec_done, n[9])
                col = dve.snap(g * 2 + AT["k_decay"])
                dve.tensor_scalar(kd_col[:, :], s.consts[:, bass.ds(col, 2)], 1.0, None, ALU.mult)\
                   .then_inc(kd_copied, 1)
                dve.wait_ge(t_read, n[12] + 3)
                dve.tensor_scalar(log_f[:, :], log_f[:, :], bound_at(1), bound_at(0), ALU.mult, ALU.add)\
                   .then_inc(f_done, 1)
                dve.tensor_scalar(hk[:, :], hk[:, :], bound_at(1), None, ALU.mult).then_inc(hk_done, 1)
                for u in range(4, 8):
                    split(u, n[8])

                def state(i):
                    w = width(i)
                    dve.wait_ge(o_done, n[9] + (i + 1))
                    dve.wait_ge(s_done, n[9] + i)
                    if i == 0:
                        dve.wait_ge(sp_stored, n[32])
                        dve.tensor_copy(s_pr[:, :, :], ps_s[:, 0:2, :]).then_inc(s_done, 1)
                        return
                    st = s_pr if i < NP_T else s_sa
                    if i == NP_T:
                        dve.wait_ge(ss_in, n[32] + 32)
                    col = dve.snap(g * 2 + (AT["s_decay"] + (0 if w == P else 1)))
                    dve.scalar_tensor_tensor(out=st[:, 0, :], in0=st[:, 0, :], scalar=s.consts[:, bass.ds(col, 1)],
                                             in1=ps_s[:, 0, :], op0=ALU.mult, op1=ALU.add)
                    dve.scalar_tensor_tensor(out=st[:, 1, :], in0=st[:, 1, :], scalar=last_f[:, i % 2:i % 2 + 1],
                                             in1=ps_s[:, 1, :], op0=ALU.mult, op1=ALU.add).then_inc(s_done, 1)

                def differences(i):
                    w = width(i)
                    if i == 0:
                        dve.wait_ge(logf_done, n[1] + 1)
                    dve.wait_ge(kl_done, n[9] + i)
                    dve.wait_ge(ql_done, n[9] + i)
                    b = decay[:, 8, 0:w]
                    dve.tensor_tensor_scan(b, ones[:, 0:w], log_f[:, i * P:i * P + w], 0.0, ALU.mult, ALU.add)\
                       .then_inc(cum_done, 1)
                    dve.wait_ge(cum_done, n[9] + (i + 1))
                    for c, h in enumerate(LEVELS):
                        if 2 * h > w:
                            continue
                        x = b.rearrange("p (n t) -> p n t", t=2 * h)
                        dve.tensor_tensor(decay[:, 1 + c, 0:w].rearrange("p (n t) -> p n t", t=2 * h), x,
                                          x[:, :, h - 1:h].broadcast_to([P, w // (2 * h), 2 * h]), ALU.subtract)
                    dve.tensor_scalar(decay[:, 0, 0:w], b, decay[:, 8, w - 1:w], None, ALU.subtract)\
                       .then_inc(diff_done, 1)

                def gated(i):
                    w, b = width(i), i % 2
                    dve.wait_ge(ot_done, n[9] + (i + 1))
                    use = i // 2
                    dve.wait_ge(o_stored[b], n[80 if b == 0 else 64] + 16 * use)
                    if i < 8:
                        if i == 0:
                            dve.wait_ge(bias_in, n[16] + 16)
                            dve.wait_ge(ada_out, n[16])
                        at = slice(i * P, (i + 1) * P)
                        last = dve.tensor_tensor(ada_row[:, at], ps_ot[0:2, 2, :], ada_bias[:, at], ALU.add)
                        if i == 7:
                            last.then_inc(ada_read, 1)
                    for c in range(2):
                        col = dve.snap(g * 1 + (32 + 4 * c))
                        last = dve.scalar_tensor_tensor(
                            out=o_out[:, b, c, 0:w], in0=ps_ot[:, c, 0:w], scalar=s.cols[:, bass.ds(col, 1)],
                            in1=gate[:, c, i * P:i * P + w], op0=ALU.mult, op1=ALU.mult)
                    last.then_inc(out_done, 1)

                def scored(i):
                    w, b = width(i), i % 2
                    dve.wait_ge(qkt_done, n[9] + (i + 1))
                    qd = dve.snap(g * P + AT["q_decay"])
                    dve.tensor_tensor(qd_t[:, 0:w], q_t[:, 0:w], s.consts[:, bass.ds(qd, w)], ALU.mult)\
                       .then_inc(qd_done, 1)
                    dve.wait_ge(lv_done, n[9] + (i + 1))
                    dve.wait_ge(ah_done, n[9] + i)
                    mask = s.const("level_mask")[0:w].rearrange("p (s l) -> p s l", l=32)
                    dve.tensor_tensor(masked[0:w], lv[0:w], mask, ALU.mult).then_inc(masked_done, 1)
                    dve.wait_ge(masked_done, n[9] + (i + 1))
                    for j in range(w // 32):
                        at = slice(32 * j, 32 * j + 32)
                        last = dve.tensor_reduce(a_hg[at, b, at], masked[at].rearrange("p s l -> p l s"), AX, ALU.add)
                    last.then_inc(ah_done, 1)
                    dve.wait_ge(ra_done, n[9] + (i + 1))
                    rd = dve.snap(g * P + AT["ret_decay"])
                    dve.tensor_tensor(a_ret[0:w, 0:w], ps_a[0:w, 0:w], s.consts[0:w, bass.ds(rd, w)], ALU.mult)\
                       .then_inc(ar_done, 1)

                def queries(i):
                    w, b = width(i), i % 2
                    dve.wait_ge(exp_done, n[9] + (i + 1))
                    dve.wait_ge(lv_done, n[9] + i)
                    dve.tensor_copy(last_f[:, b:b + 1], decay[:, 8, w - 1:w])
                    q = hq[:, i * P:i * P + w]
                    lo = 0 if w == P else 2
                    dve.tensor_tensor(q_in[:, b, 0:w], decay[:, 8, 0:w], q, ALU.mult)
                    dve.tensor_tensor(q_lv[:, lo:7, 0:w], decay[:, 1 + lo:8, 0:w],
                                      q.unsqueeze(1).broadcast_to([P, 7 - lo, w]), ALU.mult).then_inc(ql_done, 1)

                def rotary(i):
                    w = width(i)
                    dve.wait_ge(v_done, n[9] + (i + 1))
                    dve.wait_ge(rot_done, n[9] + i)
                    qk = qkv[0:w, i % 2, 0:256].rearrange("p (c d) -> p c d", c=4)
                    for name, out in (("cos", qk_cos), ("sin", qk_sin)):
                        tab = s.consts[0:w, AT[name] + 64 * i:AT[name] + 64 * i + 64]
                        last = dve.tensor_tensor(out[0:w], qk, tab.unsqueeze(1).broadcast_to([w, 4, 64]), ALU.mult)
                    last.then_inc(roped, 1)
                    dve.wait_ge(roped, n[9] + (i + 1))
                    if i:
                        dve.wait_ge(kdec_done, n[9] + i)
                    pair = lambda t, half: t[0:w].rearrange("p (c a) d -> p c a d", a=2)[:, :, half, :]
                    dve.tensor_tensor(rot[0:w, :, 0, :], pair(qk_cos, 0), pair(qk_sin, 1), ALU.subtract)
                    dve.tensor_tensor(rot[0:w, :, 1, :], pair(qk_cos, 1), pair(qk_sin, 0), ALU.add)\
                       .then_inc(rot_done, 1)

                for i in range(NT + 2):
                    if i >= 2:
                        state(i - 2)
                    if i < NT:
                        differences(i)
                    if 1 <= i <= NT:
                        scored(i - 1)
                    if i >= 2:
                        gated(i - 2)
                    if i < NT:
                        queries(i)
                        rotary(i)
                    if i == NT:
                        split_next((0,))
                split_next((1, 2, 3))


def load_chunk(e, s, x, c, arrived):
    dst = s.raw[:, c % RAW]
    if c < 8:
        half, rows = c // 4, slice((c % 4) * 256, (c % 4) * 256 + 256)
        for m, name in enumerate(("W_gate_e", "W_up_e")):
            src = s.args[name][0, bass.ds(x, 1), rows, half * 256:(half + 1) * 256]
            e.dma_start(dst.rearrange("p (k m n) -> p k m n", k=2, m=2)[:, :, m, :],
                        src.rearrange("e (k p) n -> p (e k) n", p=P)).then_inc(arrived, 16)
    else:
        rows = slice((c - 8) * P, (c - 7) * P)
        for m in range(2):
            at = slice(512 * m, 512 * m + 512)
            src = s.args["W_down_e"][0, bass.ds(x, 1), rows, at]
            e.dma_start(dst[:, at], src.rearrange("e p n -> p (e n)")).then_inc(arrived, 16)


def phase_output(nc, s):
    with ExitStack() as ctx:
        sb, ps, sem = allocate(nc, ctx, "output")
        raw = s.raw
        w_hi = sb("w_hi", [P, KD, D], F32R)
        w_lo = sb("w_lo", [P, KD, D], F32R)
        mod = [sb("mod", [P, 3, D]), raw[:, 3:6]]
        gain = sb("gain", [P, D])
        o_raw = sb("o_raw", [P, KD, P])
        o_hi = sb("o_hi", [P, 2, KD, P], F32R)
        o_lo = sb("o_lo", [P, 2, KD, P], F32R)
        x_old = sb("x_old", [P, 2, D])
        h2 = sb("h2", [P, 2, D])
        h2_t = sb("h2_t", [P, KD, P])
        squares = sb("squares", [P, D])
        w_route = sb("w_route", [P, KD, N_GROUPS + NE])
        b_route = sb("b_route", [P, N_GROUPS + NE])
        mean_sq = sb("mean_sq", [P, NT])
        rstd = sb("rstd", [P, NT])
        newton = sb("newton", [P, 1])
        ps_o = [ps(f"ps_o{b}", [P, 2, 512]) for b in range(2)]
        ps_t = ps("ps_t", [P, KD, P])
        ps_l = ps("ps_l", [P, 512])
        ps_r = ps("ps_r", [P, 512])

        raw_in = [sem(f"raw_in{n}") for n in range(2)]
        o_in, x_in = sem("o_in"), [sem(f"x_in{n}") for n in range(2)]
        rows_in, route_in = sem("rows_in"), sem("route_in")
        hi_done, lo_done, ohi_done, olo_done = sem("hi_done"), sem("lo_done"), sem("ohi_done"), sem("olo_done")
        gain_done, mm_done, gated, added, h_stored = (sem("gain_done"), sem("mm_done"), sem("gated"), sem("added"),
                                                      sem("h_stored"))
        log_done = sem("log_done")
        ms_done, root_done, rstd_step, scaled, h2_done = (sem("ms_done"), sem("root_done"), sem("rstd_step"),
                                                          sem("scaled"), sem("h2_done"))
        t_done, t_read, l_done, l_read = sem("t_done"), sem("t_read"), sem("l_done"), sem("l_read")
        cleared, list_clear, token_done = sem("cleared"), sem("list_clear"), sem("token_done")
        route, exp_done, both_done, counted = sem("route"), sem("exp_done"), sem("both_done"), sem("counted")
        less_max, slots_done, scattered, prefetched = (sem("less_max"), sem("slots_done"), sem("scattered"),
                                                       sem("prefetched"))
        no_token = sb("no_token", [P, NE * NT], I32)
        token = sb("token", [P, NT], I32)
        logits = sb("logits", [P, N_GROUPS + NE])
        probs = sb("probs", [P, 2, 4])
        eq4 = sb("eq4", [P, 4])
        one_g = sb("one_group", [P, 4])
        one_e = sb("one_expert", [P, 2, 4])
        col = sb("col", [P, 1])
        group_w = sb("group_w", [P, 1])
        top = sb("top", [P, 2])
        by_expert = sb("by_expert", [P, NE])
        chosen = sb("chosen", [P, 2, NT, NE])
        both = sb("both", [P, NT, NE])
        before = sb("before", [P, NT + 1, NE])
        rank_of = sb("rank_of", [P, NT, NE])
        prod = sb("prod", [P, 2, NE])
        rank = sb("rank", [P, 2])
        past = sb("past", [P, 2, 8])
        n_past = sb("n_past", [P, 2])
        place = sb("place", [P, 2, 2])
        entry = sb("entry", [P, 2, NT], I32)
        all_prod = sb("all_prod", [P, NT, NE])
        n_of = sb("n_of", [P, NE])
        first = sb("first", [P, NE + 1])
        over = sb("over", [P, NE, 8])
        extra = sb("extra", [P, NE])
        tiles = sb("tiles", [P, NE + 1])
        slot_f = sb("slot_f", [P, 2, NT])
        block = ctx.enter_context(nc.Block())
        a = s.args
        ident = s.const("ident")

        @block.sync
        def _(sp):
            def tile_in(i):
                w = width(i)
                if i:
                    sp.wait_ge(olo_done, i)
                sp.dma_start(o_raw[:, :, 0:w], s.o_scr.rearrange("(k p) t -> p k t", p=P)[:, :, i * P:i * P + w])\
                  .then_inc(o_in, 16)
                if i >= 2:
                    sp.wait_ge(added, i - 1)
                src = a["x_prompt"][0, i * P:(i + 1) * P, :] if i < NP_T else a["x_sample"][0]
                sp.dma_start(x_old[0:w, i % 2, :], src).then_inc(x_in[i % 2], 16)

            tile_in(0)
            for k in range(6, KD):
                sp.wait_ge(lo_done, k - 5)
                sp.dma_start(raw[:, W_OUT_AT[k]], a["W_out"][0, k * P:(k + 1) * P, :])\
                  .then_inc(raw_in[k - 6], 16)
            tile_in(1)
            for q, rows in ((0, P), (1, DEC)):
                if q == 1:
                    sp.wait_ge(lo_done, KD)
                sp.dma_start(mod[q][0:rows], s.mod_scr[q:q + 1, 0:3 * D].rearrange("o (c d) -> o c d", c=3)
                             .broadcast_to([rows, 3, D])).then_inc(rows_in, 16)
            sp.dma_start(gain[:, :], a["norm2_g"].broadcast_to([P, D])).then_inc(rows_in, 16)
            sp.dma_start(w_route[:, :, 0:4], a["W_router_group"][0].rearrange("(k p) n -> p k n", p=P))\
              .then_inc(route_in, 16)
            sp.dma_start(w_route[:, :, 4:20], a["W_router_expert"][0].rearrange("(k p) n -> p k n", p=P))\
              .then_inc(route_in, 16)
            sp.dma_start(b_route[:, 0:4], a["b_router_group"].broadcast_to([P, 4])).then_inc(route_in, 16)
            sp.dma_start(b_route[:, 4:20], a["b_router_expert"].broadcast_to([P, NE])).then_inc(route_in, 16)
            sp.wait_ge(cleared, 1)
            sp.dma_start(s.list_scr.rearrange("(p n) o -> p (n o)", p=P), no_token[:, :]).then_inc(list_clear, 16)
            for i in range(NT):
                if 2 <= i + 1 < NT:
                    tile_in(i + 1)
                w = width(i)
                sp.wait_ge(h2_done, i + 1)
                sp.dma_start(s.h_scr[i * P:i * P + w, :], h2[0:w, i % 2, :]).then_inc(h_stored, 16)
                if i == 0:
                    sp.wait_ge(lo_done, KD)
                    for c in range(3):
                        load_chunk(sp, s, 0, c, prefetched)
            sp.wait_ge(h_stored, 16 * NT)
            sp.wait_ge(prefetched, 32 * 3)

        @block.gpsimd
        def _(pool):
            pool.memset(no_token[:, :], 0).then_inc(cleared, 1)
            def o_low(i):
                w = width(i)
                pool.wait_ge(ohi_done, i + 1)
                pool.tensor_tensor(o_lo[:, i % 2, :, 0:w], o_raw[:, :, 0:w], f32(o_hi[:, i % 2, :, 0:w]),
                                  ALU.subtract).then_inc(olo_done, 1)

            for i in range(4):
                o_low(i)
            pool.wait_ge(list_clear, 16)
            pool.wait_ge(token_done, 1)
            for i in range(NT):
                w = width(i)
                if i + 4 < NT:
                    o_low(i + 4)
                pool.wait_ge(slots_done, i + 1)
                for c in range(2):
                    at = bass.IndirectOffsetOnAxis(ap=entry[0:w, c, i:i + 1], axis=0)
                    pool.indirect_dma_start(out=s.list_scr[:, :], out_offset=at, in_=token[0:w, i:i + 1],
                                            in_offset=None).then_inc(scattered, 16)
            pool.wait_ge(scattered, 16 * 2 * NT)

        @block.scalar
        def _(act):
            act.preload_act_table_set("natural_log_exp_and_others")

            def o_high(i):
                w = width(i)
                act.wait_ge(o_in, 16 * (i + 1))
                if i >= 2:
                    act.wait_ge(mm_done, 2 * (i - 1))
                act.activation(o_hi[:, i % 2, :, 0:w], o_raw[:, :, 0:w], ACT.Copy).then_inc(ohi_done, 1)

            def turned(i):
                w = width(i)
                act.wait_ge(t_done, i + 1)
                for c in range(2):
                    last = act.activation(h2_t[:, 4 * c:4 * c + 4, 0:w], ps_t[:, 4 * c:4 * c + 4, 0:w], ACT.Copy)
                last.then_inc(t_read, 1)

            def exponentials(i):
                w = width(i)
                for n in range(2):
                    act.wait_ge(less_max, 2 * i + n + 1)
                    act.activation(probs[0:w, n, :], probs[0:w, n, :], ACT.Exp).then_inc(exp_done, 1)

            for k in range(KD):
                if k >= 6:
                    act.wait_ge(raw_in[k - 6], 16)
                act.activation(w_hi[:, k], raw[:, W_OUT_AT[k]], ACT.Copy).then_inc(hi_done, 1)
                if k == 1:
                    o_high(0)
            for i in range(NT):
                w = width(i)
                if i + 1 < NT:
                    o_high(i + 1)
                if i:
                    turned(i - 1)
                act.wait_ge(added, i + 1)
                if i:
                    act.wait_ge(ms_done, i)
                act.activation(squares[0:w, :], s.x_mid[0:w, i, :], ACT.Square, scale=1.0 / 32.0,
                               accum_out=mean_sq[0:w, i:i + 1]).then_inc(ms_done, 1)
                act.wait_ge(ms_done, i + 1)
                act.activation(rstd[0:w, i:i + 1], mean_sq[0:w, i:i + 1], ACT.Ln, bias=s.eps[0:w, :])\
                   .then_inc(log_done, 1)
                act.wait_ge(log_done, i + 1)
                act.activation(rstd[0:w, i:i + 1], rstd[0:w, i:i + 1], ACT.Exp, scale=-0.5).then_inc(root_done, 1)
                if i:
                    exponentials(i - 1)
            turned(NT - 1)
            exponentials(NT - 1)

        @block.tensor
        def _(pe):
            def to_logits(i):
                w = width(i)
                pe.wait_ge(h2_done, i + 1)
                pe.wait_ge(t_read, i)
                for k in range(KD):
                    last = pe.transpose(ps_t[:, k, 0:w], h2[0:w, i % 2, k * P:(k + 1) * P], ident[0:w, 0:w])
                last.then_inc(t_done, 1)

            def score(i):
                w = width(i)
                pe.wait_ge(t_read, i + 1)
                pe.wait_ge(l_read, i)
                for k in range(KD):
                    last = pe.matmul(ps_l[0:w, 0:20], h2_t[:, k, 0:w], w_route[:, k, :],
                                     start=(k == 0), stop=(k == KD - 1))
                last.then_inc(l_done, 1)

            def count(i):
                pe.wait_ge(both_done, i + 1)
                pe.wait_ge(slots_done, i)
                at = slice(i * NE, (i + 1) * NE)
                pe.matmul(ps_r[:, at], s.const("tri"), both[:, i, :], start=True, stop=False)
                pe.matmul(ps_r[:, at], s.const("ones"), before[:, i, :], start=False, stop=True).then_inc(counted, 1)

            for i in range(NT):
                w, b = width(i), i % 2
                pe.wait_ge(olo_done, i + 1)
                if i >= 2:
                    pe.wait_ge(gated, i - 1)
                for c in range(2):
                    for k in range(KD):
                        if i == 0 and c == 0:
                            pe.wait_ge(lo_done, k + 1)
                        at = slice(512 * c, 512 * c + 512)
                        out = ps_o[b][0:w, c, :]
                        hi, lo = o_hi[:, b, k, 0:w], o_lo[:, b, k, 0:w]
                        pe.matmul(out, hi, w_hi[:, k, at], start=(k == 0), stop=False)
                        pe.matmul(out, hi, w_lo[:, k, at], start=False, stop=False)
                        last = pe.matmul(out, lo, w_hi[:, k, at], start=False, stop=(k == KD - 1))
                    last.then_inc(mm_done, 1)
                    if i and c == 0:
                        to_logits(i - 1)
                        if i >= 3:
                            count(i - 3)
                if i == 1:
                    pe.wait_ge(route_in, 64)
                if i:
                    score(i - 1)
            to_logits(NT - 1)
            count(NT - 3)
            count(NT - 2)
            score(NT - 1)
            count(NT - 1)
            pe.wait_ge(l_read, NT)
            pe.matmul(ps_l[:, 0:NE], s.const("ones"), before[:, NT, :], start=True, stop=True)\
              .then_inc(counted, 1)

        @block.vector
        def _(dve):
            steps = [0]

            def then(ins):
                steps[0] += 1
                ins.then_inc(route, 1)
                dve.wait_ge(route, steps[0])

            def pick(w, one, value, p):
                then(dve.tensor_reduce(value, p, AX, ALU.max))
                then(dve.tensor_scalar(eq4[0:w], p, value, -8.0, ALU.is_equal, ALU.mult))
                then(dve.tensor_tensor(eq4[0:w], eq4[0:w], s.const("iota", 0, 4)[0:w], ALU.add))
                then(dve.tensor_reduce(col[0:w], eq4[0:w], AX, ALU.min))
                then(dve.tensor_scalar(one, eq4[0:w], col[0:w], None, ALU.is_equal))

            def softmax(i, n, src):
                w = width(i)
                p = probs[0:w, n, :]
                then(dve.tensor_reduce(col[0:w], src, AX, ALU.max))
                dve.tensor_scalar(p, src, col[0:w], None, ALU.subtract).then_inc(less_max, 1)
                dve.wait_ge(exp_done, 2 * i + n + 1)
                then(dve.tensor_reduce(col[0:w], p, AX, ALU.add))
                then(dve.reciprocal(col[0:w], col[0:w]))
                then(dve.tensor_scalar(p, p, col[0:w], None, ALU.mult))

            def choose(i):
                w = width(i)
                dve.wait_ge(l_done, i + 1)
                dve.tensor_tensor(logits[0:w, :], ps_l[0:w, 0:20], b_route[0:w, :], ALU.add).then_inc(l_read, 1)
                dve.wait_ge(l_read, i + 1)
                softmax(i, 0, logits[0:w, 0:4])
                pick(w, one_g[0:w], group_w[0:w], probs[0:w, 0, :])
                of_group = one_g[0:w].unsqueeze(2).broadcast_to([w, 4, 4])
                view = lambda t: t.rearrange("p (g e) -> p g e", g=4)
                then(dve.tensor_tensor(view(by_expert[0:w]), view(logits[0:w, 4:20]), of_group, ALU.mult))
                then(dve.tensor_reduce(one_e[0:w, 0], view(by_expert[0:w]).rearrange("p g e -> p e g"), AX, ALU.add))
                softmax(i, 1, one_e[0:w, 0])
                p = probs[0:w, 1, :]
                pick(w, one_e[0:w, 0], top[0:w, 0:1], p)
                then(dve.scalar_tensor_tensor(out=p, in0=one_e[0:w, 0], scalar=-2.0, in1=p, op0=ALU.mult, op1=ALU.add))
                pick(w, one_e[0:w, 1], top[0:w, 1:2], p)
                for c in range(2):
                    last = dve.tensor_tensor(view(chosen[0:w, c, i]), of_group,
                                             one_e[0:w, c].unsqueeze(1).broadcast_to([w, 4, 4]), ALU.mult)
                then(last)
                then(dve.tensor_tensor(both[0:w, i], chosen[0:w, 0, i], chosen[0:w, 1, i], ALU.add))
                dve.tensor_tensor(before[:, i + 1, :], before[:, i, :], both[:, i, :], ALU.add).then_inc(both_done, 1)
                then(dve.tensor_tensor(col[0:w], top[0:w, 0:1], top[0:w, 1:2], ALU.add))
                then(dve.reciprocal(col[0:w], col[0:w]))
                then(dve.tensor_tensor(col[0:w], col[0:w], group_w[0:w], ALU.mult))
                then(dve.tensor_scalar(s.weight[0:w, :, i], top[0:w, :], col[0:w], None, ALU.mult))

            def enter(i):
                w = width(i)
                dve.wait_ge(counted, i + 1)
                then(dve.tensor_copy(rank_of[0:w, i, :], ps_r[0:w, i * NE:(i + 1) * NE]))
                of_c = lambda t: t.unsqueeze(1).broadcast_to([w, 2, NE])
                for c, table in enumerate((rank_of[0:w, i, :], s.const("place")[0:w])):
                    then(dve.tensor_tensor(prod[0:w], chosen[0:w, :, i, :], of_c(table), ALU.mult))
                    then(dve.tensor_reduce(rank[0:w] if c == 0 else place[0:w, 0], prod[0:w], AX, ALU.add))
                then(dve.tensor_tensor(past[0:w], rank[0:w].unsqueeze(2).broadcast_to([w, 2, 8]),
                                       s.const("limits")[0:w].unsqueeze(1).broadcast_to([w, 2, 8]), ALU.is_ge))
                then(dve.tensor_reduce(n_past[0:w], past[0:w], AX, ALU.add))
                then(dve.scalar_tensor_tensor(out=place[0:w, 1], in0=rank[0:w], scalar=float(NE * NT),
                                              in1=place[0:w, 0], op0=ALU.mult, op1=ALU.add))
                then(dve.scalar_tensor_tensor(out=place[0:w, 0], in0=n_past[0:w], scalar=float(1 - P * NE * NT),
                                              in1=place[0:w, 1], op0=ALU.mult, op1=ALU.add))
                dve.tensor_copy(entry[0:w, :, i], place[0:w, 0]).then_inc(slots_done, 1)

            for t in (both, before, rank_of, chosen[:, 0], chosen[:, 1]):
                then(dve.memset(t[:, :, :], 0.0))
            dve.tensor_copy(token[:, :], s.const("token")).then_inc(token_done, 1)
            for k in range(KD):
                dve.wait_ge(hi_done, k + 1)
                dve.tensor_tensor(w_lo[:, k], raw[:, W_OUT_AT[k]], f32(w_hi[:, k]), ALU.subtract).then_inc(lo_done, 1)
            dve.wait_ge(rows_in, 48)
            for q, rows in ((0, P), (1, DEC)):
                last = dve.scalar_tensor_tensor(out=mod[q][0:rows, 2], in0=mod[q][0:rows, 2], scalar=1.0,
                                                in1=gain[0:rows, :], op0=ALU.add, op1=ALU.mult)
            last.then_inc(gain_done, 1)
            dve.wait_ge(gain_done, 1)
            dve.wait_ge(route_in, 64)
            for i in range(NT):
                w, b, q = width(i), i % 2, i // NP_T
                x_new = s.x_mid[0:w, i, :]
                dve.wait_ge(mm_done, 2 * i + 2)
                dve.tensor_tensor(x_new, ps_o[b][0:w].rearrange("p c d -> p (c d)"), mod[q][0:w, 0],
                                  ALU.mult).then_inc(gated, 1)
                dve.wait_ge(gated, i + 1)
                dve.wait_ge(x_in[b], 16 * (i // 2 + 1))
                dve.tensor_tensor(x_new, x_new, x_old[0:w, b, :], ALU.add).then_inc(added, 1)
                if i >= 3:
                    enter(i - 3)
                if i >= 2:
                    dve.wait_ge(t_done, i - 1)
                    dve.wait_ge(h_stored, 16 * (i - 1))
                dve.wait_ge(root_done, i + 1)
                seed = rstd[0:w, i:i + 1]
                dve.scalar_tensor_tensor(out=newton[0:w], in0=mean_sq[0:w, i:i + 1], scalar=s.eps[0:w, :], in1=seed,
                                         op0=ALU.add, op1=ALU.mult).then_inc(rstd_step, 1)
                dve.wait_ge(rstd_step, 3 * i + 1)
                dve.tensor_scalar(newton[0:w], newton[0:w], seed, -0.5, ALU.mult, ALU.mult).then_inc(rstd_step, 1)
                dve.wait_ge(rstd_step, 3 * i + 2)
                dve.scalar_tensor_tensor(out=seed, in0=newton[0:w], scalar=1.5, in1=seed, op0=ALU.add, op1=ALU.mult)\
                   .then_inc(rstd_step, 1)
                dve.wait_ge(rstd_step, 3 * i + 3)
                dve.scalar_tensor_tensor(out=h2[0:w, b, :], in0=x_new, scalar=rstd[0:w, i:i + 1],
                                         in1=mod[q][0:w, 2], op0=ALU.mult, op1=ALU.mult).then_inc(scaled, 1)
                dve.wait_ge(scaled, i + 1)
                dve.tensor_tensor(h2[0:w, b, :], h2[0:w, b, :], mod[q][0:w, 1], ALU.add).then_inc(h2_done, 1)
                if i:
                    choose(i - 1)
            enter(NT - 3)
            enter(NT - 2)
            choose(NT - 1)
            enter(NT - 1)
            dve.wait_ge(counted, NT + 1)
            then(dve.tensor_copy(n_of[:, :], ps_l[:, 0:NE]))
            ones = s.const("ones")
            then(dve.memset(first[:, 0:1], 0.0))
            then(dve.tensor_tensor_scan(first[:, 1:NE + 1], ones[:, 0:NE], n_of[:, :], 0.0, ALU.mult, ALU.add))
            then(dve.tensor_tensor(over[:, :, :], n_of[:, :].unsqueeze(2).broadcast_to([P, NE, 8]),
                                   s.const("limits").unsqueeze(1).broadcast_to([P, NE, 8]), ALU.is_gt))
            then(dve.tensor_reduce(extra[:, :], over[:, :, :], AX, ALU.add))
            then(dve.memset(tiles[:, 0:1], 0.0))
            then(dve.tensor_tensor_scan(tiles[:, 1:NE + 1], ones[:, 0:NE], extra[:, :], 0.0, ALU.mult, ALU.add))
            then(dve.tensor_tensor(tiles[:, 0:NE], tiles[:, 0:NE], s.const("iota"), ALU.add))
            then(dve.tensor_copy(s.plan[:, 0:NE + 1], first[0:1, :]))
            then(dve.tensor_copy(s.plan[:, 32:32 + NE], extra[0:1, :]))
            then(dve.tensor_copy(s.plan[:, 64:64 + NE], tiles[0:1, 0:NE]))
            then(dve.tensor_tensor(both[:, :, :], rank_of[:, :, :], first[:, 0:NE].unsqueeze(1).broadcast_to([P, NT, NE]),
                                   ALU.add))
            for c in range(2):
                then(dve.tensor_tensor(all_prod[:, :, :], both[:, :, :], chosen[:, c], ALU.mult))
                then(dve.tensor_reduce(slot_f[:, c, :], all_prod[:, :, :], AX, ALU.add))
            dve.tensor_copy(s.slot[:, :, :], slot_f[:, :, :])


def phase_experts(nc, s):
    CH = CHUNKS
    with ExitStack() as ctx:
        sb, ps, sem = allocate(nc, ctx, "experts")
        raw, raw_in = s.raw, [sem(f"raw_in{n}") for n in range(RAW)]
        w_hi = sb("w_hi", [P, CH, D], F32R)
        w_lo = sb("w_lo", [P, CH, D], F32R)
        x_rows = sb("x_rows", [P, D])
        x_hi = sb("x_hi", [P, KD, P], F32R)
        x_lo = sb("x_lo", [P, KD, P], F32R)
        act_g = sb("act_g", [P, 2, 256])
        hid = sb("hid", [P, 512])
        h_hi = sb("h_hi", [P, KF, P], F32R)
        h_lo = sb("h_lo", [P, KF, P], F32R)
        y = sb("y", [P, D])
        ps_g = [ps(f"ps_g{n}", [P, 512]) for n in range(2)]
        ps_x = [ps(f"ps_x{n}", [P, 4, P]) for n in range(2)]
        ps_h = [ps(f"ps_h{n}", [P, 4, P]) for n in range(2)]
        ps_y = [ps(f"ps_y{n}", [P, 512]) for n in range(2)]
        lists = sb("lists", [P, NE * NT + 1], I32)
        index = sb("index", [P, 1], I32)
        lists_in, index_done = sem("lists_in"), sem("index_done")
        hi_done, lo_done, used = sem("hi_done"), sem("lo_done"), sem("used")
        x_in, xt_done, xhi_done, xlo_done = sem("x_in"), sem("xt_done"), sem("xhi_done"), sem("xlo_done")
        silu_done, hid_done = sem("silu_done"), sem("hid_done")
        ht_done, hhi_done, hlo_done = sem("ht_done"), sem("hhi_done"), sem("hlo_done")
        y0_done, y1_done, y_stored, idle = sem("y0_done"), sem("y1_done"), sem("y_stored"), sem("idle")
        block = ctx.enter_context(nc.Block())
        a = s.args
        ident = s.const("ident")

        def experts(e, tile):
            def one(x, last_expert):
                extra = e.value_load(s.plan[0:1, bass.ds(x + 32, 1)], min_val=0, max_val=8)
                base = e.value_load(s.plan[0:1, bass.ds(x + 64, 1)], min_val=0, max_val=32)
                with e.If(extra > 0):
                    with e.Fori(0, extra) as j:
                        tile(x, e.snap(base + j), j, False, last_expert)
                tile(x, e.snap(base + extra), extra, True, last_expert)

            with e.Fori(0, NE - 1) as x:
                one(x, False)
            one(NE - 1, True)

        @block.sync
        def _(sp):
            def load(x, c, wait):
                sp.wait_ge(lo_done, wait)
                if not isinstance(wait, int):
                    carry(sp, idle)
                load_chunk(sp, s, x if isinstance(x, int) else sp.snap(x * 1), c, raw_in[c % RAW])

            for c in range(3):
                sp.sem_inc(raw_in[c], 32)
            for c in range(3, RAW):
                load_chunk(sp, s, 0, c, raw_in[c])
            for c in range(RAW, CH):
                load(0, c, c + 1 - RAW)
            with sp.Fori(1, NE) as x:
                for c in range(CH):
                    load(x, c, sp.snap(x * CH + (c + 1 - RAW)))

        @block.gpsimd
        def _(pool):
            for semaphore in (y0_done, y1_done, hid_done, hlo_done):
                pool.sem_inc(semaphore, PRIMED)
            pool.dma_start(s.y_scr[SLOTS:SLOTS + P, 0:P], ident).then_inc(y_stored, 16)
            pool.wait_ge(lists_in, 16)

            def gather(column, n):
                pool.tensor_copy(index[:, :], lists[:, column]).then_inc(index_done, 1)
                pool.wait_ge(index_done, n)
                if not isinstance(n, int):
                    carry(pool, idle)
                pool.indirect_dma_start(out=x_rows[:, :], out_offset=None, in_=s.h_scr[:, :],
                                        in_offset=bass.IndirectOffsetOnAxis(ap=index[:, 0:1], axis=0))\
                    .then_inc(x_in, 16)

            pool.memset(lists[:, NE * NT:], 0)
            gather(slice(0, 1), 1)

            def tile(x, t, j, last, last_expert):
                start = pool.value_load(s.plan[0:1, bass.ds(x, 1)], min_val=0, max_val=SLOTS)
                row = pool.snap(start + j * P, min_val=0, max_val=SLOTS)
                after = (x + 1) * NT if last else x * NT + j + 1
                column = slice(after, after + 1) if last_expert and last else bass.ds(pool.snap(after), 1)
                pool.wait_ge(xt_done, pool.snap(t + 1))
                carry(pool, idle)
                gather(column, pool.snap(t + 2))
                pool.wait_ge(y_stored, pool.snap(t * 16 + 16))
                pool.wait_ge(y0_done, pool.snap(t + (1 + PRIMED)))
                pool.wait_ge(y1_done, pool.snap(t + (1 + PRIMED)))
                carry(pool, idle)
                pool.dma_start(s.y_scr[bass.ds(row, P), :], y[:, :]).then_inc(y_stored, 16)

            experts(pool, tile)
            total = pool.value_load(s.plan[0:1, 64 + NE - 1:64 + NE], min_val=0, max_val=32)
            extra = pool.value_load(s.plan[0:1, 32 + NE - 1:32 + NE], min_val=0, max_val=8)
            pool.wait_ge(y_stored, pool.snap((total + extra + 2) * 16))
            carry(pool, idle)

        @block.scalar
        def _(act):
            def split(x, c, t):
                act.wait_ge(raw_in[c % RAW], act.snap(x * 64 + 32 * (c // RAW + 1)) if t is not None
                            else 32 * (c // RAW + 1))
                if t is not None:
                    act.wait_ge(used, act.snap(t * CH + (c + 1)))
                act.activation(w_hi[:, c], raw[:, c % RAW], ACT.Copy).then_inc(hi_done, 1)

            def x_high(t):
                act.wait_ge(xt_done, t + 2 if isinstance(t, int) else act.snap(t + 2))
                for n in range(2):
                    act.activation(x_hi[:, 4 * n:4 * n + 4, :], ps_x[n][:, :, :], ACT.Copy).then_inc(xhi_done, 1)

            def tile(x, t, j, last, last_expert):
                splits = last and not last_expert
                after = act.snap(x + 1) if splits else None
                t2 = act.snap(t * 2)

                def some(lo, hi):
                    if splits:
                        for c in range(lo, hi):
                            split(after, c, t)

                def silu(n):
                    act.wait_ge(used, act.snap(t * CH + 4 * (n + 1)))
                    act.activation(act_g[:, n, :], ps_g[n][:, 0:256], ACT.Silu).then_inc(silu_done, 1)

                def h_high(n):
                    act.wait_ge(ht_done, act.snap(t2 + (n + 1)))
                    act.activation(h_hi[:, 2 * n:2 * n + 2, :], ps_h[n][:, 0:2, :], ACT.Copy).then_inc(hhi_done, 1)

                some(0, 3)
                silu(0)
                some(3, 6)
                silu(1)
                h_high(0)
                x_high(t)
                h_high(1)
                some(6, 9)
                act.wait_ge(used, act.snap(t * CH + CH))
                act.wait_ge(y_stored, act.snap(t * 16 + 16))
                act.activation(y[:, 0:512], ps_y[0][:, :], ACT.Copy).then_inc(y0_done, 1)
                some(9, CH)

            act.preload_act_table_set("silu_and_others")
            act.dma_start(lists[:, 0:NE * NT], s.list_scr.rearrange("(p n) o -> p (n o)", p=P)).then_inc(lists_in, 16)
            for c in range(6):
                split(0, c, None)
            x_high(-1)
            for c in range(6, CH):
                split(0, c, None)
            experts(act, tile)

        @block.vector
        def _(dve):
            def split(x, c, first):
                dve.wait_ge(hi_done, c + 1 if first else dve.snap(x * CH + (c + 1)))
                dve.tensor_tensor(w_lo[:, c], raw[:, c % RAW], f32(w_hi[:, c]), ALU.subtract).then_inc(lo_done, 1)

            def x_low(t):
                for n in range(2):
                    dve.wait_ge(xhi_done, 2 * t + n + 3 if isinstance(t, int) else dve.snap(t * 2 + (n + 3)))
                    last = dve.tensor_tensor(x_lo[:, 4 * n:4 * n + 4, :], ps_x[n][:, :, :],
                                             f32(x_hi[:, 4 * n:4 * n + 4, :]), ALU.subtract)
                last.then_inc(xlo_done, 1)

            def tile(x, t, j, last, last_expert):
                splits = last and not last_expert
                after = dve.snap(x + 1) if splits else None
                t2 = dve.snap(t * 2)

                def some(lo, hi):
                    if splits:
                        for c in range(lo, hi):
                            split(after, c, False)

                def product(n):
                    dve.wait_ge(silu_done, dve.snap(t2 + (n + 1)))
                    dve.tensor_tensor(hid[:, 256 * n:256 * n + 256], act_g[:, n, :], ps_g[n][:, 256:512],
                                      ALU.mult).then_inc(hid_done, 1)

                def h_low(n):
                    dve.wait_ge(hhi_done, dve.snap(t2 + (n + 1)))
                    dve.tensor_tensor(h_lo[:, 2 * n:2 * n + 2, :], ps_h[n][:, 0:2, :],
                                      f32(h_hi[:, 2 * n:2 * n + 2, :]), ALU.subtract).then_inc(hlo_done, 1)

                some(0, 3)
                product(0)
                some(3, 6)
                product(1)
                h_low(0)
                x_low(t)
                h_low(1)
                some(6, 9)
                dve.wait_ge(used, dve.snap(t * CH + CH))
                dve.wait_ge(y_stored, dve.snap(t * 16 + 16))
                dve.tensor_copy(y[:, 512:1024], ps_y[1][:, :]).then_inc(y1_done, 1)
                some(9, CH)

            for c in range(6):
                split(0, c, True)
            x_low(-1)
            for c in range(6, CH):
                split(0, c, True)
            experts(dve, tile)

        @block.tensor
        def _(pe):
            def turn_x(t):
                if isinstance(t, int):
                    pe.wait_ge(x_in, 16)
                else:
                    pe.wait_ge(x_in, pe.snap(t * 16 + 32))
                    pe.wait_ge(xlo_done, pe.snap(t + 1))
                for k in range(KD):
                    last = pe.transpose(ps_x[k // 4][:, k % 4, :], x_rows[:, k * P:(k + 1) * P], ident)
                last.then_inc(xt_done, 1)

            turn_x(-1)

            def tile(x, t, j, last, _):
                t2 = pe.snap(t * 2 + PRIMED)
                chunk0 = pe.snap(x * CH) if not isinstance(x, int) else x * CH
                pe.wait_ge(xlo_done, pe.snap(t + 1))
                pe.wait_ge(hid_done, t2)
                for half in range(2):
                    out = ps_g[half][:, :]
                    for k in range(KD):
                        c = 4 * half + k // 2
                        if k % 2 == 0:
                            pe.wait_ge(lo_done, chunk0 + (c + 1))
                        at = slice(512 * (k % 2), 512 * (k % 2) + 512)
                        pe.matmul(out, x_hi[:, k, :], w_hi[:, c, at], start=(k == 0), stop=False)
                        pe.matmul(out, x_hi[:, k, :], w_lo[:, c, at], start=False, stop=False)
                        ins = pe.matmul(out, x_lo[:, k, :], w_hi[:, c, at], start=False, stop=(k == KD - 1))
                        if k % 2:
                            ins.then_inc(used, 1)

                def turn_h(n):
                    pe.wait_ge(hid_done, pe.snap(t2 + (n + 1)))
                    pe.wait_ge(hlo_done, t2)
                    for f in range(2):
                        ins = pe.transpose(ps_h[n][:, f, :], hid[:, (2 * n + f) * P:(2 * n + f + 1) * P], ident)
                    ins.then_inc(ht_done, 1)

                turn_h(0)
                turn_x(t)
                turn_h(1)
                pe.wait_ge(y0_done, pe.snap(t + PRIMED))
                pe.wait_ge(y1_done, pe.snap(t + PRIMED))
                for f in range(KF):
                    if f % 2 == 0:
                        pe.wait_ge(hlo_done, pe.snap(t2 + (f // 2 + 1)))
                    pe.wait_ge(lo_done, chunk0 + (9 + f))
                    for m in range(2):
                        at = slice(512 * m, 512 * m + 512)
                        pe.matmul(ps_y[m][:, :], h_hi[:, f, :], w_hi[:, 8 + f, at], start=(f == 0), stop=False)
                        pe.matmul(ps_y[m][:, :], h_hi[:, f, :], w_lo[:, 8 + f, at], start=False, stop=False)
                        ins = pe.matmul(ps_y[m][:, :], h_lo[:, f, :], w_hi[:, 8 + f, at], start=False,
                                        stop=(f == KF - 1))
                    ins.then_inc(used, 1)

            experts(pe, tile)


def phase_combine(nc, s):
    with ExitStack() as ctx:
        sb, ps, sem = allocate(nc, ctx, "combine")
        B = 3
        y = sb("y", [P, B, 2, D])
        x = s.x_mid
        part = sb("part", [P, B, D])
        gate = sb("gate", [P, 2, D])
        gain = sb("gain", [P, D])
        squares = sb("squares", [P, D])
        mean_sq = sb("mean_sq", [P, NT])
        rstd = sb("rstd", [P, NT])
        rows_in, y_in = sem("rows_in"), [sem(f"y_in{n}") for n in range(B)]
        first_done, summed, gated, added, ms_done, root_done, rstd_done, out_done = (
            sem(n) for n in ("first_done", "summed", "gated", "added", "ms_done", "root_done", "rstd_done",
                             "out_done"))
        stored = sem("stored")
        block = ctx.enter_context(nc.Block())

        @block.sync
        def _(sp):
            for q, rows in ((0, P), (1, DEC)):
                sp.dma_start(gate[0:rows, q], s.mod_scr[q:q + 1, 3 * D:4 * D].broadcast_to([rows, D]))\
                  .then_inc(rows_in, 16)
            sp.dma_start(gain[:, :], s.args["final_norm_g"].unsqueeze(0).broadcast_to([P, D])).then_inc(rows_in, 16)

        @block.gpsimd
        def _(pool):
            for i in range(NT):
                w = width(i)
                if i >= B:
                    pool.wait_ge(summed, i - B + 1)
                for c in range(2):
                    pool.indirect_dma_start(out=y[0:w, i % B, c, :], out_offset=None, in_=s.y_scr[0:SLOTS, :],
                                            in_offset=bass.IndirectOffsetOnAxis(ap=s.slot[0:w, c, i:i + 1], axis=0))\
                        .then_inc(y_in[i % B], 16)

        def store(act, i):
            w, b = width(i), i % B
            act.wait_ge(out_done, i + 1)
            dst = s.outs["y_prompt"][0, i * P:i * P + w, :] if i < NP_T else s.outs["y_sample"][0]
            act.dma_start(dst, x[0:w, i]).then_inc(stored, 16)

        @block.scalar
        def _(act):
            for i in range(NT):
                w, b = width(i), i % B
                act.wait_ge(y_in[b], 32 * (i // B + 1))
                if i >= B:
                    act.wait_ge(added, i - B + 1)
                act.activation(part[0:w, b], y[0:w, b, 0], ACT.Copy, scale=s.weight[0:w, 0, i:i + 1])\
                   .then_inc(first_done, 1)
                act.wait_ge(added, i + 1)
                if i:
                    act.wait_ge(ms_done, i)
                act.activation(squares[0:w, :], x[0:w, i], ACT.Square, scale=1.0 / 32.0,
                               accum_out=mean_sq[0:w, i:i + 1]).then_inc(ms_done, 1)
                act.wait_ge(ms_done, i + 1)
                act.activation(rstd[0:w, i:i + 1], mean_sq[0:w, i:i + 1], ACT.Sqrt, bias=s.eps[0:w, :])\
                   .then_inc(root_done, 1)
                if i:
                    store(act, i - 1)
            store(act, NT - 1)
            act.wait_ge(stored, 16 * NT)

        @block.vector
        def _(dve):
            def normalise(i):
                w, b = width(i), i % B
                dve.wait_ge(root_done, i + 1)
                dve.reciprocal(rstd[0:w, i:i + 1], rstd[0:w, i:i + 1]).then_inc(rstd_done, 1)
                dve.wait_ge(rstd_done, i + 1)
                dve.scalar_tensor_tensor(out=x[0:w, i], in0=x[0:w, i], scalar=rstd[0:w, i:i + 1], in1=gain[0:w],
                                         op0=ALU.mult, op1=ALU.mult).then_inc(out_done, 1)

            dve.wait_ge(rows_in, 48)
            for i in range(NT):
                w, b, q = width(i), i % B, i // NP_T
                dve.wait_ge(first_done, i + 1)
                dve.scalar_tensor_tensor(out=part[0:w, b], in0=y[0:w, b, 1], scalar=s.weight[0:w, 1, i:i + 1],
                                         in1=part[0:w, b], op0=ALU.mult, op1=ALU.add).then_inc(summed, 1)
                dve.wait_ge(summed, i + 1)
                dve.tensor_tensor(part[0:w, b], part[0:w, b], gate[0:w, q], ALU.mult).then_inc(gated, 1)
                dve.wait_ge(gated, i + 1)
                dve.tensor_tensor(x[0:w, i], x[0:w, i], part[0:w, b], ALU.add).then_inc(added, 1)
                if i:
                    normalise(i - 1)
            normalise(NT - 1)


def build(nc, args, outs):
    s = Shared()
    s.args, s.outs = args, outs
    with ExitStack() as ctx:
        sb, ps, sem = allocate(nc, ctx, "all")
        s.consts = sb("consts_sb", [P, N_CONST])
        s.eps = sb("eps", [P, 1])
        s.o_scr = nc.dram_tensor("o_scratch", [D, NTOK], F32).ap()
        s.mod_scr = nc.dram_tensor("mod_scratch", [2, 4 * D], F32).ap()
        s.h_scr = nc.dram_tensor("h_scratch", [NTOK, D], F32).ap()
        s.list_scr = nc.dram_tensor("list_scratch", [P * NE * NT, 1], I32).ap()
        s.y_scr = nc.dram_tensor("y_scratch", [ROWS, D], F32).ap()
        s.slot = sb("slot", [P, 2, NT], I32)
        s.weight = sb("weight", [P, 2, NT])
        s.plan = sb("plan", [1, 96], I32)
        s.raw = sb("raw", [P, RAW, D])
        with ExitStack() as ctx2:
            sb2, _, _ = allocate(nc, ctx2, "early")
            s.cT = sb2("cT", [P, KD, 2])
            s.cols = sb2("cols", [P, 40])
            s.bound = sb2("bound", [P, 2, HEADS])
            s.h_hi = sb2("h_hi", [P, KD, NTOK], F32R)
            s.h_lo = sb2("h_lo", [P, KD, NTOK], F32R)
            phase_condition(nc, s)
            phase_mixers(nc, s)
        s.x_mid = sb("x_mid", [P, NT, D])
        phase_output(nc, s)
        phase_experts(nc, s)
        phase_combine(nc, s)


_INS = ["x_prompt", "x_sample", "c_prompt", "c_sample", "state_ret", "state_hgrn", "W_ada", "b_ada", "norm1_g",
        "norm2_g", "W_in", "ret_norm_g", "hgrn_norm_g", "hgrn_lb_logits", "W_out", "W_router_group",
        "b_router_group", "W_router_expert", "b_router_expert", "W_gate_e", "W_up_e", "W_down_e", "final_norm_g"]
_STATE = (1, 1, HEADS, P, P)
_OUTS = dict(y_prompt=(1, SEQ, D), y_sample=(1, DEC, D), state_ret_prompt=_STATE, state_hgrn_prompt=_STATE,
             state_ret_sample=_STATE, state_hgrn_sample=_STATE)


def kernel(**inputs):
    import concourse.bacc as _bacc
    from concourse.bass_utils import run_bass_kernel_spmd as _run

    nc = _bacc.Bacc("TRN2", target_bir_lowering=False, num_devices=1)
    arrays, args, outs = {}, {}, {}
    for name in [*_INS, "consts"]:
        a = np.ascontiguousarray(constants() if name == "consts" else inputs[name])
        arrays[f"in_{name}_dram"] = a
        args[name] = nc.dram_tensor(f"in_{name}_dram", a.shape, mybir.dt.from_np(a.dtype), kind="ExternalInput").ap()
    for name, shape in _OUTS.items():
        outs[name] = nc.dram_tensor(f"out_{name}_dram", shape, F32, kind="ExternalOutput").ap()
    build(nc, args, outs)
    r = _run(nc, [arrays], core_ids=[0])
    return tuple(r.results[0][f"out_{name}_dram"] for name in _OUTS)
```

```python
from contextlib import ExitStack

import numpy as np

import concourse.bass as bass
from concourse import mybir

F32 = mybir.dt.float32
F32R = mybir.dt.float32r
I32 = mybir.dt.int32
ALU = mybir.AluOpType
ACT = mybir.ActivationFunctionType
AX = mybir.AxisListType.X

P = 128
D = 1024
KD = D // P
SEQ = 1024
DEC = 32
PAST = 1024
NTOK = SEQ + DEC
NP_T = SEQ // P
NT = NP_T + 1
HEADS = 4
D_IN = 4096
EPS = 1e-6
N_GROUPS = 4
PER_GROUP = 4
NE = N_GROUPS * PER_GROUP
F = 512
KF = F // P
CHUNKS = 12
RAW = 6
GROUPS = ((0, 2), (2, 4), (4, 7), (7, NT))
W_OUT_AT = (4, 5, 0, 1, 2, 3, 4, 5)
UNIT_AT = (2560, 1536, 3584, 2048, 0, 512, 1024, 3072)
SLOTS = 2 * NTOK
ROWS = SLOTS + NT * P
PIECE = NTOK // 3
SCALE = float(np.float32(128.0) ** np.float32(-0.5))
LEVELS = (64, 32, 16, 8, 4, 2, 1)
SMALL = 5
PRIMED = 4

KEPT = dict(ident=P, ones=P, tri=P, iota=NE, limits=8, place=NE, token=NT)
TABLES = dict(cos=NT * 64, sin=NT * 64, ret_decay=HEADS * P, q_decay=HEADS * P, level_mask=(SMALL + 1) * 32,
              k_decay=2 * HEADS, s_decay=2 * HEADS)
CONSTS = {**KEPT, **TABLES}
N_KEPT, N_TABLES = sum(KEPT.values()), sum(TABLES.values())
AT = {name: at for part in (KEPT, TABLES) for name, at in zip(part, np.cumsum([0, *part.values()]).tolist())}


def width(i):
    return P if i < NP_T else DEC


def constants():
    f = np.float32
    c = {}
    c["ident"] = np.eye(P)
    c["ones"] = np.ones((P, P))
    c["tri"] = np.triu(np.ones((P, P)), 1)
    inv = (f(1.0) / (f(10000.0) ** (np.arange(64, dtype=f) / f(64)))).astype(f)
    pos = np.concatenate([np.arange(SEQ), PAST + np.arange(P)]).astype(f)
    ang = (pos[:, None] * inv[None, :]).astype(f).reshape(NT, P, 64).transpose(1, 0, 2)
    c["cos"], c["sin"] = np.cos(ang).reshape(P, -1), np.sin(ang).reshape(P, -1)
    lg = np.log(1.0 - np.exp2(-5.0 - np.arange(HEADS)))
    j = np.arange(P)
    diff = j[None, :] - j[:, None]
    decay = np.where(diff[:, None] >= 0, np.exp(np.maximum(diff, 0)[:, None] * lg[None, :, None]), 0.0)
    c["ret_decay"] = decay * SCALE
    c["q_decay"] = np.broadcast_to(np.exp((j[None, None] + 1.0) * lg[None, :, None]), (P, HEADS, P))
    full, short = np.exp((P - 1.0 - j)[:, None] * lg), np.exp(np.maximum(DEC - 1.0 - j, 0)[:, None] * lg)
    c["k_decay"] = np.stack([full, short], -1) * SCALE
    c["s_decay"] = np.broadcast_to(np.stack([np.exp(P * lg), np.exp(DEC * lg)], -1), (P, HEADS, 2))
    m, l = np.arange(P)[:, None] % 32, np.arange(32)[None, :]
    masks = [(m // (2 * h) == l // (2 * h)) & (m % (2 * h) < h) & (l % (2 * h) >= h) for h in LEVELS[2:]]
    c["level_mask"] = np.stack([*masks, m == l], 1)
    c["iota"] = np.broadcast_to(np.arange(NE), (P, NE))
    c["place"] = np.broadcast_to(np.arange(NE) * NT, (P, NE))
    c["token"] = np.arange(NT)[None, :] * P + np.arange(P)[:, None]
    c["limits"] = np.broadcast_to(P * (1.0 + np.arange(8)), (P, 8))
    return np.concatenate([np.asarray(c[k], f).reshape(P, -1) for k in CONSTS], 1)


class Shared:

    def const(self, name, a=0, b=None):
        b = CONSTS[name] if b is None else b
        return (self.consts if name in KEPT else self.tables)[:, AT[name] + a:AT[name] + b]


def allocate(nc, ctx, phase):
    def sb(name, shape, dt=F32):
        return ctx.enter_context(nc.sbuf_tensor(f"{phase}_{name}", shape, dt))

    def ps(name, shape):
        return ctx.enter_context(nc.psum_tensor(f"{phase}_{name}", shape, F32))

    def sem(name):
        return ctx.enter_context(nc.semaphore(f"{phase}_{name}"))

    return sb, ps, sem


def carry(e, idle):
    e.sem_inc(idle, 1)


def f32(ap):
    return ap.bitcast(F32)


def phase_condition(nc, s):
    with ExitStack() as ctx:
        sb, ps, sem = allocate(nc, ctx, "condition")
        rows = sb("rows", [56, P])
        w_ada = sb("w_ada_in", [P, 2, KD, 512])
        xt = sb("xt", [P, 3, D])
        h32 = sb("h32", [P, KD, NTOK])
        mod_row = sb("mod_row", [2, 4, 512])
        mod_col = sb("mod_col", [P, 16, 2])
        gain = sb("gain", [P, KD, 2])
        squares = sb("squares", [P, D])
        mean_sq = sb("mean_sq", [P, NT])
        rstd = sb("rstd", [P, NT])
        lbx = sb("lbx", [P, 3, HEADS])
        ps_col = ps("ps_col", [P, 512])
        ps_ada = [ps(f"ps_ada{n}", [P, 512]) for n in range(2)]
        ps_x = [ps(f"ps_x{n}", [P, 4, P]) for n in range(4)]
        ps_mod = ps("ps_mod", [P, 512])
        const_in, rows_in = sem("const_in"), sem("rows_in")
        x_in = [sem(f"x_in{n}") for n in range(3)]
        w_in = [sem(f"w_in{n}") for n in range(2)]
        c_silu, cols_t, cols_done = sem("c_silu"), sem("cols_t"), sem("cols_done")
        ms_done, rstd_done, xn_done, xt_done = sem("ms_done"), sem("rstd_done"), sem("xn_done"), sem("xt_done")
        xlow, xhigh = sem("xlow_copied"), sem("xhigh_copied")
        ada_done, ada_copied, mod_t, mod_added, gain_done = (sem("ada_done"), sem("ada_copied"), sem("mod_t"),
                                                             sem("mod_added"), sem("gain_done"))
        h_done, hi_done, lb_exp, lb_step = sem("h_done"), sem("hi_done"), sem("lb_exp"), sem("lb_step")
        root_done, eps_set, fetched = sem("root_done"), sem("eps_set"), sem("fetched")
        block = ctx.enter_context(nc.Block())
        ident = s.const("ident")
        a = s.args

        @block.sync
        def _(sp):
            sp.dma_start(ident, a["consts"][:, AT["ident"]:AT["ident"] + P]).then_inc(const_in, 16)
            split = [(0, 8, a["c_prompt"][0]), (8, 16, a["c_sample"][0]), (16, 32, a["b_ada"][0, 0:2 * D]),
                     (32, 40, a["norm1_g"][0]), (40, 44, a["hgrn_lb_logits"][0]),
                     (44, 48, a["hgrn_lb_logits"][1]), (48, 52, a["ret_norm_g"][0]),
                     (52, 56, a["hgrn_norm_g"][0])]
            for lo, hi, src in split:
                sp.dma_start(rows[lo:hi, :], src.rearrange("(k p) -> k p", p=P)).then_inc(rows_in, 16)
            w_view = a["W_ada"][0].rearrange("(k p) n -> p k n", p=P)
            for i in range(NT):
                if i % 2 == 0 and i < 8:
                    b = i // 2
                    if b >= 2:
                        sp.wait_ge(ada_done, b - 1)
                    sp.dma_start(w_ada[:, b % 2], w_view[:, :, b * 512:(b + 1) * 512]).then_inc(w_in[b % 2], 16)
                if i >= 3:
                    sp.wait_ge(xt_done, i - 2)
                src = a["x_prompt"][0, i * P:(i + 1) * P, :] if i < NP_T else a["x_sample"][0]
                sp.dma_start(xt[0:width(i), i % 3, :], src).then_inc(x_in[i % 3], 16)
            sp.dma_start(s.consts[:, P:], a["consts"][:, P:N_KEPT]).then_inc(fetched, 16)
            sp.dma_start(s.tables[:, :], a["consts"][:, N_KEPT:]).then_inc(fetched, 16)
            for u in range(4):
                sp.dma_start(s.raw[:, u].rearrange("p (k n) -> p k n", k=KD), a["W_in"][0]
                             .rearrange("(k p) n -> p k n", p=P)[:, :, UNIT_AT[u]:UNIT_AT[u] + P]).then_inc(fetched, 16)
            sp.wait_ge(fetched, 96)

        def copy_low(act, i):
            w = width(i)
            act.wait_ge(xt_done, i + 1)
            act.activation(h32[:, 0:4, i * P:i * P + w], ps_x[2 * (i % 2)][:, :, 0:w], ACT.Copy).then_inc(xlow, 1)

        @block.scalar
        def _(act):
            act.wait_ge(eps_set, 1)
            act.wait_ge(rows_in, 128)
            act.activation(rows[0:16, :], rows[0:16, :], ACT.Silu).then_inc(c_silu, 1)
            act.wait_ge(lb_step, 2)
            act.activation(lbx[:, 0:2, :], lbx[:, 0:2, :], ACT.Exp).then_inc(lb_exp, 1)
            for i in range(NT):
                w = width(i)
                act.wait_ge(x_in[i % 3], 16 * (i // 3 + 1))
                if i:
                    act.wait_ge(ms_done, i)
                act.activation(squares[0:w, :], xt[0:w, i % 3, :], ACT.Square, scale=1.0 / 32.0,
                               accum_out=mean_sq[0:w, i:i + 1]).then_inc(ms_done, 1)
                act.wait_ge(ms_done, i + 1)
                act.activation(rstd[0:w, i:i + 1], mean_sq[0:w, i:i + 1], ACT.Sqrt, bias=s.eps[0:w, :])\
                   .then_inc(root_done, 1)
                if i:
                    copy_low(act, i - 1)
            copy_low(act, NT - 1)
            for k in range(KD):
                act.wait_ge(h_done, k + 1)
                act.activation(s.h_hi[:, k, :], h32[:, k, :], ACT.Copy).then_inc(hi_done, 1)

        @block.tensor
        def _(pe):
            pe.wait_ge(const_in, 16)
            pe.wait_ge(c_silu, 1)
            pe.transpose(ps_col[:, 0:56], rows[:, :], ident[0:56, 0:56]).then_inc(cols_t, 1)
            pe.wait_ge(cols_done, 1)
            for i in range(NT):
                w = width(i)
                if i % 2 == 0 and i < 8:
                    b = i // 2
                    pe.wait_ge(w_in[b % 2], 16 * (b // 2 + 1))
                    if b >= 2:
                        pe.wait_ge(ada_copied, b - 1)
                    for k in range(KD):
                        last = pe.matmul(ps_ada[b % 2][0:2, :], s.cT[:, k, :], w_ada[:, b % 2, k, :],
                                         start=(k == 0), stop=(k == KD - 1))
                    last.then_inc(ada_done, 1)
                if i == 7:
                    pe.wait_ge(ada_copied, 4)
                    for j in range(16):
                        last = pe.transpose(ps_mod[:, 2 * j:2 * j + 2],
                                            mod_row[:, j // 4, (j % 4) * P:(j % 4 + 1) * P], ident[0:2, 0:2])
                    last.then_inc(mod_t, 1)
                pe.wait_ge(xn_done, i + 1)
                if i >= 2:
                    pe.wait_ge(xlow, i - 1)
                    pe.wait_ge(xhigh, i - 1)
                for k in range(KD):
                    last = pe.transpose(ps_x[2 * (i % 2) + k // 4][:, k % 4, 0:w],
                                        xt[0:w, i % 3, k * P:(k + 1) * P], ident[0:w, 0:w])
                last.then_inc(xt_done, 1)

        @block.vector
        def _(dve):
            dve.memset(s.eps[:, :], EPS).then_inc(eps_set, 1)
            dve.wait_ge(cols_t, 1)
            dve.tensor_copy(s.cT[:, :, :], ps_col[:, 0:16].rearrange("p (s k) -> p k s", s=2)).then_inc(cols_done, 1)
            dve.tensor_copy(s.cols[:, :], ps_col[:, 16:56]).then_inc(cols_done, 1)

            dve.wait_ge(cols_done, 2)
            logits = s.cols[:, 24:32].rearrange("p (l h) -> p l h", l=2)
            dve.tensor_tensor(lbx[:, 2, :], logits[:, 0, :], logits[:, 1, :], ALU.max).then_inc(lb_step, 1)
            dve.wait_ge(lb_step, 1)
            dve.tensor_tensor(lbx[:, 0:2, :], logits, lbx[:, 2:3, :].broadcast_to([P, 2, HEADS]),
                              ALU.subtract).then_inc(lb_step, 1)
            dve.wait_ge(lb_exp, 1)
            dve.tensor_tensor(lbx[:, 2, :], lbx[:, 0, :], lbx[:, 1, :], ALU.add).then_inc(lb_step, 1)
            dve.wait_ge(lb_step, 3)
            dve.reciprocal(lbx[:, 2, :], lbx[:, 2, :]).then_inc(lb_step, 1)
            dve.wait_ge(lb_step, 4)
            dve.tensor_tensor(s.bound[:, 0, :], lbx[:, 0, :], lbx[:, 2, :], ALU.mult).then_inc(lb_step, 1)
            dve.wait_ge(lb_step, 5)
            dve.tensor_scalar(s.bound[:, 1, :], s.bound[:, 0, :], -1.0, 1.0, ALU.mult, ALU.add)

            def turn(i):
                w = width(i)
                dve.wait_ge(root_done, i + 1)
                dve.reciprocal(rstd[0:w, i:i + 1], rstd[0:w, i:i + 1]).then_inc(rstd_done, 1)
                dve.wait_ge(rstd_done, i + 1)
                dve.tensor_scalar(xt[0:w, i % 3, :], xt[0:w, i % 3, :], rstd[0:w, i:i + 1], None,
                                  ALU.mult).then_inc(xn_done, 1)

            def copy_high(i):
                w = width(i)
                dve.wait_ge(xt_done, i + 1)
                dve.tensor_copy(h32[:, 4:8, i * P:i * P + w], ps_x[2 * (i % 2) + 1][:, :, 0:w]).then_inc(xhigh, 1)

            for i in range(NT):
                turn(i)
                if i:
                    copy_high(i - 1)
                if i % 2 == 0 and i < 8:
                    b = i // 2
                    dve.wait_ge(ada_done, b + 1)
                    dve.tensor_copy(mod_row[:, b, :], ps_ada[b % 2][0:2, :]).then_inc(ada_copied, 1)
            copy_high(NT - 1)
            dve.wait_ge(mod_t, 1)
            dve.tensor_tensor(mod_col[:, :, :], ps_mod[:, 0:32].rearrange("p (j s) -> p j s", s=2),
                              s.cols[:, 0:16].unsqueeze(2).broadcast_to([P, 16, 2]), ALU.add).then_inc(mod_added, 1)
            dve.wait_ge(mod_added, 1)
            dve.scalar_tensor_tensor(out=gain[:, :, :], in0=mod_col[:, 8:16, :], scalar=1.0,
                                     in1=s.cols[:, 16:24].unsqueeze(2).broadcast_to([P, KD, 2]),
                                     op0=ALU.add, op1=ALU.mult).then_inc(gain_done, 1)
            dve.wait_ge(gain_done, 1)
            dve.wait_ge(xlow, NT)
            dve.wait_ge(xhigh, NT)
            for k in range(KD):
                dve.tensor_scalar(h32[:, k, 0:SEQ], h32[:, k, 0:SEQ], gain[:, k, 0:1], mod_col[:, k, 0:1],
                                  ALU.mult, ALU.add)
                dve.tensor_scalar(h32[:, k, SEQ:NTOK], h32[:, k, SEQ:NTOK], gain[:, k, 1:2],
                                  mod_col[:, k, 1:2], ALU.mult, ALU.add).then_inc(h_done, 1)
                if k % 2:
                    dve.wait_ge(hi_done, k)
                    dve.tensor_tensor(s.h_lo[:, k - 1, :], h32[:, k - 1, :], f32(s.h_hi[:, k - 1, :]), ALU.subtract)

        @block.gpsimd
        def _(pool):
            for k in range(1, KD, 2):
                pool.wait_ge(hi_done, k + 1)
                pool.tensor_tensor(s.h_lo[:, k, :], h32[:, k, :], f32(s.h_hi[:, k, :]), ALU.subtract)


def phase_mixers(nc, s):
    R = HEADS
    with ExitStack() as ctx:
        sb, ps, sem = allocate(nc, ctx, "mixers")
        raw = s.raw.rearrange("p u (k n) -> p u k n", k=KD)
        w_hi = sb("w_hi", [P, KD, 4, P], F32R)
        w_lo = sb("w_lo", [P, KD, 4, P], F32R)
        log_f = sb("log_f", [P, NTOK])
        hk = sb("hk", [P, NTOK])
        hq = sb("hq", [P, NTOK])
        gate = sb("gate", [P, 2, NTOK])
        ones = s.const("ones")
        decay = sb("decay", [P, 9, P])
        q_lv = sb("q_lv", [P, 7, P])
        k_lv = sb("k_lv", [P, 8, P])
        q_in = sb("q_in", [P, 2, P])
        last_f = sb("last_f", [P, 2])
        qk_cos = sb("qk_cos", [P, 4, 64])
        qk_sin = sb("qk_sin", [P, 4, 64])
        rot = sb("rot", [P, 2, 2, 64])
        k_dec = sb("k_dec", [P, 2, P])
        kd_col = sb("kd_col", [P, 2])
        qkv = sb("qkv", [P, 2, 512])
        turned = sb("turned", [P, 3, P])
        q_t, k_t, hk_dec = (turned[:, c, :] for c in range(3))
        qd_t = sb("qd_t", [P, P])
        a_ret = sb("a_ret", [P, P])
        a_hg = sb("a_hg", [P, 2, P])
        masked = sb("masked", [P, SMALL + 1, 32])
        squares = sb("squares", [P, 2, P])
        mean_sq = sb("mean_sq", [P, 2, 2])
        norm = sb("norm", [P, 2, 4, 2])
        normed = sb("normed", [P, 2, P])
        o_out = sb("o_out", [P, 2, 2, P])
        s_pr = sb("s_prompt", [P, 2, P])
        s_sa = sb("s_sample", [P, 2, P])
        ada_bias = sb("ada_bias", [2, D])
        ada_row = sb("ada_row", [2, D])
        ps_p = [ps(f"ps_proj{n}", [P, 512]) for n in range(2)]
        ps_tr = ps("ps_tr", [P, 4, P])
        ps_a = ps("ps_a", [P, 512])
        ps_lv = ps("ps_lv", [P, 512])
        ps_o = ps("ps_o", [P, 4, P])
        ps_s = ps("ps_s", [P, 4, P])
        ps_ot = ps("ps_ot", [P, 4, P])
        wide = ps_lv[:, 256:384]
        lv = ps_lv[:, 0:(SMALL + 1) * 32].rearrange("p (s l) -> p s l", l=32)

        raw_in = [sem(f"raw_in{n}") for n in range(4)]
        hi_done, lo_done, t_done, t_read = sem("hi_done"), sem("lo_done"), sem("t_done"), sem("t_read")
        proj_done, ada_done, ada_read = sem("proj_done"), sem("ada_done"), sem("ada_read")
        bias_in, ada_out = sem("bias_in"), sem("ada_out")
        f_done, logf_done, hk_done = sem("f_done"), sem("logf_done"), sem("hk_done")
        roped, rot_done, v_done, kdec_done = sem("roped"), sem("rot_done"), sem("v_done"), sem("kdec_done")
        tr_done, qkt_done, qd_done = sem("tr_done"), sem("qkt_done"), sem("qd_done")
        cum_done, diff_done, abs_done, exp_done = sem("cum_done"), sem("diff_done"), sem("abs_done"), sem("exp_done")
        ql_done, kl_done = sem("ql_done"), sem("kl_done")
        lv_done, ra_done, masked_done, ah_done, ahc_done, ar_done = (
            sem("lv_done"), sem("ra_done"), sem("masked_done"), sem("ah_done"), sem("ahc_done"), sem("ar_done"))
        o_done, s_done, ms_done, seed_log, seed_done, norm_step, normed_done = (
            sem("o_done"), sem("s_done"), sem("ms_done"), sem("seed_log"), sem("seed_done"), sem("norm_step"),
            sem("normed_done"))
        kd_copied, ot_done, out_done = sem("kd_copied"), sem("ot_done"), sem("out_done")
        o_stored = [sem(f"o_stored{n}") for n in range(2)]
        sp_stored, ss_stored, ss_in = sem("sp_stored"), sem("ss_stored"), sem("ss_in")
        cleared, idle, fetched = sem("cleared"), sem("idle"), sem("fetched")
        primed = [*raw_in, hi_done, lo_done, t_done, t_read, proj_done, ada_done, ada_read, bias_in, ada_out,
                  f_done, logf_done, hk_done, roped, rot_done, v_done, kdec_done, tr_done, qkt_done, qd_done,
                  cum_done, diff_done, abs_done, exp_done, ql_done, kl_done, lv_done, ra_done, masked_done,
                  ah_done, ahc_done, ar_done, o_done, s_done, ms_done, seed_log, seed_done, norm_step,
                  normed_done, kd_copied, ot_done, out_done, *o_stored, sp_stored, ss_stored, ss_in]
        block = ctx.enter_context(nc.Block())
        a = s.args
        ident = s.const("ident")
        pieces = [slice(n * PIECE, (n + 1) * PIECE) for n in range(3)]

        def counts(e, g):
            n = {m: e.snap(g * m + PRIMED) for m in (1, 2, 8, 9, 12, 16, 32, 36, 64, 80)}
            n["round"] = e.snap(g * 1)
            return n

        @block.sync
        def _(sp):
            w_in = a["W_in"][0].rearrange("(k p) n -> p k n", p=P)
            w_ada = a["W_ada"][0].rearrange("(k p) n -> p k n", p=P)
            def load(g, u):
                if u < 8:
                    at = nc.s_assert_within(sp.snap(g * P + UNIT_AT[u]), 0, D_IN - P,
                                            skip_runtime_bounds_check_because="a round is at most the last")
                    src = w_in[:, :, bass.ds(at, P)]
                else:
                    at = sp.snap(g * D + (2 * D + (u - 8) * P))
                    src = w_ada[:, :, bass.ds(at, P)]
                if u < 4:
                    sp.wait_ge(ada_done, sp.snap(g * 8 + (u - 3 + PRIMED)))
                elif u < 12:
                    sp.wait_ge(lo_done, sp.snap(g * 8 + (u - 3 + PRIMED)))
                else:
                    sp.wait_ge(ada_done, sp.snap(g * 8 + (u - 11 + PRIMED)))
                carry(sp, idle)
                sp.dma_start(raw[:, u % 4], src).then_inc(raw_in[u % 4], 16)
                if u == 8:
                    head = sp.snap(g * 1)
                    sp.wait_ge(ss_stored, sp.snap(g * 32 + PRIMED))
                    carry(sp, idle)
                    for n, name in enumerate(("state_ret", "state_hgrn")):
                        sp.dma_start(s_sa[:, n:n + 1, :],
                                     a[name][0, 0, bass.ds(head, 1)].rearrange("h k v -> k h v"))\
                          .then_inc(ss_in, 16)
                    at = sp.snap(g * D + 2 * D)
                    sp.wait_ge(ada_read, sp.snap(g * 1 + PRIMED))
                    carry(sp, idle)
                    sp.dma_start(ada_bias[:, :], a["b_ada"][0:1, bass.ds(at, D)].broadcast_to([2, D]))\
                      .then_inc(bias_in, 16)

            for u in range(4):
                sp.sem_inc(raw_in[u], 16)
            with sp.Fori(0, R) as g:
                for u in range(4, 16):
                    load(g, u)
                with sp.If(g < R - 1):
                    for u in range(4):
                        load(g + 1, u)
            for k in range(6):
                if k == 2:
                    sp.wait_ge(ada_done, 8 * R + PRIMED)
                sp.dma_start(s.raw[:, W_OUT_AT[k]], a["W_out"][0, k * P:(k + 1) * P, :]).then_inc(fetched, 16)
            sp.wait_ge(fetched, 16 * 6)

        @block.gpsimd
        def _(pool):
            for semaphore in primed:
                pool.sem_inc(semaphore, PRIMED)
            pool.memset(a_hg[:, :, :], 0.0).then_inc(cleared, 1)
            with pool.Fori(0, R) as g:
                n = counts(pool, g)

                def keys(i):
                    w = width(i)
                    pool.wait_ge(exp_done, n[9] + (i + 1))
                    pool.wait_ge(lv_done, n[9] + i)
                    if i == 0:
                        pool.wait_ge(hk_done, n[1] + 1)
                    kb = hk[:, i * P:i * P + w]
                    for c, (lo, hi) in enumerate([(0, 8)] if w == P else [(0, 1), (3, 8)]):
                        last = pool.tensor_tensor(k_lv[:, lo:hi, 0:w], decay[:, lo:hi, 0:w],
                                                  kb.unsqueeze(1).broadcast_to([P, hi - lo, w]), ALU.mult)
                    last.then_inc(kl_done, 1)

                def refine(i):
                    w = width(i)
                    b = i % 2
                    step = lambda m: n[36] + (4 * i + m)
                    m, y = mean_sq[0:w, b, :], norm[0:w, b, 0, :]
                    t = [norm[0:w, b, c, :] for c in range(4)]
                    pool.wait_ge(seed_done, n[9] + (i + 1))
                    pool.tensor_tensor(t[1], y, y, ALU.mult).then_inc(norm_step, 1)
                    pool.wait_ge(norm_step, step(1))
                    pool.tensor_tensor(t[2], t[1], m, ALU.mult).then_inc(norm_step, 1)
                    pool.wait_ge(norm_step, step(2))
                    carry(pool, idle)
                    pool.tensor_scalar(t[1], t[2], -0.5, 1.5, ALU.mult, ALU.add).then_inc(norm_step, 1)
                    pool.wait_ge(norm_step, step(3))
                    pool.tensor_tensor(t[3], y, t[1], ALU.mult).then_inc(norm_step, 1)

                for i in range(NT + 2):
                    if i >= 2:
                        refine(i - 2)
                    if i < NT:
                        keys(i)

        @block.scalar
        def _(act):
            def split(u, raws, before):
                act.wait_ge(raw_in[u % 4], raws + 16 * (u // 4 + 1))
                if before is not None:
                    act.wait_ge(*before)
                act.activation(w_hi[:, :, u % 4, :], raw[:, u % 4], ACT.Copy).then_inc(hi_done, 1)

            for u in range(2):
                split(u, PRIMED, None)
            with act.Fori(0, R) as g:
                n = counts(act, g)

                def split_here(u):
                    split(u, n[64], (proj_done, n[9]) if u < 4 else (t_done, n[12] + 3 * (u - 3)))

                def split_next(units):
                    with act.If(g < R - 1):
                        for u in units:
                            split(u, n[64] + 64, (proj_done, n[9] + 9))


                def read_block(j, some=range(3)):
                    for c in some:
                        at, src = pieces[c], ps_p[(3 * j + c) % 2][:, 0:PIECE]
                        act.wait_ge(t_done, n[12] + (3 * j + c + 1))
                        if j == 0:
                            if c == 0:
                                act.wait_ge(out_done, n[9])
                            act.activation(log_f[:, at], src, ACT.Sigmoid)
                            last = act.activation(hk[:, at], src, ACT.Sigmoid, scale=-1.0)
                        elif j < 3:
                            last = act.activation(gate[:, j - 1, at], src, ACT.Silu)
                        else:
                            last = act.activation(hq[:, at], src, ACT.Copy, scale=SCALE)
                        last.then_inc(t_read, 1)

                def decays(i):
                    w = width(i)
                    act.wait_ge(diff_done, n[9] + (i + 1))
                    parts = [(0, 9)] if w == P else [(0, 1), (3, 9)]
                    for lo, hi in parts:
                        last = act.activation(decay[:, lo:hi, 0:w], decay[:, lo:hi, 0:w], ACT.Abs)
                    last.then_inc(abs_done, 1)
                    act.wait_ge(abs_done, n[9] + (i + 1))
                    for lo, hi in parts:
                        last = act.activation(decay[:, lo:hi, 0:w], decay[:, lo:hi, 0:w], ACT.Exp, scale=-1.0)
                    last.then_inc(exp_done, 1)

                read_block(0)
                split_here(2)
                read_block(1)
                split_here(3)
                split_here(4)
                read_block(2)
                split_here(5)
                act.preload_act_table_set("natural_log_exp_and_others")
                act.wait_ge(f_done, n[1] + 1)
                act.activation(log_f[:, :], log_f[:, :], ACT.Ln).then_inc(logf_done, 1)
                read_block(3, range(1))
                decays(0)
                read_block(3, range(1, 2))
                split_here(6)
                split_here(7)
                read_block(3, range(2, 3))

                def squares_of(i):
                    w, b = width(i), i % 2
                    act.wait_ge(o_done, n[9] + (i + 1))
                    for c in range(2):
                        last = act.activation(squares[0:w, c, :], ps_o[0:w, c, :], ACT.Square,
                                              scale=float(P) ** -0.5, accum_out=mean_sq[0:w, b, c:c + 1])
                    last.then_inc(ms_done, 1)
                    act.wait_ge(ms_done, n[9] + (i + 1))
                    act.activation(norm[0:w, b, 1, :], mean_sq[0:w, b, :], ACT.Ln, bias=s.eps[0:w, :])\
                       .then_inc(seed_log, 1)
                    act.wait_ge(seed_log, n[9] + (i + 1))
                    act.activation(norm[0:w, b, 0, :], norm[0:w, b, 1, :], ACT.Exp, scale=-0.5)
                    act.activation(mean_sq[0:w, b, :], mean_sq[0:w, b, :], ACT.Identity, bias=s.eps[0:w, :])\
                       .then_inc(seed_done, 1)

                def normalise(i):
                    w, b = width(i), i % 2
                    act.wait_ge(norm_step, n[36] + 4 * (i + 1))
                    act.wait_ge(ot_done, n[9] + i)
                    for c in range(2):
                        last = act.activation(normed[0:w, c, :], ps_o[0:w, c, :], ACT.Copy,
                                              scale=norm[0:w, b, 3, c:c + 1])
                    last.then_inc(normed_done, 1)

                def copies(i):
                    w = width(i)
                    act.wait_ge(tr_done, n[9] + (i + 1))
                    if w == P:
                        act.activation(turned[:, :, :], ps_tr[:, 0:3, :], ACT.Copy).then_inc(qkt_done, 1)
                    else:
                        act.activation(turned[:, 0:2, 0:w], ps_tr[:, 0:2, 0:w], ACT.Copy)
                        act.activation(turned[0:w, 2, :], ps_tr[0:w, 2, :], ACT.Copy).then_inc(qkt_done, 1)

                def wide_levels(i):
                    w, b = width(i), i % 2
                    if w == P:
                        act.wait_ge(masked_done, n[9] + (i + 1))
                        act.activation(a_hg[0:64, b, 64:128], wide[0:64, 64:128], ACT.Copy)
                        act.activation(a_hg[0:32, b, 32:64], wide[0:32, 32:64], ACT.Copy)
                        act.activation(a_hg[64:96, b, 96:128], wide[64:96, 96:128], ACT.Copy)\
                           .then_inc(ahc_done, 1)

                def values(i):
                    w, b = width(i), i % 2
                    act.wait_ge(proj_done, n[9] + (i + 1))
                    if i >= 2:
                        act.wait_ge(roped, n[9] + (i - 1))
                    act.activation(qkv[0:w, b, :], ps_p[b][0:w, :], ACT.Copy).then_inc(v_done, 1)
                    act.wait_ge(rot_done, n[9] + (i + 1))
                    act.wait_ge(kd_copied, n[1] + 1)
                    act.activation(k_dec[0:w, b, :], rot[0:w, 1].rearrange("p a d -> p (a d)"), ACT.Copy,
                                   scale=kd_col[0:w, 0:1] if w == P else kd_col[0:w, 1:2]).then_inc(kdec_done, 1)

                def store_states(which, i, stored):
                    act.wait_ge(s_done, n[9] + (i + 1))
                    buf = s_pr if which == "prompt" else s_sa
                    for c, name in enumerate(("ret", "hgrn")):
                        act.dma_start(s.outs[f"state_{name}_{which}"][0, 0, bass.ds(n["round"], 1)]
                                      .rearrange("h k v -> k h v"), buf[:, c:c + 1, :]).then_inc(stored, 16)

                for i in range(NT + 2):
                    if i >= 2:
                        squares_of(i - 2)
                    if i >= 2:
                        normalise(i - 2)
                    if 1 <= i <= NT:
                        copies(i - 1)
                    if 1 <= i < NT:
                        decays(i)
                    if 1 <= i <= NT:
                        wide_levels(i - 1)
                    if i < NT:
                        values(i)
                    if i == NT:
                        split_next((0,))
                    if i == NT + 1:
                        split_next((1,))
                    if i >= 2:
                        t = i - 2
                        w = width(t)
                        act.wait_ge(out_done, n[9] + (t + 1))
                        dst = s.o_scr.rearrange("(c g p) t -> g p c t", c=2, g=HEADS)
                        dst = dst[bass.ds(n["round"], 1), :, :, t * P:t * P + w]
                        act.dma_start(dst.rearrange("g p c t -> (g p) c t"), o_out[:, t % 2, :, 0:w])\
                           .then_inc(o_stored[t % 2], 16)
                    if i == NT:
                        store_states("prompt", NP_T - 1, sp_stored)
                    if i == NT + 1:
                        store_states("sample", NT - 1, ss_stored)
                        act.wait_ge(ada_read, n[1] + 1)
                        act.dma_start(s.mod_scr[:, bass.ds(act.snap(g * D), D)], ada_row[:, :]).then_inc(ada_out, 16)
            act.wait_ge(o_stored[0], 16 * 5 * R + PRIMED)
            act.wait_ge(o_stored[1], 16 * 4 * R + PRIMED)
            act.wait_ge(sp_stored, 32 * R + PRIMED)
            act.wait_ge(ss_stored, 32 * R + PRIMED)
            act.wait_ge(ada_out, 16 * R + PRIMED)

        @block.tensor
        def _(pe):
            def turned_piece(j, c, units, bank):
                if c == 0:
                    pe.wait_ge(lo_done, units)
                if bank is not None:
                    pe.wait_ge(*bank)
                at = pieces[c]
                for k in range(KD):
                    whi, wlo = w_hi[:, k, j, :], w_lo[:, k, j, :]
                    xhi, xlo = s.h_hi[:, k, at], s.h_lo[:, k, at]
                    out = ps_p[(3 * j + c) % 2][:, 0:PIECE]
                    pe.matmul(out, whi, xhi, start=(k == 0), stop=False)
                    pe.matmul(out, whi, xlo, start=False, stop=False)
                    last = pe.matmul(out, wlo, xhi, start=False, stop=(k == KD - 1))
                last.then_inc(t_done, 1)

            pe.wait_ge(cleared, 1)
            turned_piece(0, 0, PRIMED + 1, None)
            with pe.Fori(0, R) as g:
                n = counts(pe, g)

                def project(i, half):
                    w = width(i)
                    out = ps_p[i % 2][0:w, :]
                    if half == 0:
                        if i == 0:
                            pe.wait_ge(lo_done, n[8] + 8)
                            pe.wait_ge(t_read, n[12] + 11)
                        elif i == 1:
                            pe.wait_ge(t_read, n[12] + 12)
                        elif i >= 2:
                            pe.wait_ge(v_done, n[9] + (i - 1))
                    for k in range(4 * half, 4 * half + 4):
                        xhi, xlo = s.h_hi[:, k, i * P:i * P + w], s.h_lo[:, k, i * P:i * P + w]
                        whi = w_hi[:, k].rearrange("p u n -> p (u n)")
                        wlo = w_lo[:, k].rearrange("p u n -> p (u n)")
                        pe.matmul(out, xhi, whi, start=(k == 0), stop=False)
                        pe.matmul(out, xhi, wlo, start=False, stop=False)
                        last = pe.matmul(out, xlo, whi, start=False, stop=(k == KD - 1))
                    if half:
                        last.then_inc(proj_done, 1)

                def scores(i):
                    w = width(i)
                    pe.wait_ge(rot_done, n[9] + (i + 1))
                    pe.wait_ge(qkt_done, n[9] + i)
                    pe.wait_ge(kl_done, n[9] + (i + 1))
                    if w < P:
                        carry(pe, idle)
                    for c in range(2):
                        pe.transpose(ps_tr[:, c, 0:w], rot[0:w, c].rearrange("p a d -> p (a d)"), ident[0:w, 0:w])
                    pe.transpose(ps_tr[0:w, 2, :], k_lv[:, 0, 0:w], ident).then_inc(tr_done, 1)
                    pe.wait_ge(ql_done, n[9] + (i + 1))
                    pe.wait_ge(ah_done, n[9] + i)
                    pe.wait_ge(ahc_done, n[8] + min(i, 8))
                    if w < P:
                        carry(pe, idle)
                    if w == P:
                        pe.matmul(wide[0:64, 64:128], k_lv[:, 1, 0:64], q_lv[:, 0, 64:128], start=True, stop=True)
                        for lo in (0, 64):
                            pe.matmul(wide[lo:lo + 32, lo + 32:lo + 64], k_lv[:, 2, lo:lo + 32],
                                      q_lv[:, 1, lo + 32:lo + 64], start=True, stop=True)
                    for j in range(w // 32):
                        at = slice(32 * j, 32 * j + 32)
                        for c in range(SMALL):
                            pe.matmul(lv[at, c, :], k_lv[:, 3 + c, at], q_lv[:, 2 + c, at], start=True, stop=True)
                        tok = slice(i * P + 32 * j, i * P + 32 * j + 32)
                        last = pe.matmul(lv[at, SMALL, :], hk[:, tok], hq[:, tok], start=True, stop=True)
                    last.then_inc(lv_done, 1)

                def retention_scores(i):
                    w = width(i)
                    pe.wait_ge(qkt_done, n[9] + (i + 1))
                    pe.wait_ge(ar_done, n[9] + i)
                    if w < P:
                        carry(pe, idle)
                    pe.matmul(ps_a[0:w, 0:w], k_t[:, 0:w], q_t[:, 0:w], start=True, stop=True).then_inc(ra_done, 1)

                def mix(i):
                    w, b = width(i), i % 2
                    st = s_pr if i < NP_T else s_sa
                    pe.wait_ge(v_done, n[9] + (i + 1))
                    pe.wait_ge(kdec_done, n[9] + (i + 1))
                    pe.wait_ge(qd_done, n[9] + (i + 1))
                    pe.wait_ge(normed_done, n[9] + i)
                    pe.wait_ge(s_done, n[9] + i)
                    pe.wait_ge(ar_done, n[9] + (i + 1))
                    if i == NP_T:
                        pe.wait_ge(ss_in, n[32] + 32)
                    if w < P:
                        carry(pe, idle)
                    pe.matmul(ps_o[0:w, 0, :], a_ret[0:w, 0:w], qkv[0:w, b, 256:384], start=True, stop=(i == 0))
                    if i:
                        pe.matmul(ps_o[0:w, 0, :], qd_t[:, 0:w], st[:, 0, :], start=False, stop=True)
                    pe.matmul(ps_s[:, 0, :], k_dec[0:w, b, :], qkv[0:w, b, 256:384], start=True, stop=True)
                    pe.matmul(ps_s[:, 1, :], hk_dec[0:w, :], qkv[0:w, b, 384:512], start=True, stop=True)
                    pe.wait_ge(ah_done, n[9] + (i + 1))
                    if w == P:
                        pe.wait_ge(ahc_done, n[8] + (i + 1))
                    else:
                        carry(pe, idle)
                    last = pe.matmul(ps_o[0:w, 1, :], a_hg[0:w, b, 0:w], qkv[0:w, b, 384:512], start=True,
                                     stop=(i == 0))
                    if i:
                        last = pe.matmul(ps_o[0:w, 1, :], q_in[:, b, 0:w], st[:, 1, :], start=False, stop=True)
                    last.then_inc(o_done, 1)

                def condition(v):
                    u = 8 + v
                    pe.wait_ge(out_done, n[9] + max(v - 1, 0))
                    pe.wait_ge(raw_in[u % 4], n[64] + 16 * (u // 4 + 1))
                    for k in range(KD):
                        last = pe.matmul(ps_ot[0:2, 2 + v % 2, :], s.cT[:, k, :], raw[:, u % 4, k, :],
                                         start=(k == 0), stop=(k == KD - 1))
                    last.then_inc(ada_done, 1)

                def turn_out(i):
                    w = width(i)
                    pe.wait_ge(out_done, n[9] + i)
                    pe.wait_ge(normed_done, n[9] + (i + 1))
                    if w < P:
                        carry(pe, idle)
                    for c in range(2):
                        last = pe.transpose(ps_ot[:, c, 0:w], normed[0:w, c, :], ident[0:w, 0:w])
                    last.then_inc(ot_done, 1)

                for p in range(1, 12):
                    turned_piece(p // 3, p % 3, n[8] + (p // 3 + 1),
                                 (t_read, n[12] + (p - 1)) if p >= 2 else (v_done, n[9]))
                for i in range(NT + 2):
                    if i < NT:
                        project(i, 0)
                    if 1 <= i <= 8:
                        condition(i - 1)
                    if 1 <= i <= NT:
                        scores(i - 1)
                    if i == NT + 1:
                        with pe.If(g < R - 1):
                            turned_piece(0, 0, n[8] + 9, (v_done, n[9] + 9))
                    if i >= 2:
                        turn_out(i - 2)
                    if 1 <= i <= NT:
                        retention_scores(i - 1)
                    if i < NT:
                        project(i, 1)
                    if 1 <= i <= NT:
                        mix(i - 1)

        @block.vector
        def _(dve):
            def split(u, units):
                dve.wait_ge(hi_done, units + (u + 1))
                dve.tensor_tensor(w_lo[:, :, u % 4, :], raw[:, u % 4], f32(w_hi[:, :, u % 4, :]),
                                  ALU.subtract).then_inc(lo_done, 1)

            for u in range(2):
                split(u, PRIMED)
            with dve.Fori(0, R) as g:
                n = counts(dve, g)

                def split_next(units):
                    with dve.If(g < R - 1):
                        for u in units:
                            split(u, n[8] + 8)

                bound_at = lambda c: s.bound[:, c, bass.ds(n["round"], 1)]

                dve.wait_ge(kdec_done, n[9])
                col = dve.snap(g * 2 + AT["k_decay"])
                dve.tensor_scalar(kd_col[:, :], s.tables[:, bass.ds(col, 2)], 1.0, None, ALU.mult)\
                   .then_inc(kd_copied, 1)
                def differences(i):
                    w = width(i)
                    if i == 0:
                        dve.wait_ge(logf_done, n[1] + 1)
                    dve.wait_ge(kl_done, n[9] + i)
                    dve.wait_ge(ql_done, n[9] + i)
                    b = decay[:, 8, 0:w]
                    dve.tensor_tensor_scan(b, ones[:, 0:w], log_f[:, i * P:i * P + w], 0.0, ALU.mult, ALU.add)\
                       .then_inc(cum_done, 1)
                    dve.wait_ge(cum_done, n[9] + (i + 1))
                    for c, h in enumerate(LEVELS):
                        if 2 * h > w:
                            continue
                        x = b.rearrange("p (n t) -> p n t", t=2 * h)
                        dve.tensor_tensor(decay[:, 1 + c, 0:w].rearrange("p (n t) -> p n t", t=2 * h), x,
                                          x[:, :, h - 1:h].broadcast_to([P, w // (2 * h), 2 * h]), ALU.subtract)
                    dve.tensor_scalar(decay[:, 0, 0:w], b, decay[:, 8, w - 1:w], None, ALU.subtract)\
                       .then_inc(diff_done, 1)

                def queries(i):
                    w, b = width(i), i % 2
                    dve.wait_ge(exp_done, n[9] + (i + 1))
                    dve.wait_ge(lv_done, n[9] + i)
                    dve.tensor_copy(last_f[:, b:b + 1], decay[:, 8, w - 1:w])
                    q = hq[:, i * P:i * P + w]
                    lo = 0 if w == P else 2
                    dve.tensor_tensor(q_in[:, b, 0:w], decay[:, 8, 0:w], q, ALU.mult)
                    dve.tensor_tensor(q_lv[:, lo:7, 0:w], decay[:, 1 + lo:8, 0:w],
                                      q.unsqueeze(1).broadcast_to([P, 7 - lo, w]), ALU.mult).then_inc(ql_done, 1)

                dve.wait_ge(t_read, n[12] + 3)
                dve.tensor_scalar(log_f[:, :], log_f[:, :], bound_at(1), bound_at(0), ALU.mult, ALU.add)\
                   .then_inc(f_done, 1)
                dve.tensor_scalar(hk[:, :], hk[:, :], bound_at(1), None, ALU.mult).then_inc(hk_done, 1)
                for u in range(2, 6):
                    split(u, n[8])
                differences(0)
                for u in range(6, 8):
                    split(u, n[8])

                def state(i):
                    w = width(i)
                    dve.wait_ge(o_done, n[9] + (i + 1))
                    dve.wait_ge(s_done, n[9] + i)
                    if i == 0:
                        dve.wait_ge(sp_stored, n[32])
                        dve.tensor_copy(s_pr[:, :, :], ps_s[:, 0:2, :]).then_inc(s_done, 1)
                        return
                    st = s_pr if i < NP_T else s_sa
                    if i == NP_T:
                        dve.wait_ge(ss_in, n[32] + 32)
                    col = dve.snap(g * 2 + (AT["s_decay"] + (0 if w == P else 1)))
                    dve.scalar_tensor_tensor(out=st[:, 0, :], in0=st[:, 0, :], scalar=s.tables[:, bass.ds(col, 1)],
                                             in1=ps_s[:, 0, :], op0=ALU.mult, op1=ALU.add)
                    dve.scalar_tensor_tensor(out=st[:, 1, :], in0=st[:, 1, :], scalar=last_f[:, i % 2:i % 2 + 1],
                                             in1=ps_s[:, 1, :], op0=ALU.mult, op1=ALU.add).then_inc(s_done, 1)

                def gated(i):
                    w, b = width(i), i % 2
                    dve.wait_ge(ot_done, n[9] + (i + 1))
                    use = i // 2
                    dve.wait_ge(o_stored[b], n[80 if b == 0 else 64] + 16 * use)
                    if i < 8:
                        if i == 0:
                            dve.wait_ge(bias_in, n[16] + 16)
                            dve.wait_ge(ada_out, n[16])
                        at = slice(i * P, (i + 1) * P)
                        last = dve.tensor_tensor(ada_row[:, at], ps_ot[0:2, 2 + i % 2, :], ada_bias[:, at], ALU.add)
                        if i == 7:
                            last.then_inc(ada_read, 1)
                    for c in range(2):
                        col = dve.snap(g * 1 + (32 + 4 * c))
                        last = dve.scalar_tensor_tensor(
                            out=o_out[:, b, c, 0:w], in0=ps_ot[:, c, 0:w], scalar=s.cols[:, bass.ds(col, 1)],
                            in1=gate[:, c, i * P:i * P + w], op0=ALU.mult, op1=ALU.mult)
                    last.then_inc(out_done, 1)

                def scored(i):
                    w, b = width(i), i % 2
                    dve.wait_ge(qkt_done, n[9] + (i + 1))
                    qd = dve.snap(g * P + AT["q_decay"])
                    dve.tensor_tensor(qd_t[:, 0:w], q_t[:, 0:w], s.tables[:, bass.ds(qd, w)], ALU.mult)\
                       .then_inc(qd_done, 1)
                    dve.wait_ge(lv_done, n[9] + (i + 1))
                    dve.wait_ge(ah_done, n[9] + i)
                    mask = s.const("level_mask")[0:w].rearrange("p (s l) -> p s l", l=32)
                    dve.tensor_tensor(masked[0:w], lv[0:w], mask, ALU.mult).then_inc(masked_done, 1)
                    dve.wait_ge(masked_done, n[9] + (i + 1))
                    for j in range(w // 32):
                        at = slice(32 * j, 32 * j + 32)
                        last = dve.tensor_reduce(a_hg[at, b, at], masked[at].rearrange("p s l -> p l s"), AX, ALU.add)
                    last.then_inc(ah_done, 1)
                    dve.wait_ge(ra_done, n[9] + (i + 1))
                    rd = dve.snap(g * P + AT["ret_decay"])
                    dve.tensor_tensor(a_ret[0:w, 0:w], ps_a[0:w, 0:w], s.tables[0:w, bass.ds(rd, w)], ALU.mult)\
                       .then_inc(ar_done, 1)

                def rotary(i):
                    w = width(i)
                    dve.wait_ge(v_done, n[9] + (i + 1))
                    dve.wait_ge(rot_done, n[9] + i)
                    qk = qkv[0:w, i % 2, 0:256].rearrange("p (c d) -> p c d", c=4)
                    for name, out in (("cos", qk_cos), ("sin", qk_sin)):
                        tab = s.tables[0:w, AT[name] + 64 * i:AT[name] + 64 * i + 64]
                        last = dve.tensor_tensor(out[0:w], qk, tab.unsqueeze(1).broadcast_to([w, 4, 64]), ALU.mult)
                    last.then_inc(roped, 1)
                    dve.wait_ge(roped, n[9] + (i + 1))
                    if i:
                        dve.wait_ge(kdec_done, n[9] + i)
                    pair = lambda t, half: t[0:w].rearrange("p (c a) d -> p c a d", a=2)[:, :, half, :]
                    dve.tensor_tensor(rot[0:w, :, 0, :], pair(qk_cos, 0), pair(qk_sin, 1), ALU.subtract)
                    dve.tensor_tensor(rot[0:w, :, 1, :], pair(qk_cos, 1), pair(qk_sin, 0), ALU.add)\
                       .then_inc(rot_done, 1)

                for i in range(NT + 2):
                    if i >= 2:
                        state(i - 2)
                    if 1 <= i < NT:
                        differences(i)
                    if 1 <= i <= NT:
                        scored(i - 1)
                    if i >= 2:
                        gated(i - 2)
                    if i < NT:
                        queries(i)
                        rotary(i)
                    if i == NT:
                        split_next((0,))
                split_next((1,))


def load_chunk(e, s, x, c, dst, arrived):
    if c < 8:
        half, rows = c // 4, slice((c % 4) * 256, (c % 4) * 256 + 256)
        for m, name in enumerate(("W_gate_e", "W_up_e")):
            src = s.args[name][0, bass.ds(x, 1), rows, half * 256:(half + 1) * 256]
            e.dma_start(dst.rearrange("p (k m n) -> p k m n", k=2, m=2)[:, :, m, :],
                        src.rearrange("e (k p) n -> p (e k) n", p=P)).then_inc(arrived, 16)
    else:
        rows = slice((c - 8) * P, (c - 7) * P)
        for m in range(2):
            at = slice(512 * m, 512 * m + 512)
            src = s.args["W_down_e"][0, bass.ds(x, 1), rows, at]
            e.dma_start(dst[:, at], src.rearrange("e p n -> p (e n)")).then_inc(arrived, 16)


def phase_output(nc, s):
    with ExitStack() as ctx:
        sb, ps, sem = allocate(nc, ctx, "output")
        raw = s.raw
        w_hi = sb("w_hi", [P, KD, D], F32R)
        w_lo = sb("w_lo", [P, KD, D], F32R)
        mod = [sb("mod", [P, 3, D]), raw[:, 3:6]]
        gain = sb("gain", [P, D])
        o_raw = sb("o_raw", [P, 2, KD, P])
        o_hi = sb("o_hi", [P, 2, KD, P], F32R)
        o_lo = sb("o_lo", [P, 2, KD, P], F32R)
        x_old = sb("x_old", [P, 2, D])
        h2 = sb("h2", [P, 2, D])
        h2_t = sb("h2_t", [P, KD, P])
        squares = sb("squares", [P, D])
        w_route = sb("w_route", [P, KD, N_GROUPS + NE])
        b_route = sb("b_route", [P, N_GROUPS + NE])
        mean_sq = sb("mean_sq", [P, NT])
        rstd = sb("rstd", [P, NT])
        newton = sb("newton", [P, 1])
        ps_o = [ps(f"ps_o{b}", [P, 2, 512]) for b in range(2)]
        ps_t = ps("ps_t", [P, KD, P])
        ps_l = ps("ps_l", [P, 512])
        ps_r = ps("ps_r", [P, 512])

        raw_in = [sem(f"raw_in{n}") for n in range(2)]
        o_in, x_in = [sem(f"o_in{n}") for n in range(2)], [sem(f"x_in{n}") for n in range(2)]
        rows_in, route_in = sem("rows_in"), sem("route_in")
        hi_done, lo_done, ohi_done, olo_done = sem("hi_done"), sem("lo_done"), sem("ohi_done"), sem("olo_done")
        gain_done, mm_done, gated, added, h_stored = (sem("gain_done"), sem("mm_done"), sem("gated"), sem("added"),
                                                      sem("h_stored"))
        log_done = sem("log_done")
        ms_done, root_done, rstd_step, scaled, h2_done = (sem("ms_done"), sem("root_done"), sem("rstd_step"),
                                                          sem("scaled"), sem("h2_done"))
        t_done, t_read, l_done, l_read = sem("t_done"), sem("t_read"), sem("l_done"), sem("l_read")
        cleared, list_clear, token_done = sem("cleared"), sem("list_clear"), sem("token_done")
        route, exp_done, both_done, counted = sem("route"), sem("exp_done"), sem("both_done"), sem("counted")
        less_max, slots_done, scattered, prefetched = (sem("less_max"), sem("slots_done"), sem("scattered"),
                                                       sem("prefetched"))
        no_token = sb("no_token", [P, NE * NT], I32)
        token = sb("token", [P, NT], I32)
        logits = sb("logits", [P, NT, N_GROUPS + NE])
        probs = sb("probs", [P, 2, 3, 4])
        eq4 = sb("eq4", [P, 3, 4])
        one_g = sb("one_group", [P, 3, 4])
        one_e = sb("one_expert", [P, 2, 3, 4])
        col = sb("col", [P, 3])
        group_w = sb("group_w", [P, 3])
        top = sb("top", [P, 2, 3])
        by_expert = sb("by_expert", [P, 3, NE])
        chosen = sb("chosen", [P, 2, NT, NE])
        both = sb("both", [P, NT, NE])
        before = sb("before", [P, NT + 1, NE])
        rank_of = sb("rank_of", [P, NT, NE])
        prod = sb("prod", [P, 2, 3, NE])
        rank = sb("rank", [P, 2, 3])
        past = sb("past", [P, 2, 3, 8])
        n_past = sb("n_past", [P, 2, 3])
        place = sb("place", [P, 2, 2, 3])
        entry = sb("entry", [P, 2, NT], I32)
        all_prod = sb("all_prod", [P, NT, NE])
        n_of = sb("n_of", [P, NE])
        first = sb("first", [P, NE + 1])
        over = sb("over", [P, NE, 8])
        extra = sb("extra", [P, NE])
        tiles = sb("tiles", [P, NE + 1])
        slot_f = sb("slot_f", [P, 2, NT])
        block = ctx.enter_context(nc.Block())
        a = s.args
        ident = s.const("ident")

        @block.sync
        def _(sp):
            def o_tile(i):
                w = width(i)
                if i >= 2:
                    sp.wait_ge(olo_done, i - 1)
                src = s.o_scr.rearrange("(k p) t -> p k t", p=P)[:, :, i * P:i * P + w]
                sp.dma_start(o_raw[:, i % 2, :, 0:w], src).then_inc(o_in[i % 2], 16)

            def x_tile(i):
                if i >= 2:
                    sp.wait_ge(added, i - 1)
                src = a["x_prompt"][0, i * P:(i + 1) * P, :] if i < NP_T else a["x_sample"][0]
                sp.dma_start(x_old[0:width(i), i % 2, :], src).then_inc(x_in[i % 2], 16)

            o_tile(0)
            for k in range(6, KD):
                sp.wait_ge(lo_done, k - 5)
                sp.dma_start(raw[:, W_OUT_AT[k]], a["W_out"][0, k * P:(k + 1) * P, :])\
                  .then_inc(raw_in[k - 6], 16)
            x_tile(0)
            o_tile(1)
            for q, rows in ((0, P), (1, DEC)):
                if q == 1:
                    sp.wait_ge(lo_done, KD)
                sp.dma_start(mod[q][0:rows], s.mod_scr[q:q + 1, 0:3 * D].rearrange("o (c d) -> o c d", c=3)
                             .broadcast_to([rows, 3, D])).then_inc(rows_in, 16)
            sp.dma_start(gain[:, :], a["norm2_g"].broadcast_to([P, D])).then_inc(rows_in, 16)
            sp.dma_start(w_route[:, :, 0:4], a["W_router_group"][0].rearrange("(k p) n -> p k n", p=P))\
              .then_inc(route_in, 16)
            sp.dma_start(w_route[:, :, 4:20], a["W_router_expert"][0].rearrange("(k p) n -> p k n", p=P))\
              .then_inc(route_in, 16)
            sp.dma_start(b_route[:, 0:4], a["b_router_group"].broadcast_to([P, 4])).then_inc(route_in, 16)
            sp.dma_start(b_route[:, 4:20], a["b_router_expert"].broadcast_to([P, NE])).then_inc(route_in, 16)
            sp.wait_ge(cleared, 1)
            sp.dma_start(s.list_scr.rearrange("(p n) o -> p (n o)", p=P), no_token[:, :]).then_inc(list_clear, 16)
            for i in range(NT):
                w = width(i)
                if i + 2 < NT:
                    o_tile(i + 2)
                if i + 1 < NT:
                    x_tile(i + 1)
                sp.wait_ge(h2_done, i + 1)
                sp.dma_start(s.h_scr[i * P:i * P + w, :], h2[0:w, i % 2, :]).then_inc(h_stored, 16)
                if i == 4:
                    sp.wait_ge(lo_done, KD)
                    for c in range(3):
                        load_chunk(sp, s, 0, c, raw[:, c], prefetched)
            for c in range(3, RAW):
                load_chunk(sp, s, 0, c, raw[:, c], prefetched)
            sp.wait_ge(h_stored, 16 * NT)
            sp.wait_ge(prefetched, 32 * RAW)

        @block.gpsimd
        def _(pool):
            pool.memset(no_token[:, :], 0).then_inc(cleared, 1)
            pool.wait_ge(list_clear, 16)
            pool.wait_ge(token_done, 1)
            for n, (lo, hi) in enumerate(GROUPS):
                pool.wait_ge(slots_done, n + 1)
                for i in range(lo, hi):
                    w = width(i)
                    for c in range(2):
                        at = bass.IndirectOffsetOnAxis(ap=entry[0:w, c, i:i + 1], axis=0)
                        pool.indirect_dma_start(out=s.list_scr[:, :], out_offset=at, in_=token[0:w, i:i + 1],
                                                in_offset=None).then_inc(scattered, 16)
            pool.wait_ge(scattered, 16 * 2 * NT)

        @block.scalar
        def _(act):
            act.preload_act_table_set("natural_log_exp_and_others")

            def o_high(i):
                w = width(i)
                act.wait_ge(o_in[i % 2], 16 * (i // 2 + 1))
                if i >= 2:
                    act.wait_ge(mm_done, 2 * (i - 1))
                act.activation(o_hi[:, i % 2, :, 0:w], o_raw[:, i % 2, :, 0:w], ACT.Copy).then_inc(ohi_done, 1)

            def turned(i):
                w = width(i)
                act.wait_ge(t_done, i + 1)
                for c in range(2):
                    last = act.activation(h2_t[:, 4 * c:4 * c + 4, 0:w], ps_t[:, 4 * c:4 * c + 4, 0:w], ACT.Copy)
                last.then_inc(t_read, 1)

            def exponentials(group):
                lo, hi = GROUPS[group]
                for n in range(2):
                    act.wait_ge(less_max, 2 * group + n + 1)
                    act.activation(probs[:, n, 0:hi - lo], probs[:, n, 0:hi - lo], ACT.Exp).then_inc(exp_done, 1)

            for k in range(KD):
                if k >= 6:
                    act.wait_ge(raw_in[k - 6], 16)
                act.activation(w_hi[:, k], raw[:, W_OUT_AT[k]], ACT.Copy).then_inc(hi_done, 1)
                if k == 1:
                    o_high(0)
            for i in range(NT):
                w = width(i)
                if i + 1 < NT:
                    o_high(i + 1)
                if i:
                    turned(i - 1)
                act.wait_ge(added, i + 1)
                if i:
                    act.wait_ge(ms_done, i)
                act.activation(squares[0:w, :], s.x_mid[0:w, i, :], ACT.Square, scale=1.0 / 32.0,
                               accum_out=mean_sq[0:w, i:i + 1]).then_inc(ms_done, 1)
                act.wait_ge(ms_done, i + 1)
                act.activation(rstd[0:w, i:i + 1], mean_sq[0:w, i:i + 1], ACT.Ln, bias=s.eps[0:w, :])\
                   .then_inc(log_done, 1)
                act.wait_ge(log_done, i + 1)
                act.activation(rstd[0:w, i:i + 1], rstd[0:w, i:i + 1], ACT.Exp, scale=-0.5).then_inc(root_done, 1)
                for group, (_, end) in enumerate(GROUPS[:-1]):
                    if i == end:
                        exponentials(group)
            turned(NT - 1)
            exponentials(len(GROUPS) - 1)

        @block.tensor
        def _(pe):
            def to_logits(i):
                w = width(i)
                pe.wait_ge(h2_done, i + 1)
                pe.wait_ge(t_read, i)
                for k in range(KD):
                    last = pe.transpose(ps_t[:, k, 0:w], h2[0:w, i % 2, k * P:(k + 1) * P], ident[0:w, 0:w])
                last.then_inc(t_done, 1)

            def score(i):
                w = width(i)
                pe.wait_ge(t_read, i + 1)
                pe.wait_ge(l_read, i)
                for k in range(KD):
                    last = pe.matmul(ps_l[0:w, 0:20], h2_t[:, k, 0:w], w_route[:, k, :],
                                     start=(k == 0), stop=(k == KD - 1))
                last.then_inc(l_done, 1)

            def count(group):
                pe.wait_ge(both_done, group + 1)
                pe.wait_ge(slots_done, group)
                for i in range(*GROUPS[group]):
                    at = slice(i * NE, (i + 1) * NE)
                    pe.matmul(ps_r[:, at], s.const("tri"), both[:, i, :], start=True, stop=False)
                    last = pe.matmul(ps_r[:, at], s.const("ones"), before[:, i, :], start=False, stop=True)
                last.then_inc(counted, 1)

            for i in range(NT):
                w, b = width(i), i % 2
                pe.wait_ge(olo_done, i + 1)
                if i >= 2:
                    pe.wait_ge(gated, i - 1)
                for c in range(2):
                    for k in range(KD):
                        if i == 0 and c == 0:
                            pe.wait_ge(lo_done, k + 1)
                        at = slice(512 * c, 512 * c + 512)
                        out = ps_o[b][0:w, c, :]
                        hi, lo = o_hi[:, b, k, 0:w], o_lo[:, b, k, 0:w]
                        pe.matmul(out, hi, w_hi[:, k, at], start=(k == 0), stop=False)
                        pe.matmul(out, hi, w_lo[:, k, at], start=False, stop=False)
                        last = pe.matmul(out, lo, w_hi[:, k, at], start=False, stop=(k == KD - 1))
                        if i and c == 1 and k == 1:
                            to_logits(i - 1)
                            for group, (_, end) in enumerate(GROUPS[:-1]):
                                if i == end + 2:
                                    count(group)
                    last.then_inc(mm_done, 1)
                if i == 1:
                    pe.wait_ge(route_in, 64)
                if i:
                    score(i - 1)
                for group, (_, end) in enumerate(GROUPS[:-1]):
                    if i == end + 1 == NT - 1:
                        count(group)
            to_logits(NT - 1)
            score(NT - 1)
            count(len(GROUPS) - 1)
            pe.wait_ge(l_read, NT)
            pe.matmul(ps_l[:, 0:NE], s.const("ones"), before[:, NT, :], start=True, stop=True)\
              .then_inc(counted, 1)

        @block.vector
        def _(dve):
            def o_low(i):
                w = width(i)
                dve.wait_ge(ohi_done, i + 1)
                dve.tensor_tensor(o_lo[:, i % 2, :, 0:w], o_raw[:, i % 2, :, 0:w], f32(o_hi[:, i % 2, :, 0:w]),
                                  ALU.subtract).then_inc(olo_done, 1)

            steps = [0]

            def then(ins):
                steps[0] += 1
                ins.then_inc(route, 1)
                dve.wait_ge(route, steps[0])

            def wide(t, n=4):
                return t.unsqueeze(2).broadcast_to([*t.shape, n])

            def pick(N, one, value, p):
                e = eq4[:, 0:N]
                then(dve.tensor_reduce(value, p, AX, ALU.max))
                then(dve.tensor_tensor(e, p, wide(value), ALU.is_equal))
                then(dve.scalar_tensor_tensor(out=e, in0=e, scalar=-8.0, op0=ALU.mult, op1=ALU.add,
                                              in1=s.const("iota", 0, 4).unsqueeze(1).broadcast_to([P, N, 4])))
                then(dve.tensor_reduce(col[:, 0:N], e, AX, ALU.min))
                then(dve.tensor_tensor(one, e, wide(col[:, 0:N]), ALU.is_equal))

            def softmax(group, N, n, src):
                p, c = probs[:, n, 0:N], col[:, 0:N]
                then(dve.tensor_reduce(c, src, AX, ALU.max))
                dve.tensor_tensor(p, src, wide(c), ALU.subtract).then_inc(less_max, 1)
                dve.wait_ge(exp_done, 2 * group + n + 1)
                then(dve.tensor_reduce(c, p, AX, ALU.add))
                then(dve.reciprocal(c, c))
                then(dve.tensor_tensor(p, p, wide(c), ALU.mult))

            def add_bias(i):
                w = width(i)
                dve.wait_ge(l_done, i + 1)
                dve.tensor_tensor(logits[0:w, i, :], ps_l[0:w, 0:20], b_route[0:w, :], ALU.add).then_inc(l_read, 1)

            def choose(group):
                lo, hi = GROUPS[group]
                N, T = hi - lo, slice(lo, hi)
                dve.wait_ge(l_read, hi)
                softmax(group, N, 0, logits[:, T, 0:4])
                pick(N, one_g[:, 0:N], group_w[:, 0:N], probs[:, 0, 0:N])
                of_group = one_g[:, 0:N].unsqueeze(3).broadcast_to([P, N, 4, 4])
                view = lambda t: t.rearrange("p t (g e) -> p t g e", g=4)
                x = view(by_expert[:, 0:N])
                then(dve.tensor_tensor(x, view(logits[:, T, 4:20]), of_group, ALU.mult))
                then(dve.tensor_reduce(one_e[:, 0, 0:N], x.rearrange("p t g e -> p t e g"), AX, ALU.add))
                softmax(group, N, 1, one_e[:, 0, 0:N])
                p = probs[:, 1, 0:N]
                pick(N, one_e[:, 0, 0:N], top[:, 0, 0:N], p)
                then(dve.scalar_tensor_tensor(out=p, in0=one_e[:, 0, 0:N], scalar=-2.0, in1=p,
                                              op0=ALU.mult, op1=ALU.add))
                pick(N, one_e[:, 1, 0:N], top[:, 1, 0:N], p)
                for c in range(2):
                    last = dve.tensor_tensor(view(chosen[:, c, T]), of_group,
                                             one_e[:, c, 0:N].unsqueeze(2).broadcast_to([P, N, 4, 4]), ALU.mult)
                then(last)
                if hi == NT:
                    for a_, b_ in ((DEC, 2 * DEC), (2 * DEC, P)):
                        last = dve.memset(chosen[a_:b_, :, NT - 1, :], 0.0)
                    then(last)
                then(dve.tensor_tensor(both[:, T], chosen[:, 0, T], chosen[:, 1, T], ALU.add))
                for i in range(lo, hi):
                    last = dve.tensor_tensor(before[:, i + 1, :], before[:, i, :], both[:, i, :], ALU.add)
                    if i + 1 < hi:
                        then(last)
                last.then_inc(both_done, 1)
                c = col[:, 0:N]
                then(dve.tensor_tensor(c, top[:, 0, 0:N], top[:, 1, 0:N], ALU.add))
                then(dve.reciprocal(c, c))
                then(dve.tensor_tensor(c, c, group_w[:, 0:N], ALU.mult))
                then(dve.tensor_tensor(s.weight[:, :, T], top[:, :, 0:N], c.unsqueeze(1).broadcast_to([P, 2, N]),
                                       ALU.mult))

            def enter(group):
                lo, hi = GROUPS[group]
                N, T = hi - lo, slice(lo, hi)
                def of_chosen(out, table):
                    for c in range(2):
                        last = dve.tensor_tensor(prod[:, c, 0:N], chosen[:, c, T], table, ALU.mult)
                    then(last)
                    then(dve.tensor_reduce(out[:, :, 0:N], prod[:, :, 0:N], AX, ALU.add))

                of_chosen(place[:, 0], s.const("place").unsqueeze(1).broadcast_to([P, N, NE]))
                dve.wait_ge(counted, group + 1)
                then(dve.tensor_copy(rank_of[:, T, :], ps_r[:, lo * NE:hi * NE].rearrange("p (t e) -> p t e", e=NE)))
                of_chosen(rank, rank_of[:, T])
                r, n_p, p0, p1 = rank[:, :, 0:N], n_past[:, :, 0:N], place[:, 0, :, 0:N], place[:, 1, :, 0:N]
                for c in range(2):
                    last = dve.tensor_tensor(past[:, c, 0:N], wide(rank[:, c, 0:N], 8),
                                             s.const("limits").unsqueeze(1).broadcast_to([P, N, 8]), ALU.is_ge)
                then(last)
                then(dve.tensor_reduce(n_p, past[:, :, 0:N], AX, ALU.add))
                then(dve.scalar_tensor_tensor(out=p1, in0=r, scalar=float(NE * NT), in1=p0,
                                              op0=ALU.mult, op1=ALU.add))
                then(dve.scalar_tensor_tensor(out=p0, in0=n_p, scalar=float(1 - P * NE * NT), in1=p1,
                                              op0=ALU.mult, op1=ALU.add))
                dve.tensor_copy(entry[:, :, T], p0).then_inc(slots_done, 1)

            then(dve.memset(logits[:, :, :], 0.0))
            for t in (both, before, rank_of, chosen[:, 0], chosen[:, 1]):
                then(dve.memset(t[:, :, :], 0.0))
            dve.tensor_copy(token[:, :], s.const("token")).then_inc(token_done, 1)
            for k in range(KD):
                dve.wait_ge(hi_done, k + 1)
                dve.tensor_tensor(w_lo[:, k], raw[:, W_OUT_AT[k]], f32(w_hi[:, k]), ALU.subtract).then_inc(lo_done, 1)
                if k == 1:
                    o_low(0)
            dve.wait_ge(rows_in, 48)
            for q, rows in ((0, P), (1, DEC)):
                last = dve.scalar_tensor_tensor(out=mod[q][0:rows, 2], in0=mod[q][0:rows, 2], scalar=1.0,
                                                in1=gain[0:rows, :], op0=ALU.add, op1=ALU.mult)
            last.then_inc(gain_done, 1)
            dve.wait_ge(gain_done, 1)
            dve.wait_ge(route_in, 64)
            for i in range(NT):
                w, b, q = width(i), i % 2, i // NP_T
                x_new = s.x_mid[0:w, i, :]
                if i + 1 < NT:
                    o_low(i + 1)
                dve.wait_ge(mm_done, 2 * i + 2)
                dve.tensor_tensor(x_new, ps_o[b][0:w].rearrange("p c d -> p (c d)"), mod[q][0:w, 0],
                                  ALU.mult).then_inc(gated, 1)
                dve.wait_ge(gated, i + 1)
                dve.wait_ge(x_in[b], 16 * (i // 2 + 1))
                dve.tensor_tensor(x_new, x_new, x_old[0:w, b, :], ALU.add).then_inc(added, 1)
                for group, (_, end) in enumerate(GROUPS[:-1]):
                    if i == end + 2:
                        enter(group)
                if i >= 2:
                    dve.wait_ge(t_done, i - 1)
                    dve.wait_ge(h_stored, 16 * (i - 1))
                dve.wait_ge(root_done, i + 1)
                seed = rstd[0:w, i:i + 1]
                dve.scalar_tensor_tensor(out=newton[0:w], in0=mean_sq[0:w, i:i + 1], scalar=s.eps[0:w, :], in1=seed,
                                         op0=ALU.add, op1=ALU.mult).then_inc(rstd_step, 1)
                dve.wait_ge(rstd_step, 3 * i + 1)
                dve.tensor_scalar(newton[0:w], newton[0:w], seed, -0.5, ALU.mult, ALU.mult).then_inc(rstd_step, 1)
                dve.wait_ge(rstd_step, 3 * i + 2)
                dve.scalar_tensor_tensor(out=seed, in0=newton[0:w], scalar=1.5, in1=seed, op0=ALU.add, op1=ALU.mult)\
                   .then_inc(rstd_step, 1)
                dve.wait_ge(rstd_step, 3 * i + 3)
                dve.scalar_tensor_tensor(out=h2[0:w, b, :], in0=x_new, scalar=rstd[0:w, i:i + 1],
                                         in1=mod[q][0:w, 2], op0=ALU.mult, op1=ALU.mult).then_inc(scaled, 1)
                dve.wait_ge(scaled, i + 1)
                dve.tensor_tensor(h2[0:w, b, :], h2[0:w, b, :], mod[q][0:w, 1], ALU.add).then_inc(h2_done, 1)
                if i:
                    add_bias(i - 1)
                for group, (_, end) in enumerate(GROUPS[:-1]):
                    if i == end + 1 == NT - 1:
                        enter(group)
                for group, (_, end) in enumerate(GROUPS[:-1]):
                    if i == end:
                        choose(group)
            add_bias(NT - 1)
            choose(len(GROUPS) - 1)
            enter(len(GROUPS) - 1)
            dve.wait_ge(counted, len(GROUPS) + 1)
            then(dve.tensor_copy(n_of[:, :], ps_l[:, 0:NE]))
            ones = s.const("ones")
            then(dve.memset(first[:, 0:1], 0.0))
            then(dve.tensor_tensor_scan(first[:, 1:NE + 1], ones[:, 0:NE], n_of[:, :], 0.0, ALU.mult, ALU.add))
            then(dve.tensor_tensor(over[:, :, :], n_of[:, :].unsqueeze(2).broadcast_to([P, NE, 8]),
                                   s.const("limits").unsqueeze(1).broadcast_to([P, NE, 8]), ALU.is_gt))
            then(dve.tensor_reduce(extra[:, :], over[:, :, :], AX, ALU.add))
            then(dve.memset(tiles[:, 0:1], 0.0))
            then(dve.tensor_tensor_scan(tiles[:, 1:NE + 1], ones[:, 0:NE], extra[:, :], 0.0, ALU.mult, ALU.add))
            then(dve.tensor_tensor(tiles[:, 0:NE], tiles[:, 0:NE], s.const("iota"), ALU.add))
            then(dve.tensor_copy(s.plan[:, 0:NE + 1], first[0:1, :]))
            then(dve.tensor_copy(s.plan[:, 32:32 + NE], extra[0:1, :]))
            then(dve.tensor_copy(s.plan[:, 64:64 + NE], tiles[0:1, 0:NE]))
            then(dve.tensor_tensor(both[:, :, :], rank_of[:, :, :],
                                   first[:, 0:NE].unsqueeze(1).broadcast_to([P, NT, NE]), ALU.add))
            for c in range(2):
                then(dve.tensor_tensor(all_prod[:, :, :], both[:, :, :], chosen[:, c], ALU.mult))
                then(dve.tensor_reduce(slot_f[:, c, :], all_prod[:, :, :], AX, ALU.add))
            dve.tensor_copy(s.slot[:, :, :], slot_f[:, :, :])


def phase_experts(nc, s):
    CH = CHUNKS
    with ExitStack() as ctx:
        sb, ps, sem = allocate(nc, ctx, "experts")
        more = sb("raw_more", [P, CH - RAW, D])
        raw = [s.raw[:, c] if c < RAW else more[:, c - RAW] for c in range(CH)]
        raw_in = [sem(f"raw_in{n}") for n in range(CH // 2)]
        w_hi = sb("w_hi", [P, CH, D], F32R)
        w_lo = sb("w_lo", [P, CH, D], F32R)
        x_rows = sb("x_rows", [P, D])
        x_hi = sb("x_hi", [P, KD, P], F32R)
        x_lo = sb("x_lo", [P, KD, P], F32R)
        act_g = sb("act_g", [P, 2, 256])
        hid = sb("hid", [P, 512])
        h_hi = sb("h_hi", [P, KF, P], F32R)
        h_lo = sb("h_lo", [P, KF, P], F32R)
        y = sb("y", [P, D])
        ps_g = [ps(f"ps_g{n}", [P, 512]) for n in range(2)]
        ps_x = [ps(f"ps_x{n}", [P, 4, P]) for n in range(2)]
        ps_h = [ps(f"ps_h{n}", [P, 4, P]) for n in range(2)]
        ps_y = [ps(f"ps_y{n}", [P, 512]) for n in range(2)]
        lists = sb("lists", [P, NE * NT + 1], I32)
        index = sb("index", [P, 1], I32)
        lists_in, index_done = sem("lists_in"), sem("index_done")
        hi_done, lo_done, used = sem("hi_done"), sem("lo_done"), sem("used")
        x_in, xt_done, xhi_done, xlo_done = sem("x_in"), sem("xt_done"), sem("xhi_done"), sem("xlo_done")
        silu_done, hid_done = sem("silu_done"), sem("hid_done")
        ht_done, hhi_done, hlo_done = sem("ht_done"), sem("hhi_done"), sem("hlo_done")
        y0_done, y1_done, y_stored, idle = sem("y0_done"), sem("y1_done"), sem("y_stored"), sem("idle")
        block = ctx.enter_context(nc.Block())
        a = s.args
        ident = s.const("ident")

        def experts(e, tile):
            def one(x, last_expert):
                extra = e.value_load(s.plan[0:1, bass.ds(x + 32, 1)], min_val=0, max_val=8)
                base = e.value_load(s.plan[0:1, bass.ds(x + 64, 1)], min_val=0, max_val=32)
                with e.If(extra > 0):
                    with e.Fori(0, extra) as j:
                        tile(x, e.snap(base + j), j, False, last_expert)
                tile(x, e.snap(base + extra), extra, True, last_expert)

            with e.Fori(0, NE - 1) as x:
                one(x, False)
            one(NE - 1, True)

        @block.sync
        def _(sp):
            sp.dma_start(lists[:, 0:NE * NT], s.list_scr.rearrange("(p n) o -> p (n o)", p=P)).then_inc(lists_in, 16)
            for n in range(RAW // 2):
                sp.sem_inc(raw_in[n], 64)
            for c in range(RAW, CH):
                load_chunk(sp, s, 0, c, raw[c], raw_in[c // 2])
            with sp.Fori(1, NE) as x:
                for c in range(CH):
                    sp.wait_ge(lo_done, sp.snap(x * CH + (c + 1 - CH)))
                    carry(sp, idle)
                    load_chunk(sp, s, sp.snap(x * 1), c, raw[c], raw_in[c // 2])

        @block.gpsimd
        def _(pool):
            for semaphore in (y0_done, y1_done, hid_done, hlo_done):
                pool.sem_inc(semaphore, PRIMED)
            pool.memset(lists[:, NE * NT:], 0)
            pool.wait_ge(lists_in, 16)

            def gather(column, n):
                pool.tensor_copy(index[:, :], lists[:, column]).then_inc(index_done, 1)
                pool.wait_ge(index_done, n)
                if not isinstance(n, int):
                    carry(pool, idle)
                pool.indirect_dma_start(out=x_rows[:, :], out_offset=None, in_=s.h_scr[:, :],
                                        in_offset=bass.IndirectOffsetOnAxis(ap=index[:, 0:1], axis=0))\
                    .then_inc(x_in, 16)

            gather(slice(0, 1), 1)
            pool.dma_start(s.y_scr[SLOTS:SLOTS + P, 0:P], ident).then_inc(y_stored, 16)

            def tile(x, t, j, last, last_expert):
                start = pool.value_load(s.plan[0:1, bass.ds(x, 1)], min_val=0, max_val=SLOTS)
                row = pool.snap(start + j * P, min_val=0, max_val=SLOTS)
                after = (x + 1) * NT if last else x * NT + j + 1
                column = slice(after, after + 1) if last_expert and last else bass.ds(pool.snap(after), 1)
                pool.wait_ge(xt_done, pool.snap(t + 1))
                carry(pool, idle)
                gather(column, pool.snap(t + 2))
                pool.wait_ge(y_stored, pool.snap(t * 16 + 16))
                pool.wait_ge(y0_done, pool.snap(t + (1 + PRIMED)))
                pool.wait_ge(y1_done, pool.snap(t + (1 + PRIMED)))
                carry(pool, idle)
                pool.dma_start(s.y_scr[bass.ds(row, P), :], y[:, :]).then_inc(y_stored, 16)

            experts(pool, tile)
            total = pool.value_load(s.plan[0:1, 64 + NE - 1:64 + NE], min_val=0, max_val=32)
            extra = pool.value_load(s.plan[0:1, 32 + NE - 1:32 + NE], min_val=0, max_val=8)
            pool.wait_ge(y_stored, pool.snap((total + extra + 2) * 16))
            carry(pool, idle)

        @block.scalar
        def _(act):
            def split(x, c, t):
                act.wait_ge(raw_in[c // 2], act.snap(x * 64 + 64) if t is not None else 64)
                if t is not None:
                    act.wait_ge(used, act.snap(t * CH + (c + 1)))
                act.activation(w_hi[:, c], raw[c], ACT.Copy).then_inc(hi_done, 1)

            def x_high(t):
                act.wait_ge(xt_done, t + 2 if isinstance(t, int) else act.snap(t + 2))
                for n in range(2):
                    act.activation(x_hi[:, 4 * n:4 * n + 4, :], ps_x[n][:, :, :], ACT.Copy).then_inc(xhi_done, 1)

            def tile(x, t, j, last, last_expert):
                splits = last and not last_expert
                after = act.snap(x + 1) if splits else None
                t2 = act.snap(t * 2)

                def some(lo, hi):
                    if splits:
                        for c in range(lo, hi):
                            split(after, c, t)

                def silu(n):
                    act.wait_ge(used, act.snap(t * CH + 4 * (n + 1)))
                    act.activation(act_g[:, n, :], ps_g[n][:, 0:256], ACT.Silu).then_inc(silu_done, 1)

                def h_high(n):
                    act.wait_ge(ht_done, act.snap(t2 + (n + 1)))
                    act.activation(h_hi[:, 2 * n:2 * n + 2, :], ps_h[n][:, 0:2, :], ACT.Copy).then_inc(hhi_done, 1)

                some(0, 3)
                silu(0)
                some(3, 6)
                silu(1)
                h_high(0)
                x_high(t)
                h_high(1)
                some(6, 9)
                act.wait_ge(used, act.snap(t * CH + CH))
                act.wait_ge(y_stored, act.snap(t * 16 + 16))
                act.activation(y[:, 0:512], ps_y[0][:, :], ACT.Copy).then_inc(y0_done, 1)
                some(9, CH)

            act.preload_act_table_set("silu_and_others")
            for c in range(6):
                split(0, c, None)
            x_high(-1)
            for c in range(6, CH):
                split(0, c, None)
            experts(act, tile)

        @block.vector
        def _(dve):
            def split(x, c, first):
                dve.wait_ge(hi_done, c + 1 if first else dve.snap(x * CH + (c + 1)))
                dve.tensor_tensor(w_lo[:, c], raw[c], f32(w_hi[:, c]), ALU.subtract).then_inc(lo_done, 1)

            def x_low(t):
                for n in range(2):
                    dve.wait_ge(xhi_done, 2 * t + n + 3 if isinstance(t, int) else dve.snap(t * 2 + (n + 3)))
                    last = dve.tensor_tensor(x_lo[:, 4 * n:4 * n + 4, :], ps_x[n][:, :, :],
                                             f32(x_hi[:, 4 * n:4 * n + 4, :]), ALU.subtract)
                last.then_inc(xlo_done, 1)

            def tile(x, t, j, last, last_expert):
                splits = last and not last_expert
                after = dve.snap(x + 1) if splits else None
                t2 = dve.snap(t * 2)

                def some(lo, hi):
                    if splits:
                        for c in range(lo, hi):
                            split(after, c, False)

                def product(n):
                    dve.wait_ge(silu_done, dve.snap(t2 + (n + 1)))
                    dve.tensor_tensor(hid[:, 256 * n:256 * n + 256], act_g[:, n, :], ps_g[n][:, 256:512],
                                      ALU.mult).then_inc(hid_done, 1)

                def h_low(n):
                    dve.wait_ge(hhi_done, dve.snap(t2 + (n + 1)))
                    dve.tensor_tensor(h_lo[:, 2 * n:2 * n + 2, :], ps_h[n][:, 0:2, :],
                                      f32(h_hi[:, 2 * n:2 * n + 2, :]), ALU.subtract).then_inc(hlo_done, 1)

                some(0, 3)
                product(0)
                some(3, 6)
                product(1)
                h_low(0)
                x_low(t)
                h_low(1)
                some(6, 9)
                dve.wait_ge(used, dve.snap(t * CH + CH))
                dve.wait_ge(y_stored, dve.snap(t * 16 + 16))
                dve.tensor_copy(y[:, 512:1024], ps_y[1][:, :]).then_inc(y1_done, 1)
                some(9, CH)

            for c in range(6):
                split(0, c, True)
            x_low(-1)
            for c in range(6, CH):
                split(0, c, True)
            experts(dve, tile)

        @block.tensor
        def _(pe):
            def turn_x(t):
                if isinstance(t, int):
                    pe.wait_ge(x_in, 16)
                else:
                    pe.wait_ge(x_in, pe.snap(t * 16 + 32))
                    pe.wait_ge(xlo_done, pe.snap(t + 1))
                for k in range(KD):
                    last = pe.transpose(ps_x[k // 4][:, k % 4, :], x_rows[:, k * P:(k + 1) * P], ident)
                last.then_inc(xt_done, 1)

            turn_x(-1)

            def tile(x, t, j, last, _):
                t2 = pe.snap(t * 2 + PRIMED)
                chunk0 = pe.snap(x * CH) if not isinstance(x, int) else x * CH
                pe.wait_ge(xlo_done, pe.snap(t + 1))
                pe.wait_ge(hid_done, t2)
                for half in range(2):
                    out = ps_g[half][:, :]
                    for k in range(KD):
                        c = 4 * half + k // 2
                        if k % 2 == 0:
                            pe.wait_ge(lo_done, chunk0 + (c + 1))
                        at = slice(512 * (k % 2), 512 * (k % 2) + 512)
                        pe.matmul(out, x_hi[:, k, :], w_hi[:, c, at], start=(k == 0), stop=False)
                        pe.matmul(out, x_hi[:, k, :], w_lo[:, c, at], start=False, stop=False)
                        ins = pe.matmul(out, x_lo[:, k, :], w_hi[:, c, at], start=False, stop=(k == KD - 1))
                        if k % 2:
                            ins.then_inc(used, 1)

                def turn_h(n):
                    pe.wait_ge(hid_done, pe.snap(t2 + (n + 1)))
                    pe.wait_ge(hlo_done, t2)
                    for f in range(2):
                        ins = pe.transpose(ps_h[n][:, f, :], hid[:, (2 * n + f) * P:(2 * n + f + 1) * P], ident)
                    ins.then_inc(ht_done, 1)

                turn_h(0)
                turn_x(t)
                turn_h(1)
                pe.wait_ge(y0_done, pe.snap(t + PRIMED))
                pe.wait_ge(y1_done, pe.snap(t + PRIMED))
                for f in range(KF):
                    if f % 2 == 0:
                        pe.wait_ge(hlo_done, pe.snap(t2 + (f // 2 + 1)))
                    pe.wait_ge(lo_done, chunk0 + (9 + f))
                    for m in range(2):
                        at = slice(512 * m, 512 * m + 512)
                        pe.matmul(ps_y[m][:, :], h_hi[:, f, :], w_hi[:, 8 + f, at], start=(f == 0), stop=False)
                        pe.matmul(ps_y[m][:, :], h_hi[:, f, :], w_lo[:, 8 + f, at], start=False, stop=False)
                        ins = pe.matmul(ps_y[m][:, :], h_lo[:, f, :], w_hi[:, 8 + f, at], start=False,
                                        stop=(f == KF - 1))
                    ins.then_inc(used, 1)

            experts(pe, tile)


def phase_combine(nc, s):
    with ExitStack() as ctx:
        sb, ps, sem = allocate(nc, ctx, "combine")
        B = 3
        y = sb("y", [P, B, 2, D])
        x = s.x_mid
        part = sb("part", [P, B, D])
        gate = sb("gate", [P, 2, D])
        gain = sb("gain", [P, D])
        squares = sb("squares", [P, D])
        mean_sq = sb("mean_sq", [P, NT])
        rstd = sb("rstd", [P, NT])
        rows_in, y_in = sem("rows_in"), [sem(f"y_in{n}") for n in range(B)]
        first_done, summed, gated, added, ms_done, root_done, rstd_done, out_done = (
            sem(n) for n in ("first_done", "summed", "gated", "added", "ms_done", "root_done", "rstd_done",
                             "out_done"))
        stored = sem("stored")
        block = ctx.enter_context(nc.Block())

        @block.sync
        def _(sp):
            for q, rows in ((0, P), (1, DEC)):
                sp.dma_start(gate[0:rows, q], s.mod_scr[q:q + 1, 3 * D:4 * D].broadcast_to([rows, D]))\
                  .then_inc(rows_in, 16)
            sp.dma_start(gain[:, :], s.args["final_norm_g"].unsqueeze(0).broadcast_to([P, D])).then_inc(rows_in, 16)
            for i in range(NT):
                w = width(i)
                sp.wait_ge(out_done, i + 1)
                dst = s.outs["y_prompt"][0, i * P:i * P + w, :] if i < NP_T else s.outs["y_sample"][0]
                sp.dma_start(dst, x[0:w, i]).then_inc(stored, 16)
            sp.wait_ge(stored, 16 * NT)

        @block.gpsimd
        def _(pool):
            for i in range(NT):
                w = width(i)
                if i >= B:
                    pool.wait_ge(summed, i - B + 1)
                for c in range(2):
                    pool.indirect_dma_start(out=y[0:w, i % B, c, :], out_offset=None, in_=s.y_scr[0:SLOTS, :],
                                            in_offset=bass.IndirectOffsetOnAxis(ap=s.slot[0:w, c, i:i + 1], axis=0))\
                        .then_inc(y_in[i % B], 16)

        @block.scalar
        def _(act):
            def first(i):
                w, b = width(i), i % B
                act.wait_ge(y_in[b], 32 * (i // B + 1))
                if i >= B:
                    act.wait_ge(added, i - B + 1)
                act.activation(part[0:w, b], y[0:w, b, 0], ACT.Copy, scale=s.weight[0:w, 0, i:i + 1])\
                   .then_inc(first_done, 1)

            first(0)
            for i in range(NT):
                w, b = width(i), i % B
                if i + 1 < NT:
                    first(i + 1)
                act.wait_ge(added, i + 1)
                if i:
                    act.wait_ge(ms_done, i)
                act.activation(squares[0:w, :], x[0:w, i], ACT.Square, scale=1.0 / 32.0,
                               accum_out=mean_sq[0:w, i:i + 1]).then_inc(ms_done, 1)
                act.wait_ge(ms_done, i + 1)
                act.activation(rstd[0:w, i:i + 1], mean_sq[0:w, i:i + 1], ACT.Sqrt, bias=s.eps[0:w, :])\
                   .then_inc(root_done, 1)

        @block.vector
        def _(dve):
            def normalise(i):
                w, b = width(i), i % B
                dve.wait_ge(root_done, i + 1)
                dve.reciprocal(rstd[0:w, i:i + 1], rstd[0:w, i:i + 1]).then_inc(rstd_done, 1)
                dve.wait_ge(rstd_done, i + 1)
                dve.scalar_tensor_tensor(out=x[0:w, i], in0=x[0:w, i], scalar=rstd[0:w, i:i + 1], in1=gain[0:w],
                                         op0=ALU.mult, op1=ALU.mult).then_inc(out_done, 1)

            dve.wait_ge(rows_in, 48)
            for i in range(NT):
                w, b, q = width(i), i % B, i // NP_T
                dve.wait_ge(first_done, i + 1)
                dve.scalar_tensor_tensor(out=part[0:w, b], in0=y[0:w, b, 1], scalar=s.weight[0:w, 1, i:i + 1],
                                         in1=part[0:w, b], op0=ALU.mult, op1=ALU.add).then_inc(summed, 1)
                dve.wait_ge(summed, i + 1)
                dve.tensor_tensor(part[0:w, b], part[0:w, b], gate[0:w, q], ALU.mult).then_inc(gated, 1)
                dve.wait_ge(gated, i + 1)
                dve.tensor_tensor(x[0:w, i], x[0:w, i], part[0:w, b], ALU.add).then_inc(added, 1)
                if i:
                    normalise(i - 1)
            normalise(NT - 1)


def build(nc, args, outs):
    s = Shared()
    s.args, s.outs = args, outs
    with ExitStack() as ctx:
        sb, ps, sem = allocate(nc, ctx, "all")
        s.consts = sb("consts_sb", [P, N_KEPT])
        s.eps = sb("eps", [P, 1])
        s.o_scr = nc.dram_tensor("o_scratch", [D, NTOK], F32).ap()
        s.mod_scr = nc.dram_tensor("mod_scratch", [2, 4 * D], F32).ap()
        s.h_scr = nc.dram_tensor("h_scratch", [NTOK, D], F32).ap()
        s.list_scr = nc.dram_tensor("list_scratch", [P * NE * NT, 1], I32).ap()
        s.y_scr = nc.dram_tensor("y_scratch", [ROWS, D], F32).ap()
        s.slot = sb("slot", [P, 2, NT], I32)
        s.weight = sb("weight", [P, 2, NT])
        s.plan = sb("plan", [1, 96], I32)
        s.raw = sb("raw", [P, RAW, D])
        with ExitStack() as ctx2:
            sb2, _, _ = allocate(nc, ctx2, "early")
            s.tables = sb2("tables", [P, N_TABLES])
            s.cT = sb2("cT", [P, KD, 2])
            s.cols = sb2("cols", [P, 40])
            s.bound = sb2("bound", [P, 2, HEADS])
            s.h_hi = sb2("h_hi", [P, KD, NTOK], F32R)
            s.h_lo = sb2("h_lo", [P, KD, NTOK], F32R)
            phase_condition(nc, s)
            phase_mixers(nc, s)
        s.x_mid = sb("x_mid", [P, NT, D])
        phase_output(nc, s)
        phase_experts(nc, s)
        phase_combine(nc, s)


_INS = ["x_prompt", "x_sample", "c_prompt", "c_sample", "state_ret", "state_hgrn", "W_ada", "b_ada", "norm1_g",
        "norm2_g", "W_in", "ret_norm_g", "hgrn_norm_g", "hgrn_lb_logits", "W_out", "W_router_group",
        "b_router_group", "W_router_expert", "b_router_expert", "W_gate_e", "W_up_e", "W_down_e", "final_norm_g"]
_STATE = (1, 1, HEADS, P, P)
_OUTS = dict(y_prompt=(1, SEQ, D), y_sample=(1, DEC, D), state_ret_prompt=_STATE, state_hgrn_prompt=_STATE,
             state_ret_sample=_STATE, state_hgrn_sample=_STATE)


def kernel(**inputs):
    import concourse.bacc as _bacc
    from concourse.bass_utils import run_bass_kernel_spmd as _run

    nc = _bacc.Bacc("TRN2", target_bir_lowering=False, num_devices=1)
    arrays, args, outs = {}, {}, {}
    for name in [*_INS, "consts"]:
        a = np.ascontiguousarray(constants() if name == "consts" else inputs[name])
        arrays[f"in_{name}_dram"] = a
        args[name] = nc.dram_tensor(f"in_{name}_dram", a.shape, mybir.dt.from_np(a.dtype), kind="ExternalInput").ap()
    for name, shape in _OUTS.items():
        outs[name] = nc.dram_tensor(f"out_{name}_dram", shape, F32, kind="ExternalOutput").ap()
    build(nc, args, outs)
    r = _run(nc, [arrays], core_ids=[0])
    return tuple(r.results[0][f"out_{name}_dram"] for name in _OUTS)
```
